# Optimizing a Trainium2 kernel written in Bass

```python
import math
import jax, jax.numpy as jnp
from jax import lax
import numpy as np

D_MODEL = 1024
BATCH = 1
SEQ = 256
DEPTH = 1

ATTN_HEADS = 8
ATTN_HEAD_DIM = 64
ATTN_W = ATTN_HEADS * ATTN_HEAD_DIM
ROT_DIM = ATTN_HEAD_DIM // 4
ROPE_THETA = 500000.0
MOBA_BLOCK = 256
MOBA_TOPK = 3
MOBA_Q_CHUNK = 32
MLSTM_HEADS = 4
MLSTM_HEAD_DIM = 128
MLSTM_W = MLSTM_HEADS * MLSTM_HEAD_DIM
MLSTM_CHUNK = 64
CONV_WIDTH = 4
PEER_HEADS = 8
PEER_N_KEYS = 128
PEER_N_EXPERTS = PEER_N_KEYS * PEER_N_KEYS
PEER_KEY_DIM = 256
PEER_HALF = PEER_KEY_DIM // 2
PEER_TOPK = 16
PEER_TOKEN_CHUNK = 128
EPS = 1e-6

IN_SPLITS = (ATTN_W, ATTN_W, ATTN_W, MLSTM_W, MLSTM_W, MLSTM_W, MLSTM_W,
             MLSTM_HEADS, MLSTM_HEADS, D_MODEL, D_MODEL)
IN_COLS = sum(IN_SPLITS)

kernel_name = "hybrid_moba_mlstm_peer_block"

def rms_norm(x, w):
    xf = x.astype(jnp.float32)
    xf = xf * lax.rsqrt(jnp.mean(xf * xf, axis=-1, keepdims=True) + EPS)
    return (xf * w.astype(jnp.float32)).astype(x.dtype)

def apply_partial_rope(t):
    S = t.shape[2]
    pos = jnp.arange(S, dtype=jnp.float32)
    inv_freq = ROPE_THETA ** (-jnp.arange(0, ROT_DIM, 2, dtype=jnp.float32) / ROT_DIM)
    ang = pos[:, None] * inv_freq[None, :]
    cos, sin = jnp.cos(ang), jnp.sin(ang)
    tf = t.astype(jnp.float32)
    half = ROT_DIM // 2
    x1, x2, rest = tf[..., :half], tf[..., half:ROT_DIM], tf[..., ROT_DIM:]
    out = jnp.concatenate([x1 * cos - x2 * sin, x2 * cos + x1 * sin, rest], axis=-1)
    return out.astype(t.dtype)

def causal_depthwise_conv(u, w, b):
    S = u.shape[1]
    up = jnp.pad(u, ((0, 0), (CONV_WIDTH - 1, 0), (0, 0)))
    y = sum(up[:, j:j + S] * w[j] for j in range(CONV_WIDTH))
    return y + b

def moba_attention(q, k, v):
    B, H, S, hd = q.shape
    n_blocks = -(-S // MOBA_BLOCK)
    s_pad = n_blocks * MOBA_BLOCK
    pad = ((0, 0), (0, 0), (0, s_pad - S), (0, 0))
    q, k, v = jnp.pad(q, pad), jnp.pad(k, pad), jnp.pad(v, pad)
    k_blocks = k.reshape(B, H, n_blocks, MOBA_BLOCK, hd)
    v_blocks = v.reshape(B, H, n_blocks, MOBA_BLOCK, hd)
    k_mean = jnp.mean(k_blocks.astype(jnp.float32), axis=3)
    topk = min(MOBA_TOPK, n_blocks)
    scale = hd ** -0.5
    b_idx = jnp.arange(B)[:, None, None, None]
    h_idx = jnp.arange(H)[None, :, None, None]
    block_ids = jnp.arange(n_blocks)

    def one_chunk(ci):
        start = ci * MOBA_Q_CHUNK
        blk = start // MOBA_BLOCK
        qc = lax.dynamic_slice_in_dim(q, start, MOBA_Q_CHUNK, axis=2).astype(jnp.float32)
        k_own = lax.dynamic_slice_in_dim(k, blk * MOBA_BLOCK, MOBA_BLOCK, axis=2).astype(jnp.float32)
        v_own = lax.dynamic_slice_in_dim(v, blk * MOBA_BLOCK, MOBA_BLOCK, axis=2).astype(jnp.float32)
        q_pos = start + jnp.arange(MOBA_Q_CHUNK)
        k_pos = blk * MOBA_BLOCK + jnp.arange(MOBA_BLOCK)
        s_own = jnp.einsum('bhqd,bhkd->bhqk', qc, k_own) * scale
        s_own = jnp.where(k_pos[None, :] <= q_pos[:, None], s_own, -jnp.inf)
        gate = jnp.einsum('bhqd,bhnd->bhqn', qc, k_mean)
        gate = jnp.where(block_ids < blk, gate, -jnp.inf)
        _, sel = lax.top_k(gate, topk)
        valid = sel < blk
        k_sel = k_blocks[b_idx, h_idx, sel].astype(jnp.float32)
        v_sel = v_blocks[b_idx, h_idx, sel].astype(jnp.float32)
        s_sel = jnp.einsum('bhqd,bhqjkd->bhqjk', qc, k_sel) * scale
        s_sel = jnp.where(valid[..., None], s_sel, -jnp.inf)
        s_sel = s_sel.reshape(B, H, MOBA_Q_CHUNK, topk * MOBA_BLOCK)
        p = jax.nn.softmax(jnp.concatenate([s_sel, s_own], axis=-1), axis=-1)
        p_sel = p[..., :topk * MOBA_BLOCK].reshape(B, H, MOBA_Q_CHUNK, topk, MOBA_BLOCK)
        p_own = p[..., topk * MOBA_BLOCK:]
        out = (jnp.einsum('bhqjk,bhqjkd->bhqd', p_sel, v_sel)
               + jnp.einsum('bhqk,bhkd->bhqd', p_own, v_own))
        return out.astype(q.dtype)

    n_chunks = s_pad // MOBA_Q_CHUNK
    out = lax.map(one_chunk, jnp.arange(n_chunks))
    out = jnp.moveaxis(out, 0, 2).reshape(B, H, s_pad, hd)[:, :, :S]
    return out

def mlstm_chunkwise(q, k, v, i_pre, f_pre):
    B, H, S, d = q.shape
    L = MLSTM_CHUNK
    nc = S // L
    log_f = jax.nn.log_sigmoid(f_pre)

    def to_chunks(t):
        return jnp.moveaxis(t.reshape((B, H, nc, L) + t.shape[3:]), 2, 0)

    causal = jnp.tril(jnp.ones((L, L), dtype=bool))

    def step(carry, inp):
        C, n, m = carry
        qc, kc, vc, ig, lf = inp
        b = jnp.cumsum(lf, axis=-1)
        log_d = b[..., :, None] - b[..., None, :] + ig[..., None, :]
        log_d = jnp.where(causal, log_d, -jnp.inf)
        m_inter = b + m[..., None]
        m_t = jnp.maximum(m_inter, jnp.max(log_d, axis=-1))
        A = jnp.exp(log_d - m_t[..., None]) * jnp.einsum('bhtd,bhsd->bhts', qc, kc)
        w_inter = jnp.exp(m_inter - m_t)
        num = (jnp.einsum('bhts,bhsv->bhtv', A, vc)
               + w_inter[..., None] * jnp.einsum('bhtd,bhdv->bhtv', qc, C))
        den = jnp.sum(A, axis=-1) + w_inter * jnp.einsum('bhtd,bhd->bht', qc, n)
        h = num / jnp.maximum(jnp.abs(den), jnp.exp(-m_t))[..., None]
        m_new = m_t[..., -1]
        w_s = jnp.exp(b[..., -1:] - b + ig - m_new[..., None])
        decay = jnp.exp(b[..., -1] + m - m_new)
        C_new = decay[..., None, None] * C + jnp.einsum('bhs,bhsd,bhsv->bhdv', w_s, kc, vc)
        n_new = decay[..., None] * n + jnp.einsum('bhs,bhsd->bhd', w_s, kc)
        return (C_new, n_new, m_new), h

    init = (jnp.zeros((B, H, d, d), jnp.float32),
            jnp.zeros((B, H, d), jnp.float32),
            jnp.zeros((B, H), jnp.float32))
    _, h = lax.scan(step, init, (to_chunks(q), to_chunks(k), to_chunks(v),
                                 to_chunks(i_pre), to_chunks(log_f)))
    return jnp.moveaxis(h, 0, 2).reshape(B, H, S, d)

def peer_ffn(h, w_query, keys_1, keys_2, w_down, w_up):
    B, S, D = h.shape
    T = B * S
    hf = h.reshape(T, D)
    q = (hf @ w_query).reshape(T, PEER_HEADS, PEER_KEY_DIM)
    q1, q2 = q[..., :PEER_HALF], q[..., PEER_HALF:]
    s1 = jnp.einsum('thd,hnd->thn', q1, keys_1).astype(jnp.float32)
    s2 = jnp.einsum('thd,hnd->thn', q2, keys_2).astype(jnp.float32)
    v1, i1 = lax.top_k(s1, PEER_TOPK)
    v2, i2 = lax.top_k(s2, PEER_TOPK)
    cand = (v1[..., :, None] + v2[..., None, :]).reshape(T, PEER_HEADS, PEER_TOPK * PEER_TOPK)
    sc, ci = lax.top_k(cand, PEER_TOPK)
    e1 = jnp.take_along_axis(i1, ci // PEER_TOPK, axis=-1)
    e2 = jnp.take_along_axis(i2, ci % PEER_TOPK, axis=-1)
    expert = e1 * PEER_N_KEYS + e2
    g = jax.nn.softmax(sc, axis=-1).astype(h.dtype)

    def one_chunk(args):
        xc, ec, gc = args
        u = w_down[ec]
        a = jax.nn.gelu(jnp.einsum('cd,chkd->chk', xc, u), approximate=False)
        vv = w_up[ec]
        return jnp.einsum('chk,chkd->cd', gc * a, vv)

    nc = T // PEER_TOKEN_CHUNK
    out = lax.map(one_chunk, (hf.reshape(nc, PEER_TOKEN_CHUNK, D),
                              expert.reshape(nc, PEER_TOKEN_CHUNK, PEER_HEADS, PEER_TOPK),
                              g.reshape(nc, PEER_TOKEN_CHUNK, PEER_HEADS, PEER_TOPK)))
    return out.reshape(B, S, D)

def setup_inputs(seed: int = 0) -> dict:
    key = jax.random.key(seed)
    ks = jax.random.split(key, 24)
    D = D_MODEL
    nrm = lambda k, shape, s: jax.random.normal(k, shape, jnp.float32) * s
    gain = lambda k, shape: 1.0 + 0.02 * jax.random.normal(k, shape, jnp.float32)
    return {
        "x": nrm(ks[0], (BATCH, SEQ, D), 1.0),
        "mix_norm_w": gain(ks[1], (D,)),
        "w_in": nrm(ks[2], (D, IN_COLS), D ** -0.5),
        "q_norm_w": gain(ks[3], (ATTN_HEAD_DIM,)),
        "k_norm_w": gain(ks[4], (ATTN_HEAD_DIM,)),
        "conv_w": nrm(ks[5], (CONV_WIDTH, 2 * MLSTM_W), CONV_WIDTH ** -0.5),
        "conv_b": nrm(ks[6], (2 * MLSTM_W,), 0.01),
        "igate_b": nrm(ks[7], (MLSTM_HEADS,), 0.1),
        "fgate_b": 3.0 + jax.random.uniform(ks[8], (MLSTM_HEADS,), jnp.float32, 0.0, 3.0),
        "mlstm_norm_w": gain(ks[9], (MLSTM_W,)),
        "w_attn_branch": nrm(ks[10], (ATTN_W, D), ATTN_W ** -0.5),
        "w_mlstm_branch": nrm(ks[11], (MLSTM_W, D), MLSTM_W ** -0.5),
        "merge_b": nrm(ks[12], (2, D), 0.01),
        "w_out": nrm(ks[13], (D, D), D ** -0.5),
        "ffn_norm_w": gain(ks[14], (D,)),
        "peer_w_query": nrm(ks[15], (D, PEER_HEADS * PEER_KEY_DIM), D ** -0.5),
        "peer_keys_1": nrm(ks[16], (PEER_HEADS, PEER_N_KEYS, PEER_HALF), PEER_HALF ** -0.5),
        "peer_keys_2": nrm(ks[17], (PEER_HEADS, PEER_N_KEYS, PEER_HALF), PEER_HALF ** -0.5),
        "peer_w_down": nrm(ks[18], (PEER_N_EXPERTS, D), D ** -0.5),
        "peer_w_up": nrm(ks[19], (PEER_N_EXPERTS, D), 0.5),
    }

def reference(x, mix_norm_w, w_in, q_norm_w, k_norm_w, conv_w, conv_b, igate_b, fgate_b,
              mlstm_norm_w, w_attn_branch, w_mlstm_branch, merge_b, w_out, ffn_norm_w,
              peer_w_query, peer_keys_1, peer_keys_2, peer_w_down, peer_w_up):
    B, S, _ = x.shape
    offsets = [int(o) for o in np.cumsum(IN_SPLITS)[:-1]]

    def to_heads(t, n, d):
        return t.reshape(B, S, n, d).transpose(0, 2, 1, 3)

    for _layer in range(DEPTH):
        h = rms_norm(x, mix_norm_w)
        proj = h @ w_in
        aq, ak, av, mq, mk, mv, mo, mi, mf, ga, gm = jnp.split(proj, offsets, axis=-1)

        qa = apply_partial_rope(rms_norm(to_heads(aq, ATTN_HEADS, ATTN_HEAD_DIM), q_norm_w))
        ka = apply_partial_rope(rms_norm(to_heads(ak, ATTN_HEADS, ATTN_HEAD_DIM), k_norm_w))
        va = to_heads(av, ATTN_HEADS, ATTN_HEAD_DIM)
        attn = moba_attention(qa, ka, va)
        attn = attn.transpose(0, 2, 1, 3).reshape(B, S, ATTN_W)

        qk = jax.nn.silu(causal_depthwise_conv(jnp.concatenate([mq, mk], axis=-1), conv_w, conv_b))
        mq_c, mk_c = qk[..., :MLSTM_W], qk[..., MLSTM_W:]
        qm = to_heads(mq_c, MLSTM_HEADS, MLSTM_HEAD_DIM).astype(jnp.float32)
        km = to_heads(mk_c, MLSTM_HEADS, MLSTM_HEAD_DIM).astype(jnp.float32) * (MLSTM_HEAD_DIM ** -0.5)
        vm = to_heads(mv, MLSTM_HEADS, MLSTM_HEAD_DIM).astype(jnp.float32)
        i_pre = (mi + igate_b).astype(jnp.float32).transpose(0, 2, 1)
        f_pre = (mf + fgate_b).astype(jnp.float32).transpose(0, 2, 1)
        hm = mlstm_chunkwise(qm, km, vm, i_pre, f_pre)
        hm = hm.transpose(0, 2, 1, 3).astype(x.dtype)
        hm = rms_norm(hm, mlstm_norm_w.reshape(MLSTM_HEADS, MLSTM_HEAD_DIM)).reshape(B, S, MLSTM_W)
        hm = jax.nn.sigmoid(mo) * hm

        y = (jax.nn.sigmoid(ga + merge_b[0]) * (attn @ w_attn_branch)
             + jax.nn.sigmoid(gm + merge_b[1]) * (hm @ w_mlstm_branch))
        x = x + y @ w_out

        x = x + peer_ffn(rms_norm(x, ffn_norm_w), peer_w_query, peer_keys_1, peer_keys_2,
                         peer_w_down, peer_w_up)
    return x


_drawn_inputs = setup_inputs


def setup_inputs(seed=0):
    import zlib

    import numpy as np

    out = dict(_drawn_inputs(seed))
    spreads = {}
    factors = {'q_norm_w': 5.434,
     'k_norm_w': 4.594,
     'conv_b': 3.701,
     'igate_b': 64.0,
     'mlstm_norm_w': 2.921,
     'merge_b': 6.482}
    for name, (base, spread) in spreads.items():
        noise = np.random.default_rng([zlib.crc32(name.encode()), seed]).standard_normal(out[name].shape)
        drawn = base * np.exp(spread * noise) if base else spread * noise
        out[name] = __import__('jax').numpy.asarray(drawn.astype(out[name].dtype))
    for name, factor in factors.items():
        out[name] = (out[name] * factor).astype(out[name].dtype)
    return out
```

```python
from contextlib import ExitStack

import concourse.bass as bass
from concourse import mybir

T, D = 256, 1024
TT, KD = T // 128, D // 128
AH, AD = 8, 64
MH, MD = 4, 128
ROT = AD // 4
CONV = 4
PH, NK, TOPK = 8, 128, 16
EPS = 1e-6
BIG = 1e30
LOWEST = -3.4028234663852886e38

COL = {}
_at = 0
for _n, _w in (("aq", 512), ("ak", 512), ("av", 512), ("mq", 512), ("mk", 512), ("mv", 512),
               ("mo", 512), ("mi", MH), ("mf", MH), ("ga", D), ("gm", D)):
    COL[_n] = _at
    _at += _w

CW = 256
CE = KD * CW
CHUNKS = [(_n, _j) for _n, _k in (("mq", 2), ("mk", 2), ("aq", 2), ("ak", 2), ("av", 2), ("mv", 2),
                                  ("mo", 2), ("ga", 4), ("gm", 4), ("wab", 2), ("wmb", 2),
                                  ("wo", 4), ("wq", 8)) for _j in range(_k)]
INDEX = {_c: _i for _i, _c in enumerate(CHUNKS)}
BRANCH = ("wab", "wmb")
GROUPS = [(_c, _h) for _c in CHUNKS for _h in range(2 if _c[0] in BRANCH else 1)]
BY_DVE = ("wab", "wmb", "wo")
POOL_LO = 704

VEC = {}
_at = 0
for _n, _w in (("mixw", 8), ("cw", 32), ("cb", 8), ("mnw", 4), ("mb", 16), ("ffw", 8)):
    VEC[_n] = _at
    _at += _w
NVEC = _at

MISC = {}
for _n, _k in (("vec", 1), ("xT", 4), ("gates", 1), ("qkT", 4), ("S", 6), ("gcol", 1), ("negM", 2),
               ("ST", 3), ("PT", 6), ("PV", 2), ("num", 4), ("hmT", 2), ("key", 4), ("h2T", 4),
               ("sc", 8)):
    for _j in range(_k):
        MISC[_n, _j] = len(MISC)

XSS, QKSS, MSS, X2SS = 0, 2, 34, 42

UA = 8
NA = NK // UA
UG = 4
UC = 8


def groups_before(group, dve):
    return sum((c[0] in BY_DVE) == dve for c, _ in GROUPS[:group + 1])


def groups_through(n):
    return sum(len([g for g in GROUPS if g[0] == c]) for c in CHUNKS[:n + 1])


def build(nc, a, out):
    f32, f32r, bf16, u32 = mybir.dt.float32, mybir.dt.float32r, mybir.dt.bfloat16, mybir.dt.uint32
    ALU, ACT, AXX = mybir.AluOpType, mybir.ActivationFunctionType, mybir.AxisListType.X
    keep = ExitStack()
    sems = {}

    def S(name):
        if name not in sems:
            sems[name] = keep.enter_context(nc.semaphore(name))
        return sems[name]

    def sb(stack, name, shape, dt=f32):
        return stack.enter_context(nc.sbuf_tensor(name, shape, dt))

    def ps(stack, name, shape, dt=f32):
        return stack.enter_context(nc.psum_tensor(name, shape, dt))

    class Link:

        def __init__(self, eng, name):
            self.eng, self.sem, self.n = eng, S(name), 0

        def mark(self, ins):
            self.n += 1
            ins.then_inc(self.sem, 1)

        def settle(self):
            self.eng.wait_ge(self.sem, self.n)

        def __call__(self, ins):
            self.mark(ins)
            self.settle()

    def three(out_, lh, ll, rh, rl, start, stop):
        nc.tensor.matmul(out_, lh, rh, start=start, stop=False)
        nc.tensor.matmul(out_, lh, rl, start=False, stop=False)
        return nc.tensor.matmul(out_, ll, rh, start=False, stop=stop)

    with keep:
        x = sb(keep, "x", [128, TT, D])
        hTh = sb(keep, "hTh", [128, KD, T], f32r)
        hTl = sb(keep, "hTl", [128, KD, T], f32r)
        ident = sb(keep, "ident", [128, 128])
        sc = sb(keep, "sc", [128, TT, PH, 2, NK])

        front = ExitStack()
        with front:
            raw = sb(front, "raw", [128, 3, CE])
            whi = sb(front, "whi", [128, 2, CE], f32r)
            wlo = sb(front, "wlo", [128, 2, CE], f32r)
            vcol = sb(front, "vcol", [128, NVEC])
            minus_half = sb(front, "minus_half", [128, 32])
            stat = sb(front, "stat", [128, 64])
            work = sb(front, "work", [128, 2048])
            hq = sb(front, "hq", [128, KD, T])
            qk = sb(front, "qk", [128, TT, 2 * AH * AD])
            probT = sb(front, "probT", [128, 3072])
            cv = sb(front, "cv", [128, 2 * MH, T])
            upv = sb(front, "upv", [128, 2072])
            v = sb(front, "v", [128, TT, AH * AD])
            gsig = sb(front, "gsig", [128, 16, T])
            aTh = sb(front, "aTh", [128, 4, T], f32r)
            aTl = sb(front, "aTl", [128, 4, T], f32r)
            mTh = sb(front, "mTh", [128, 4, T], f32r)
            mTl = sb(front, "mTl", [128, 4, T], f32r)
            tri_q = sb(front, "tri_q", [128, 128])
            tri_s = sb(front, "tri_s", [128, 256])
            sel = sb(front, "sel", [MH, MH, 128])
            vrow = sb(front, "vrow", [NVEC, 128])
            qkw = sb(front, "qkw", [128, 2, AD])
            rot = sb(front, "rot", [128, TT, ROT])
            gbias = sb(front, "gbias", [MH, 2])
            wgate = sb(front, "wgate", [128, KD, 2 * MH])
            grow = sb(front, "grow", [MH, 6, T])
            gcol = sb(front, "gcol", [128, TT, 2, MH])
            den = sb(front, "den", [128, TT, MH])
            arow = sb(front, "arow", [128, 3, TT, AH])
            ones4 = sb(front, "ones4", [MH, T])
            proj = ps(front, "proj", [128, 4, 512])
            misc = ps(front, "misc", [128, 4, 512])

            up = upv[:].rearrange("p (c t) -> p c t", c=8)
            v1 = upv[:, 0:TT * MH * (MD + 1)].rearrange("p (t h c) -> p t h c", t=TT, h=MH)
            mosig = upv[:, 1032:1032 + 1024].rearrange("p (t c) -> p t c", t=TT)
            scf = sc[:].rearrange("p a b c d -> p (a b c d)")
            sig = scf[:, 0:2048].rearrange("p (c t) -> p c t", c=8)
            hwork = work[:].rearrange("p (t c) -> p t c", t=TT)
            dT0 = work[:, 0:1024].rearrange("p (h t) -> p h t", h=MH)
            dT1 = work[:, 1024:1536].rearrange("p (h t) -> p h t", h=MH)
            keyn = work[:].rearrange("p (b h d) -> p b h d", b=2, h=PH)
            p0 = scf[:, 0:1024].rearrange("p (h k) -> p h k", h=AH)
            p1 = scf[:, 1024:3072].rearrange("p (h k) -> p h k", h=AH)
            pT0 = probT[:, 0:2048].rearrange("p (h q) -> p h q", h=AH)
            pT1 = probT[:, 2048:3072].rearrange("p (h q) -> p h q", h=AH)
            keyT = probT[:, 0:2048].rearrange("p (b h n) -> p b h n", b=2, h=PH)
            aT = cv[:, 0:4, :]
            mT = cv[:, 4:8, :]
            hm = qk[:, :, 0:512]
            hsq = qk[:, :, 512:1024]
            rI, rLF, rTMP, rF, rG, rNM = range(6)

            def bank(name, i=0):
                return misc[:, MISC[name, i] % 4, :]

            def chunk_source(c):
                name, j = c
                if name in BRANCH:
                    src = a["w_attn_branch" if name == "wab" else "w_mlstm_branch"]
                    return src[:, j * 512:(j + 1) * 512].rearrange("(k p) n -> p k n", p=128)
                if name == "wo":
                    src, at = a["w_out"], j * CW
                elif name == "wq":
                    src, at = a["peer_w_query"], j * CW
                else:
                    src, at = a["w_in"], COL[name] + j * CW
                return src[:, at:at + CW].rearrange("(k p) n -> p k n", p=128)

            def as_chunk(flat, c):
                return flat.rearrange("p (k n) -> p k n", k=4 if c[0] in BRANCH else KD)

            blk = front.enter_context(nc.Block())

            @blk.sync
            def _(sp):
                for t in range(TT):
                    sp.dma_start(x[:, t, :], a["x"][0, t * 128:(t + 1) * 128, :]).then_inc(S("x_loaded%d" % t), 16)
                for n, c in enumerate(CHUNKS):
                    if n >= 3:
                        sp.wait_ge(S("hi_ready"), n - 2)
                        sp.wait_ge(S("lo_dve_ready"), n - 2)
                        sp.wait_ge(S("lo_pool_ready"), n - 2)
                    sp.dma_start(as_chunk(raw[:, n % 3, :], c), chunk_source(c)).then_inc(S("raw_loaded%d" % (n % 3)), 16)
                    if n == 0:
                        for name, src in (("mixw", a["mix_norm_w"]), ("cb", a["conv_b"]),
                                          ("mnw", a["mlstm_norm_w"]), ("ffw", a["ffn_norm_w"])):
                            rows = src.rearrange("(r c) -> r c", c=128)
                            sp.dma_start(vrow[VEC[name]:VEC[name] + rows.shape[0], :], rows).then_inc(S("vec_loaded"), 16)
                        for j in range(CONV):
                            sp.dma_start(vrow[VEC["cw"] + 8 * j:VEC["cw"] + 8 * j + 8, :],
                                         a["conv_w"][j, :].rearrange("(r c) -> r c", c=128)).then_inc(S("vec_loaded"), 16)
                        for j in range(2):
                            sp.dma_start(vrow[VEC["mb"] + 8 * j:VEC["mb"] + 8 * j + 8, :],
                                         a["merge_b"][j, :].rearrange("(r c) -> r c", c=128)).then_inc(S("vec_loaded"), 16)
                        sp.dma_start(qkw[:, 0, :], a["q_norm_w"].partition_broadcast(128)).then_inc(S("small_loaded"), 16)
                        sp.dma_start(qkw[:, 1, :], a["k_norm_w"].partition_broadcast(128)).then_inc(S("small_loaded"), 16)
                        sp.dma_start(rot[:], a["rope"].rearrange("(t p) r -> p t r", p=128)).then_inc(S("small_loaded"), 16)
                        sp.dma_start(gbias[:, 0:1], a["igate_b"].rearrange("(n o) -> n o", o=1)).then_inc(S("small_loaded"), 16)
                        sp.dma_start(gbias[:, 1:2], a["fgate_b"].rearrange("(n o) -> n o", o=1)).then_inc(S("small_loaded"), 16)
                        sp.dma_start(wgate[:], a["w_in"][:, COL["mi"]:COL["mi"] + 2 * MH].rearrange(
                            "(k p) n -> p k n", p=128)).then_inc(S("small_loaded"), 16)
                    if c == ("gm", 3):
                        sp.wait_ge(S("num_done"), 1)
                        sp.dma_start(keyn[:, 0], a["peer_keys_1"].rearrange("h n d -> n h d")).then_inc(S("key_loaded"), 16)
                        sp.dma_start(keyn[:, 1], a["peer_keys_2"].rearrange("h n d -> n h d")).then_inc(S("key_loaded"), 16)

            @blk.gpsimd
            def _(pool):
                link = Link(pool, "pool_link")
                g = nc.gpsimd
                link(g.memset(ident[:], 0.0))
                g.affine_select(out=ident[:], in_=ident[:], compare_op=ALU.not_equal, fill=1.0, base=0,
                                pattern=[[-1, 128]], channel_multiplier=1).then_inc(S("ident_ready"), 1)
                link.mark(g.memset(minus_half[:], -0.5))
                g.memset(up[:, :, 0:CONV - 1], 0.0).then_inc(S("pad_ready"), 1)
                g.memset(ones4[:], 1.0).then_inc(S("const_ready"), 1)
                link.mark(g.memset(tri_q[:], 0.0))
                link.mark(g.memset(tri_s[:], 0.0))
                link(g.memset(sel[:], 0.0))
                g.affine_select(out=tri_q[:], in_=tri_q[:], compare_op=ALU.is_ge, fill=-BIG, base=0,
                                pattern=[[-1, 128]], channel_multiplier=1).then_inc(S("const_ready"), 1)
                g.affine_select(out=tri_s[:], in_=tri_s[:], compare_op=ALU.is_ge, fill=-BIG, base=0,
                                pattern=[[1, 256]], channel_multiplier=-1).then_inc(S("const_ready"), 1)
                g.affine_select(out=sel[:], in_=sel[:], compare_op=ALU.not_equal, fill=1.0, base=0,
                                pattern=[[-1, MH], [0, 128]], channel_multiplier=1).then_inc(S("const_ready"), 1)

                def rsqrt(at, n, width, done):
                    link(g.tensor_scalar(stat[:, at:at + n], stat[:, at:at + n], 1.0 / width, EPS, ALU.mult, ALU.add))
                    g.tensor_tensor(stat[:, at:at + n], stat[:, at:at + n], minus_half[:, 0:n], ALU.pow).then_inc(S(done), 1)

                pool.wait_ge(S("x_squared"), 2)
                rsqrt(XSS, TT, D, "x_rstd")
                for n, c in enumerate(CHUNKS):
                    pool.wait_ge(S("raw_loaded%d" % (n % 3)), 16 * (n // 3 + 1))
                    pool.wait_ge(S("hi_ready"), n + 1)
                    if n >= 2:
                        pool.wait_ge(S("proj_done"), groups_through(n - 2))
                    g.tensor_tensor(wlo[:, n % 2, 0:POOL_LO], raw[:, n % 3, 0:POOL_LO],
                                    whi[:, n % 2, 0:POOL_LO].bitcast(f32), ALU.subtract).then_inc(S("lo_pool_ready"), 1)
                    if c in (("aq", 0), ("ak", 0)):
                        j = 0 if c[0] == "aq" else 1
                        pool.wait_ge(S("conv_sig"), j + 1)
                        g.tensor_tensor(cv[:, 4 * j:4 * j + 4, :], cv[:, 4 * j:4 * j + 4, :],
                                        sig[:, 4 * j:4 * j + 4, :], ALU.mult).then_inc(S("silu_done"), 1)
                    if c == ("av", 0):
                        pool.wait_ge(S("qk_squared"), 1)
                        rsqrt(QKSS, 32, AD, "qk_rstd")
                    if c == ("gm", 1):
                        pool.wait_ge(S("hm_squared"), 1)
                        rsqrt(MSS, 8, MD, "hm_rstd")
                    if c == ("wq", 0):
                        pool.wait_ge(S("x2_squared"), 2)
                        rsqrt(X2SS, TT, D, "x2_rstd")

            @blk.scalar
            def _(act):
                link = Link(act, "act_link")

                def hi(n):
                    act.wait_ge(S("raw_loaded%d" % (n % 3)), 16 * (n // 3 + 1))
                    if n >= 2:
                        act.wait_ge(S("proj_done"), groups_through(n - 2))
                        act.wait_ge(S("lo_dve_ready"), n - 1)
                        act.wait_ge(S("lo_pool_ready"), n - 1)
                    nc.scalar.activation(whi[:, n % 2, :], raw[:, n % 3, :], ACT.Copy).then_inc(S("hi_ready"), 1)

                def take(c):
                    name, j = c
                    g = GROUPS.index((c, 0))
                    bank2 = proj[:, g % 4, :].rearrange("p (i n) -> p i n", i=2)
                    act.wait_ge(S("proj_done"), g + 1)
                    if name in ("mq", "mk"):
                        at = (0 if name == "mq" else 4) + 2 * j
                        nc.scalar.activation(up[:, at:at + 2, CONV - 1:], bank2, ACT.Copy).then_inc(S("proj_taken_act"), 1)
                    elif name in ("aq", "ak"):
                        at = (0 if name == "aq" else 512) + CW * j
                        nc.scalar.activation(qk[:, :, at:at + CW], bank2, ACT.Copy).then_inc(S("proj_taken_act"), 1)
                    elif name == "av":
                        nc.scalar.activation(v[:, :, CW * j:CW * j + CW], bank2, ACT.Copy).then_inc(S("proj_taken_act"), 1)
                    elif name == "mv":
                        act.wait_ge(S("conv_done"), 2)
                        for t in range(TT):
                            last = nc.scalar.activation(v1[:, t, 2 * j:2 * j + 2, 0:MD],
                                                        bank2[:, t, :].rearrange("p (h c) -> p h c", h=2), ACT.Copy)
                            last.then_inc(*((S("proj_taken_act"), 1) if t else (S("v1_half"), 1)))
                    elif name == "mo":
                        nc.scalar.activation(mosig[:, :, CW * j:CW * j + CW], bank2, ACT.Sigmoid).then_inc(S("proj_taken_act"), 1)
                    elif name in ("ga", "gm"):
                        at = (0 if name == "ga" else 8) + 2 * j
                        for i in range(2):
                            b = VEC["mb"] + at + i
                            last = nc.scalar.activation(gsig[:, at + i, :], bank2[:, i, :], ACT.Sigmoid, bias=vcol[:, b:b + 1])
                            last.then_inc(*((S("proj_taken_act"), 1) if i else (S("gate_half"), 1)))
                    elif name == "wq":
                        act.wait_ge(S("y_ready"), 2)
                        nc.scalar.activation(gsig[:, 2 * j:2 * j + 2, :], bank2, ACT.Copy).then_inc(S("proj_taken_act"), 1)

                def split_hi(dst, src, bank_taken, done):
                    act.wait_ge(S("misc_free"), MISC[bank_taken] + 1)
                    nc.scalar.activation(dst, src, ACT.Copy).then_inc(S(done), 1)

                hi(0)
                for t in range(TT):
                    act.wait_ge(S("x_loaded%d" % t), 16)
                    nc.scalar.activation(hwork[:, t, :], x[:, t, :], ACT.Square,
                                         accum_out=stat[:, XSS + t:XSS + t + 1]).then_inc(S("x_squared"), 1)
                split_hi(hTh[:], hq[:], ("xT", 3), "h_hi")
                for n, c in enumerate(CHUNKS):
                    if n + 1 < len(CHUNKS):
                        hi(n + 1)
                    if c[0] not in BY_DVE:
                        take(c)
                    if c == ("mk", 1):
                        for j in range(2):
                            act.wait_ge(S("conv_done"), j + 1)
                            nc.scalar.activation(sig[:, 4 * j:4 * j + 4, :], cv[:, 4 * j:4 * j + 4, :],
                                                 ACT.Sigmoid).then_inc(S("conv_sig"), 1)
                    if c == ("aq", 0):
                        act.wait_ge(S("gates_read"), 1)
                        link(nc.scalar.activation(grow[:, rTMP, :], grow[:, rTMP, :], ACT.Exp, scale=-1.0))
                        nc.scalar.activation(grow[:, rTMP, :], grow[:, rTMP, :], ACT.Ln, bias=1.0).then_inc(S("softplus_done"), 1)
                    if c == ("mo", 1):
                        act.wait_ge(S("s_max"), 1)
                        for t, p in enumerate((p0, p1)):
                            for h in range(AH):
                                nc.scalar.activation(p[:, h, :], p[:, h, :], ACT.Exp, bias=arow[:, 1, t, h:h + 1], scale=AD ** -0.5,
                                                     accum_out=arow[:, 2, t, h:h + 1]).then_inc(S("p_exp"), 1)
                    if c == ("ga", 0):
                        act.wait_ge(S("misc_free"), MISC["negM", 1] + 1)
                        for h in range(MH):
                            nc.scalar.activation(dT0[:, h, :], dT0[:, h, :], ACT.Exp, bias=gcol[:, 0, 0, h:h + 1]).then_inc(S("decay"), 1)
                            nc.scalar.activation(dT1[:, h, :], dT1[:, h, :], ACT.Exp, bias=gcol[:, 1, 0, h:h + 1]).then_inc(S("decay"), 1)
                        nc.scalar.activation(gcol[:, :, 1, :], gcol[:, :, 1, :], ACT.Exp).then_inc(S("decay"), 1)
                    if c == ("gm", 2):
                        split_hi(aTh[:], aT, ("PV", 1), "aT_hi")
                    if c == ("wab", 1):
                        split_hi(mTh[:], mT, ("hmT", 1), "mT_hi")
                    if c == ("wmb", 1):
                        for j in range(2):
                            act.wait_ge(S("y_ready"), j + 1)
                            nc.scalar.activation(hTh[:, 4 * j:4 * j + 4, :], hq[:, 4 * j:4 * j + 4, :], ACT.Copy).then_inc(S("y_hi"), 1)
                    if c == ("wo", 3):
                        act.wait_ge(S("proj_taken_dve"), groups_before(len(GROUPS) - 1, True))
                        act.wait_ge(S("misc_free"), MISC["key", 3] + 1)
                        for t in range(TT):
                            nc.scalar.activation(hwork[:, t, :], x[:, t, :], ACT.Square,
                                                 accum_out=stat[:, X2SS + t:X2SS + t + 1]).then_inc(S("x2_squared"), 1)
                        for j in range(2):
                            split_hi(hTh[:, 4 * j:4 * j + 4, :], hq[:, 4 * j:4 * j + 4, :], ("h2T", 2 * j + 1), "h2_hi")

            @blk.vector
            def _(dve):
                link = Link(dve, "dve_link")
                V = nc.vector

                def lo(n):
                    dve.wait_ge(S("raw_loaded%d" % (n % 3)), 16 * (n // 3 + 1))
                    dve.wait_ge(S("hi_ready"), n + 1)
                    if n >= 2:
                        dve.wait_ge(S("proj_done"), groups_through(n - 2))
                    V.tensor_tensor(wlo[:, n % 2, POOL_LO:], raw[:, n % 3, POOL_LO:],
                                    whi[:, n % 2, POOL_LO:].bitcast(f32), ALU.subtract).then_inc(S("lo_dve_ready"), 1)

                def full(name, i=0):
                    dve.wait_ge(S("misc_full"), MISC[name, i] + 1)
                    return bank(name, i)

                def free(ins):
                    ins.then_inc(S("misc_free"), 1)

                def by2(ap):
                    return ap.rearrange("p (i n) -> p i n", i=2)

                free(V.tensor_copy(vcol[:], full("vec")[:, 0:NVEC]))
                dve.wait_ge(S("misc_free"), 1)
                dve.wait_ge(S("x_rstd"), 1)
                for t in range(TT):
                    dve.wait_ge(S("x_loaded%d" % t), 16)
                    V.tensor_scalar(hwork[:, t, :], x[:, t, :], stat[:, XSS + t:XSS + t + 1], None, ALU.mult).then_inc(S("h_nat"), 1)

                def weighted_transpose(name, vec):
                    for b in range(4):
                        src = by2(full(name, b))
                        for i in range(2):
                            k = 2 * b + i
                            ins = V.tensor_scalar(hq[:, k, :], src[:, i, :], vcol[:, VEC[vec] + k:VEC[vec] + k + 1], None, ALU.mult)
                        free(ins)

                weighted_transpose("xT", "mixw")
                dve.wait_ge(S("h_hi"), 1)
                V.tensor_tensor(hTl[:], hq[:], hTh[:].bitcast(f32), ALU.subtract).then_inc(S("h_lo"), 1)
                lo(0)
                for n, c in enumerate(CHUNKS):
                    if n + 1 < len(CHUNKS):
                        lo(n + 1)
                    if c in (("mk", 0), ("mk", 1)):
                        j = c[1]
                        dve.wait_ge(S("pad_ready"), 1)
                        dve.wait_ge(S("proj_taken_act"), 2 * j + 2)
                        for tap in range(CONV):
                            for i in range(4 * j, 4 * j + 4):
                                w = vcol[:, VEC["cw"] + 8 * tap + i:VEC["cw"] + 8 * tap + i + 1]
                                src = up[:, i, tap:tap + T]
                                if tap == 0:
                                    ins = V.tensor_scalar(cv[:, i, :], src, w, None, ALU.mult)
                                else:
                                    ins = V.scalar_tensor_tensor(out=cv[:, i, :], in0=src, scalar=w, in1=cv[:, i, :],
                                                                 op0=ALU.mult, op1=ALU.add)
                                link.mark(ins)
                            link.settle()
                        for i in range(4 * j, 4 * j + 4):
                            ins = V.tensor_scalar(cv[:, i, :], cv[:, i, :], vcol[:, VEC["cb"] + i:VEC["cb"] + i + 1], None, ALU.add)
                        ins.then_inc(S("conv_done"), 1)
                        if j == 1:
                            dve.wait_ge(S("small_loaded"), 96)
                            src = by2(full("gates"))
                            link.mark(V.tensor_scalar(grow[:, rI, :], src[0:MH, 0, :], gbias[:, 0:1], None, ALU.add))
                            free(V.tensor_scalar(grow[:, rLF, :], src[0:MH, 1, :], gbias[:, 1:2], None, ALU.add))
                            dve.wait_ge(S("misc_free"), MISC["gates", 0] + 1)
                            V.scalar_tensor_tensor(out=grow[:, rTMP, :], in0=grow[:, rLF, :], scalar=-1.0, in1=grow[:, rLF, :],
                                                   op0=ALU.mult, op1=ALU.max).then_inc(S("gates_read"), 1)
                    if c == ("aq", 1):
                        dve.wait_ge(S("softplus_done"), 1)
                        dve.wait_ge(S("const_ready"), 4)
                        link(V.scalar_tensor_tensor(out=grow[:, rLF, :], in0=grow[:, rLF, :], scalar=0.0, in1=grow[:, rTMP, :],
                                                    op0=ALU.min, op1=ALU.subtract))
                        link(V.tensor_tensor_scan(grow[:, rF, :], ones4[:], grow[:, rLF, :], 0.0, ALU.mult, ALU.add))
                        link(V.tensor_tensor(grow[:, rG, :], grow[:, rI, :], grow[:, rF, :], ALU.subtract))
                        link(V.tensor_tensor_scan(grow[:, rNM, :], grow[:, rG, :], grow[:, rG, :], 0.0, ALU.max, ALU.max))
                        link(V.scalar_tensor_tensor(out=grow[:, rTMP, :], in0=grow[:, rF, :], scalar=-1.0, in1=grow[:, rNM, :],
                                                    op0=ALU.mult, op1=ALU.subtract))
                        V.tensor_scalar(grow[:, rNM, :], grow[:, rNM, :], -1.0, None, ALU.mult).then_inc(S("gate_rows"), 1)
                    if c == ("ak", 1):
                        dve.wait_ge(S("proj_taken_act"), 8)
                        dve.wait_ge(S("h_hi"), 1)
                        link(V.tensor_tensor(hwork[:], qk[:], qk[:], ALU.mult))
                        V.tensor_reduce(stat[:, QKSS:QKSS + 32], hwork[:].rearrange("p t (h c) -> p (t h) c", c=AD), AXX,
                                        ALU.add).then_inc(S("qk_squared"), 1)
                    if c == ("mv", 0):
                        dve.wait_ge(S("qk_rstd"), 1)
                        qh = qk[:].rearrange("p t (h c) -> p (t h) c", c=AD)
                        link(V.tensor_tensor(qh, qh, stat[:, QKSS:QKSS + 32].unsqueeze(2).broadcast_to([128, 32, AD]), ALU.mult))
                        for t in range(TT):
                            for i in range(2):
                                q1 = qk[:, t, 512 * i:512 * i + 512].rearrange("p (h c) -> p h c", c=AD)
                                link.mark(V.tensor_tensor(q1, q1, qkw[:, i, :].unsqueeze(1).broadcast_to([128, AH, AD]), ALU.mult))
                        link.settle()
                        half = ROT // 2
                        for t in range(TT):
                            qt = qk[:, t, :].rearrange("p (h c) -> p h c", c=AD)
                            x1, x2 = qt[:, :, 0:half], qt[:, :, half:ROT]
                            cos = rot[:, t, 0:half].unsqueeze(1).broadcast_to([128, 2 * AH, half])
                            sin = rot[:, t, half:ROT].unsqueeze(1).broadcast_to([128, 2 * AH, half])
                            tmp = [hwork[:, t, 128 * i:128 * i + 128].rearrange("p (h c) -> p h c", c=half) for i in range(4)]
                            for i, (u, w) in enumerate(((x1, cos), (x2, sin), (x2, cos), (x1, sin))):
                                link.mark(V.tensor_tensor(tmp[i], u, w, ALU.mult))
                            link.settle()
                            link.mark(V.tensor_tensor(x1, tmp[0], tmp[1], ALU.subtract))
                            V.tensor_tensor(x2, tmp[2], tmp[3], ALU.add).then_inc(S("qk_ready"), 1)
                        link.settle()
                    if c == ("mv", 1):
                        dve.wait_ge(S("conv_done"), 2)
                        V.memset(v1[:, :, :, MD:MD + 1], 1.0).then_inc(S("v1_ones"), 1)
                        for b in range(4):
                            src = by2(full("qkT", b))
                            free(V.tensor_copy(hq[:, 2 * b:2 * b + 2, :], src))
                    if c == ("mo", 1):
                        dve.wait_ge(S("silu_done"), 2)
                        for b in range(2):
                            src = full("S", b).rearrange("p (h k) -> p h k", h=4)
                            free(V.tensor_tensor(p0.rearrange("p (i o) k -> p o i k", o=2)[:, b], src, tri_q[:].unsqueeze(1).broadcast_to([128, 4, 128]), ALU.add))
                        for b in range(4):
                            src = full("S", 2 + b).rearrange("p (h k) -> p h k", h=2)
                            dst = p1.rearrange("p (q i o) k -> p q o i k", i=2, o=2)[:, b // 2, b % 2]
                            link.mark(V.tensor_copy(dst[:, :, 0:128], src[:, :, 0:128]))
                            free(V.tensor_tensor(dst[:, :, 128:256], src[:, :, 128:256],
                                                 tri_q[:].unsqueeze(1).broadcast_to([128, 2, 128]), ALU.add))
                        link.settle()
                        dve.wait_ge(S("misc_free"), MISC["S", 5] + 1)
                        link.mark(V.tensor_reduce(arow[:, 0, 0, :], p0, AXX, ALU.max))
                        link.mark(V.tensor_reduce(arow[:, 0, 1, :], p1, AXX, ALU.max))
                        link.settle()
                        V.tensor_scalar(arow[:, 1], arow[:, 0], -(AD ** -0.5), None, ALU.mult).then_inc(S("s_max"), 1)
                    if c == ("ga", 0):
                        free(V.tensor_copy(gcol[:].rearrange("p t a h -> p (t a h)"), full("gcol")[:, 0:16]))
                        for b in range(2):
                            src = by2(full("negM", b))
                            V.tensor_tensor(dT0[:, 2 * b:2 * b + 2, :], src, tri_s[:].unsqueeze(1).broadcast_to([128, 2, 256]), ALU.add)
                            free(V.tensor_tensor(dT1[:, 2 * b:2 * b + 2, :], src[:, :, 128:256],
                                                 tri_s[:, 0:128].unsqueeze(1).broadcast_to([128, 2, 128]), ALU.add))
                        dve.wait_ge(S("p_exp"), 16)
                        link(V.reciprocal(arow[:, 0], arow[:, 2]))
                        for t, p in enumerate((p0, p1)):
                            V.tensor_tensor(p, p, arow[:, 0, t, :].unsqueeze(2).broadcast_to([128, AH, 128 * (t + 1)]),
                                            ALU.mult).then_inc(S("p_ready"), 1)
                    if c == ("ga", 1):
                        dve.wait_ge(S("decay"), 9)
                        for b in range(2):
                            src = by2(full("ST", b))
                            free(V.scalar_tensor_tensor(out=dT0[:, 2 * b:2 * b + 2, :], in0=src, scalar=MD ** -0.5,
                                                        in1=dT0[:, 2 * b:2 * b + 2, :], op0=ALU.mult, op1=ALU.mult))
                        src = full("ST", 2).rearrange("p (h t) -> p h t", h=MH)
                        free(V.scalar_tensor_tensor(out=dT1, in0=src, scalar=MD ** -0.5, in1=dT1, op0=ALU.mult, op1=ALU.mult))
                    if c == ("ga", 2):
                        for b in range(6):
                            src = full("PT", b).rearrange("p (h k) -> p h k", h=4)
                            if b < 2:
                                dst = pT0[:, 4 * b:4 * b + 4, 0:128]
                            elif b < 4:
                                dst = pT0[:, 4 * (b - 2):4 * (b - 2) + 4, 128:256]
                            else:
                                dst = pT1[:, 4 * (b - 4):4 * (b - 4) + 4, :]
                            free(V.tensor_copy(dst, src))
                    if c == ("gm", 0):
                        for b in range(2):
                            free(V.tensor_copy(aT[:, 2 * b:2 * b + 2, :], by2(full("PV", b))))
                        for b in range(4):
                            t, hp = b // 2, b % 2
                            src = by2(full("num", b))
                            dd = den[:, t, 2 * hp:2 * hp + 2]
                            link(V.scalar_tensor_tensor(out=dd, in0=src[:, :, MD], scalar=-1.0,
                                                        in1=gcol[:, t, 1, 2 * hp:2 * hp + 2], op0=ALU.mult, op1=ALU.max))
                            link(V.tensor_tensor(dd, src[:, :, MD], dd, ALU.max))
                            link(V.reciprocal(dd, dd))
                            free(V.tensor_tensor(hm[:, t, 256 * hp:256 * hp + 256].rearrange("p (h c) -> p h c", h=2), src[:, :, 0:MD],
                                                 dd.unsqueeze(2).broadcast_to([128, 2, MD]), ALU.mult))
                        dve.wait_ge(S("misc_free"), MISC["num", 3] + 1)
                        link(V.tensor_tensor(hsq, hm, hm, ALU.mult))
                        for t in range(TT):
                            ins = V.tensor_reduce(stat[:, MSS + 4 * t:MSS + 4 * t + 4], hsq[:, t, :].rearrange("p (h c) -> p h c", h=MH), AXX, ALU.add)
                            if t == 0:
                                link(ins)
                        ins.then_inc(S("hm_squared"), 1)
                    if c == ("gm", 2):
                        dve.wait_ge(S("aT_hi"), 1)
                        V.tensor_tensor(aTl[:], aT, aTh[:].bitcast(f32), ALU.subtract).then_inc(S("aT_lo"), 1)
                    if c == ("gm", 3):
                        dve.wait_ge(S("hm_rstd"), 1)
                        for t in range(TT):
                            hh = hm[:, t, :].rearrange("p (h c) -> p h c", h=MH)
                            link.mark(V.tensor_tensor(hh, hh, stat[:, MSS + 4 * t:MSS + 4 * t + 4].unsqueeze(2).broadcast_to([128, MH, MD]), ALU.mult))
                        link.settle()
                        V.tensor_tensor(hm, hm, mosig, ALU.mult).then_inc(S("hm_ready"), 1)
                        for b in range(2):
                            src = by2(full("hmT", b))
                            for i in range(2):
                                h = 2 * b + i
                                ins = V.tensor_scalar(mT[:, h, :], src[:, i, :], vcol[:, VEC["mnw"] + h:VEC["mnw"] + h + 1], None, ALU.mult)
                            free(ins)
                        for b in range(4):
                            free(V.tensor_copy(keyT[:, b // 2, 4 * (b % 2):4 * (b % 2) + 4, :],
                                               full("key", b).rearrange("p (h n) -> p h n", h=4)))
                    if c == ("wab", 0):
                        dve.wait_ge(S("mT_hi"), 1)
                        V.tensor_tensor(mTl[:], mT, mTh[:].bitcast(f32), ALU.subtract).then_inc(S("mT_lo"), 1)
                    if c[0] in BRANCH:
                        for half in range(2):
                            g = GROUPS.index((c, half))
                            at = 4 * c[1] + 2 * half
                            dve.wait_ge(S("proj_done"), g + 1)
                            dve.wait_ge(S("proj_taken_act"), groups_before(g, False))
                            src = by2(proj[:, g % 4, :])
                            if c[0] == "wab":
                                V.tensor_tensor(hq[:, at:at + 2, :], gsig[:, at:at + 2, :], src, ALU.mult).then_inc(S("proj_taken_dve"), 1)
                            else:
                                V.tensor_tensor(gsig[:, 8 + at:10 + at, :], gsig[:, 8 + at:10 + at, :], src, ALU.mult).then_inc(S("proj_taken_dve"), 1)
                                dve.wait_ge(S("proj_taken_dve"), groups_before(g, True))
                                ins = V.tensor_tensor(hq[:, at:at + 2, :], hq[:, at:at + 2, :], gsig[:, 8 + at:10 + at, :], ALU.add)
                                if half == 0:
                                    link(ins)
                                else:
                                    ins.then_inc(S("y_ready"), 1)
                    if c == ("wmb", 1):
                        for j in range(2):
                            dve.wait_ge(S("y_hi"), j + 1)
                            V.tensor_tensor(hTl[:, 4 * j:4 * j + 4, :], hq[:, 4 * j:4 * j + 4, :], hTh[:, 4 * j:4 * j + 4, :].bitcast(f32),
                                            ALU.subtract).then_inc(S("y_lo"), 1)
                    if c[0] == "wo":
                        g = GROUPS.index((c, 0))
                        dve.wait_ge(S("proj_done"), g + 1)
                        xx = x[:, :, CW * c[1]:CW * c[1] + CW]
                        V.tensor_tensor(xx, xx, by2(proj[:, g % 4, :]), ALU.add).then_inc(S("proj_taken_dve"), 1)
                        if c[1] == 3:
                            dve.wait_ge(S("proj_taken_dve"), groups_before(g, True))
                            dve.wait_ge(S("x2_rstd"), 1)
                            for t in range(TT):
                                V.tensor_scalar(hwork[:, t, :], x[:, t, :], stat[:, X2SS + t:X2SS + t + 1], None, ALU.mult).then_inc(S("h_nat"), 1)
                            weighted_transpose("h2T", "ffw")
                            for j in range(2):
                                dve.wait_ge(S("h2_hi"), j + 1)
                                V.tensor_tensor(hTl[:, 4 * j:4 * j + 4, :], hq[:, 4 * j:4 * j + 4, :], hTh[:, 4 * j:4 * j + 4, :].bitcast(f32),
                                                ALU.subtract).then_inc(S("h2_lo"), 1)
                for b in range(8):
                    free(V.tensor_copy(sc[:, b // 4, 4 * (b % 2):4 * (b % 2) + 4, (b // 2) % 2, :],
                                       full("sc", b).rearrange("p (h n) -> p h n", h=4)))

            @blk.tensor
            def _(pe):
                mm = nc.tensor.matmul

                def use(name, i=0):
                    if MISC[name, i] >= 4:
                        pe.wait_ge(S("misc_free"), MISC[name, i] - 3)
                    return bank(name, i)

                def filled(ins):
                    ins.then_inc(S("misc_full"), 1)

                def transposes(name, src, n, ready=None):
                    for b in range(n):
                        dst = use(name, b)
                        for i in range(4):
                            last = nc.tensor.transpose(dst[:, 128 * i:128 * i + 128], src(2 * b + i // 2, i % 2), ident[:])
                        filled(last)

                pe.wait_ge(S("ident_ready"), 1)
                pe.wait_ge(S("vec_loaded"), 16 * 10)
                filled(nc.tensor.transpose(use("vec")[:, 0:NVEC], vrow[:], ident[0:NVEC, 0:NVEC]))
                pe.wait_ge(S("h_nat"), 2)
                transposes("xT", lambda k, t: hwork[:, t, 128 * k:128 * k + 128], 4)
                pe.wait_ge(S("h_lo"), 1)
                for n, c in enumerate(CHUNKS):
                    name, j = c
                    if c == ("wab", 0):
                        pe.wait_ge(S("aT_lo"), 1)
                    if c == ("wmb", 0):
                        pe.wait_ge(S("mT_lo"), 1)
                    if c == ("wo", 0):
                        pe.wait_ge(S("y_lo"), 2)
                    if c == ("wq", 0):
                        pe.wait_ge(S("h_nat"), 4)
                        transposes("h2T", lambda k, t: hwork[:, t, 128 * k:128 * k + 128], 4)
                        pe.wait_ge(S("h2_lo"), 2)
                    pe.wait_ge(S("hi_ready"), n + 1)
                    pe.wait_ge(S("lo_dve_ready"), n + 1)
                    pe.wait_ge(S("lo_pool_ready"), n + 1)
                    wh, wl = as_chunk(whi[:, n % 2, :], c), as_chunk(wlo[:, n % 2, :], c)
                    parts = [g for g in GROUPS if g[0] == c]
                    for gr in parts:
                        g = GROUPS.index(gr)
                        if g >= 4:
                            old = g - 4
                            by_dve = GROUPS[old][0][0] in BY_DVE
                            pe.wait_ge(S("proj_taken_dve" if by_dve else "proj_taken_act"), groups_before(old, by_dve))
                        for i in range(2):
                            dst = proj[:, g % 4, 256 * i:256 * i + 256]
                            for k in range(4 if name in BRANCH else KD):
                                f = dict(start=k == 0, stop=k == (3 if name in BRANCH else KD - 1))
                                if name in BRANCH:
                                    th, tl = (aTh, aTl) if name == "wab" else (mTh, mTl)
                                    at = 256 * gr[1] + 128 * i
                                    last = three(dst, wh[:, k, at:at + 128], wl[:, k, at:at + 128], th[:, k, :], tl[:, k, :], **f)
                                elif name in ("aq", "ak", "av", "mv", "mo", "wo"):
                                    tk = slice(128 * i, 128 * i + 128)
                                    last = three(dst, hTh[:, k, tk], hTl[:, k, tk], wh[:, k, :], wl[:, k, :], **f)
                                else:
                                    at = 128 * i
                                    last = three(dst, wh[:, k, at:at + 128], wl[:, k, at:at + 128], hTh[:, k, :], hTl[:, k, :], **f)
                        last.then_inc(S("proj_done"), 1)
                    if c == ("mk", 1):
                        pe.wait_ge(S("small_loaded"), 96)
                        dst = use("gates")
                        for i in range(2):
                            for k in range(KD):
                                last = mm(dst[0:MH, 256 * i:256 * i + 256], wgate[:, k, MH * i:MH * i + MH], hq[:, k, :],
                                          start=k == 0, stop=k == KD - 1)
                        filled(last)
                    if c == ("mv", 1):
                        pe.wait_ge(S("qk_ready"), 2)
                        transposes("qkT", lambda k, t: qk[:, t, 128 * k:128 * k + 128], 4)
                    if c == ("mo", 1):
                        pe.wait_ge(S("misc_free"), MISC["qkT", 3] + 1)
                        for t in range(TT):
                            per, w = (4, 128) if t == 0 else (2, 256)
                            for b in range(AH // per):
                                dst = use("S", b + 2 * t)
                                rows = slice(64 * (b % 2), 64 * (b % 2) + 64)
                                for i in range(per):
                                    pr = per * (b // 2) + i
                                    last = mm(dst[:, i * w:i * w + w], hq[rows, pr, 128 * t:128 * t + 128], hq[rows, 4 + pr, 0:w],
                                              start=True, stop=True)
                                filled(last)
                        pe.wait_ge(S("gate_rows"), 1)
                        dst = use("gcol")
                        for t in range(TT):
                            for i, r in enumerate((rG, rTMP)):
                                at = 8 * t + 4 * i
                                last = mm(dst[:, at:at + MH], grow[:, r, 128 * t:128 * t + 128], ident[0:MH, 0:MH], start=True, stop=True)
                        filled(last)
                        for h in range(MH):
                            if h % 2 == 0:
                                dst = use("negM", h // 2)
                            last = mm(dst[:, 256 * (h % 2):256 * (h % 2) + 256], sel[:, h, :], grow[:, rNM, :], start=True, stop=True)
                            if h % 2:
                                filled(last)
                    if c == ("ga", 0):
                        pe.wait_ge(S("silu_done"), 2)
                        for h in range(MH):
                            if h % 2 == 0:
                                dst = use("ST", h // 2)
                            last = mm(dst[:, 256 * (h % 2):256 * (h % 2) + 256], cv[:, MH + h, 0:128], cv[:, h, :], start=True, stop=True)
                            if h % 2:
                                filled(last)
                        dst = use("ST", 2)
                        for h in range(MH):
                            last = mm(dst[:, 128 * h:128 * h + 128], cv[:, MH + h, 128:256], cv[:, h, 128:256], start=True, stop=True)
                        filled(last)
                    if c == ("ga", 1):
                        pe.wait_ge(S("p_ready"), 2)
                        for b in range(6):
                            dst = use("PT", b)
                            for i in range(4):
                                h = 4 * (b % 2) + i
                                src = p0[:, h, :] if b < 2 else p1[:, h, 128 * (b // 4):128 * (b // 4) + 128]
                                last = nc.tensor.transpose(dst[:, 128 * i:128 * i + 128], src, ident[:])
                            filled(last)
                    if c == ("ga", 3):
                        pe.wait_ge(S("misc_free"), MISC["PT", 5] + 1)
                        pe.wait_ge(S("proj_taken_act"), 10)
                        for h in range(AH):
                            if h % 4 == 0:
                                dst = use("PV", h // 4)
                            rows = slice(64 * (h % 2), 64 * (h % 2) + 64)
                            at = 256 * ((h // 2) % 2)
                            mm(dst[rows, at:at + 256], v[:, 0, AD * h:AD * h + AD], pT0[:, h, :], start=True, stop=False)
                            last = mm(dst[rows, at + 128:at + 256], v[:, 1, AD * h:AD * h + AD], pT1[:, h, :], start=False, stop=True)
                            if h % 4 == 3:
                                filled(last)
                        pe.wait_ge(S("v1_ones"), 1)
                        pe.wait_ge(S("v1_half"), 2)
                        pe.wait_ge(S("proj_taken_act"), 12)
                        for b in range(4):
                            t, hp = b // 2, b % 2
                            dst = use("num", b)
                            for i in range(2):
                                h = 2 * hp + i
                                o = dst[:, 256 * i:256 * i + MD + 1]
                                last = mm(o, dT0[:, h, 128 * t:128 * t + 128], v1[:, 0, h, :], start=True, stop=t == 0)
                                if t == 1:
                                    last = mm(o, dT1[:, h, :], v1[:, 1, h, :], start=False, stop=True)
                            filled(last)
                        pe.wait_ge(S("misc_full"), MISC["num", 3] + 1)
                        pe.sem_inc(S("num_done"), 1)
                    if c == ("gm", 3):
                        pe.wait_ge(S("hm_ready"), 1)
                        transposes("hmT", lambda k, t: hm[:, t, 128 * k:128 * k + 128], 2)
                        pe.wait_ge(S("key_loaded"), 32)
                        for b in range(4):
                            dst = use("key", b)
                            for i in range(4):
                                last = nc.tensor.transpose(dst[:, 128 * i:128 * i + 128], keyn[:, b // 2, 4 * (b % 2) + i, :], ident[:])
                            filled(last)
                pe.wait_ge(S("proj_taken_act"), groups_before(len(GROUPS) - 1, False))
                pe.wait_ge(S("misc_free"), MISC["key", 3] + 1)
                for b in range(8):
                    t, half, hh = b // 4, (b // 2) % 2, b % 2
                    dst = use("sc", b)
                    for i in range(4):
                        h = 4 * hh + i
                        last = mm(dst[:, 128 * i:128 * i + 128], gsig[:, 2 * h + half, 128 * t:128 * t + 128], keyT[:, half, h, :],
                                  start=True, stop=True)
                    filled(last)
        build_peer(nc, a, out, keep, S, Link, three, sb, ps, x, hTh, hTl, ident, sc)


def build_peer(nc, a, out, keep, S, Link, three, sb, ps, x, hTh, hTl, ident, sc):
    f32, f32r, bf16, u32 = mybir.dt.float32, mybir.dt.float32r, mybir.dt.bfloat16, mybir.dt.uint32
    ALU, ACT, AXX = mybir.AluOpType, mybir.ActivationFunctionType, mybir.AxisListType.X
    w_down = a["peer_w_down"].rearrange("(p e) d -> p (e d)", e=NK)
    w_up = a["peer_w_up"].rearrange("(p e) d -> p (e d)", e=NK)
    V = nc.vector
    UNITS = TT * PH

    def wait(eng, name, u, per, at):
        if not (isinstance(u, int) and u * per + at <= 0):
            eng.wait_ge(S(name), u * per + at)

    def steps(eng, n, body):
        body(0)
        with eng.Fori(1, n - 1) as u:
            body(u)
        body(n - 1)

    peer = ExitStack()
    with peer:
        act_all = sb(peer, "act_all", [128, NK, T])
        idx = sb(peer, "idx", [128, 2, UNITS, TOPK], u32)
        pair = sb(peer, "pair", [128, UNITS, TOPK], u32)
        best = sb(peer, "best", [128, UNITS, TOPK])

        down = ExitStack()
        with down:
            wd = sb(down, "wd", [128, 2, D])
            wTh = sb(down, "wTh", [128, 2, KD, 128], f32r)
            wTl = sb(down, "wTl", [128, 2, KD, 128], f32r)
            score = sb(down, "score", [128, 2, NK])
            val = sb(down, "val", [128, 2, TOPK])
            cand = sb(down, "cand", [128, TOPK * TOPK])
            ix = sb(down, "ix", [128, 3, TOPK], u32)
            top = sb(down, "top", [128, TOPK])
            tps = ps(down, "tps", [128, 2, KD, 128])
            ups = ps(down, "ups", [128, 2, 512])
            blk = down.enter_context(nc.Block())

            @blk.sync
            def _(sp):
                def body(u):
                    for j in range(UA):
                        wait(sp, "wd_transposed", u, UA, j - 1)
                        sp.dma_start(wd[:, j % 2, :], w_down[:, bass.ds((u * UA + j) * D, D)]).then_inc(S("wd_loaded%d" % (j % 2)), 16)
                steps(sp, NA, body)

            @blk.tensor
            def _(pe):
                def transpose_tile(u, m):
                    wait(pe, "wd_loaded%d" % (m % 2), u, 16 * UA // 2, 16 * (m // 2 + 1))
                    wait(pe, "wT_hi", u, UA, m - 1)
                    wait(pe, "wT_lo", u, UA, m - 1)
                    for k in range(KD):
                        last = nc.tensor.transpose(tps[:, m % 2, k, :], wd[:, m % 2, 128 * k:128 * k + 128], ident[:])
                    last.then_inc(S("wd_transposed"), 1)

                def body(u):
                    for j in range(UA):
                        if not (isinstance(u, int) and u == NA - 1 and j == UA - 1):
                            transpose_tile(u, j + 1)
                        wait(pe, "wT_hi", u, UA, j + 1)
                        wait(pe, "wT_lo", u, UA, j + 1)
                        wait(pe, "gelu_done", u, UA, j - 1)
                        for k in range(KD):
                            last = three(ups[:, j % 2, 0:T], wTh[:, j % 2, k, :], wTl[:, j % 2, k, :], hTh[:, k, :], hTl[:, k, :],
                                         start=k == 0, stop=k == KD - 1)
                        last.then_inc(S("u_done"), 1)

                transpose_tile(0, 0)
                steps(pe, NA, body)

            @blk.scalar
            def _(act):
                def hi(u, m):
                    wait(act, "wd_transposed", u, UA, m + 1)
                    wait(act, "u_done", u, UA, m - 1)
                    nc.scalar.activation(wTh[:, m % 2], tps[:, m % 2], ACT.Copy).then_inc(S("wT_hi"), 1)

                def body(u):
                    for j in range(UA):
                        if not (isinstance(u, int) and u == NA - 1 and j == UA - 1):
                            hi(u, j + 1)
                        wait(act, "u_done", u, UA, j + 1)
                        nc.scalar.activation(act_flat[:, bass.ds((u * UA + j) * T, T)], ups[:, j % 2, 0:T], ACT.Gelu).then_inc(S("gelu_done"), 1)

                act_flat = act_all[:].rearrange("p e t -> p (e t)")
                hi(0, 0)
                steps(act, NA, body)

            @blk.vector
            def _(dve):
                PER = 21

                def lo(u, m):
                    wait(dve, "wT_hi", u, UA, m + 1)
                    wait(dve, "u_done", u, UA, m - 1)
                    V.tensor_tensor(wTl[:, m % 2], tps[:, m % 2], wTh[:, m % 2].bitcast(f32), ALU.subtract).then_inc(S("wT_lo"), 1)

                def choice(u):
                    done = [0]

                    def mark(ins):
                        ins.then_inc(S("choice_step"), 1)
                        done[0] += 1

                    def settle():
                        wait(dve, "choice_step", u, PER, done[0])
                        dve.sem_inc(S("choice_go"), 1)

                    flat = sc[:].rearrange("p t h b n -> p (t h b n)")
                    mark(V.tensor_copy(score[:], flat[:, bass.ds(u * 2 * NK, 2 * NK)].rearrange("p (b n) -> p b n", b=2)))
                    settle()
                    yield
                    for r in range(2):
                        eight = slice(8 * r, 8 * r + 8)
                        for b in range(2):
                            mark(V.max(val[:, b, eight], score[:, b, :]))
                        settle()
                        yield
                        for b in range(2):
                            mark(V.max_index(ix[:, b, eight], val[:, b, eight], score[:, b, :]))
                        settle()
                        if r == 0:
                            for b in range(2):
                                mark(V.match_replace(score[:, b, :], val[:, b, eight], score[:, b, :], LOWEST))
                            settle()
                            yield
                    grid = cand[:].rearrange("p (i j) -> p i j", i=TOPK)
                    mark(V.tensor_tensor(grid, val[:, 0, :].unsqueeze(2).broadcast_to([128, TOPK, TOPK]),
                                         val[:, 1, :].unsqueeze(1).broadcast_to([128, TOPK, TOPK]), ALU.add))
                    settle()
                    yield
                    for r in range(2):
                        eight = slice(8 * r, 8 * r + 8)
                        mark(V.max(top[:, eight], cand[:]))
                        settle()
                        mark(V.max_index(ix[:, 2, eight], top[:, eight], cand[:]))
                        settle()
                        yield
                        if r == 0:
                            mark(V.match_replace(cand[:], top[:, eight], cand[:], LOWEST))
                            settle()
                    at = bass.ds(u * TOPK, TOPK)
                    mark(V.tensor_copy(idx[:, 0].rearrange("p u k -> p (u k)")[:, at], ix[:, 0, :]))
                    mark(V.tensor_copy(idx[:, 1].rearrange("p u k -> p (u k)")[:, at], ix[:, 1, :]))
                    mark(V.tensor_copy(pair[:].rearrange("p u k -> p (u k)")[:, at], ix[:, 2, :]))
                    mark(V.tensor_copy(best[:].rearrange("p u k -> p (u k)")[:, at], top[:]))
                    settle()
                    assert done[0] == PER, done
                    yield

                def body(u):
                    parts = choice(u)
                    for j in range(UA):
                        if not (isinstance(u, int) and u == NA - 1 and j == UA - 1):
                            lo(u, j + 1)
                        next(parts, None)
                    for _ in parts:
                        pass

                lo(0, 0)
                steps(dve, NA, body)

        gate = ExitStack()
        with gate:
            iota16 = sb(gate, "iota16", [128, TOPK])
            iota128 = sb(gate, "iota128", [128, NK], bf16)
            part = sb(gate, "part", [128, 2, UNITS * TOPK], u32)
            partf = sb(gate, "partf", [128, 2, UNITS * TOPK])
            idxf = sb(gate, "idxf", [128, 2, UNITS * TOPK])
            hit = sb(gate, "hit", [128, PH * TOPK, TOPK])
            chosen = sb(gate, "chosen", [128, 3, UNITS * TOPK])
            total = sb(gate, "total", [128, UNITS])
            chosenT = sb(gate, "chosenT", [128, 3, T])
            gpart = sb(gate, "gpart", [128, 3, T])
            gbf = sb(gate, "gbf", [128, T], bf16)
            one1 = sb(gate, "one1", [128, 2, UG, NK], bf16)
            one2 = sb(gate, "one2", [128, 2, UG, 3, NK], bf16)
            gps = ps(gate, "gps", [128, 4, UG, NK])
            cps = ps(gate, "cps", [128, 3, 512])
            blk = gate.enter_context(nc.Block())
            NG, PG = T // (4 * UG), 4

            @blk.gpsimd
            def _(pool):
                nc.gpsimd.iota(iota16[:], [[1, TOPK]], base=0, channel_multiplier=0, allow_small_or_imprecise_dtypes=True).then_inc(S("iotas"), 1)
                nc.gpsimd.iota(iota128[:], [[1, NK]], base=0, channel_multiplier=0, allow_small_or_imprecise_dtypes=True).then_inc(S("iotas"), 1)

            @blk.scalar
            def _(act):
                act.wait_ge(S("logits"), 1)
                nc.scalar.activation(chosen[:, 2, :], chosen[:, 2, :], ACT.Exp).then_inc(S("gate_exp"), 1)

            @blk.tensor
            def _(pe):
                pe.wait_ge(S("chosen_ready"), 1)
                for i in range(3):
                    for t in range(TT):
                        last = nc.tensor.transpose(cps[:, i, 128 * t:128 * t + 128], chosen[:, i, 128 * t:128 * t + 128], ident[:])
                last.then_inc(S("chosen_transposed"), 1)

                def body(u):
                    for j in range(PG):
                        wait(pe, "ones_ready", u, PG, j + 1)
                        wait(pe, "gates_used", u, PG, j - 3)
                        for i in range(UG):
                            for p in range(3):
                                last = nc.tensor.matmul(gps[:, j, i, :], one1[:, j % 2, i, :], one2[:, j % 2, i, p, :], start=p == 0, stop=p == 2)
                        last.then_inc(S("gates_done"), 1)

                steps(pe, NG, body)

            @blk.vector
            def _(dve):
                link = Link(dve, "gate_link")
                flat = lambda ap: ap.rearrange("p u k -> p (u k)")
                dve.wait_ge(S("iotas"), 2)
                V.tensor_tensor(chosen[:, 2, :].rearrange("p (u k) -> p u k", u=UNITS), best[:],
                                best[:, :, 0:1].broadcast_to([128, UNITS, TOPK]), ALU.subtract).then_inc(S("logits"), 1)
                link.mark(V.tensor_scalar(part[:, 0, :], flat(pair[:]), 4, None, ALU.logical_shift_right))
                link.mark(V.tensor_scalar(part[:, 1, :], flat(pair[:]), TOPK - 1, None, ALU.bitwise_and))
                link.mark(V.tensor_copy(idxf[:], idx[:].rearrange("p b u k -> p b (u k)")))
                link.settle()
                link(V.tensor_copy(partf[:], part[:]))
                for b in range(2):
                    for t in range(TT):
                        own, n = slice(PH * TOPK * t, PH * TOPK * (t + 1)), PH * TOPK
                        link(V.tensor_tensor(hit[:], partf[:, b, own].unsqueeze(2).broadcast_to([128, n, TOPK]),
                                             iota16[:].unsqueeze(1).broadcast_to([128, n, TOPK]), ALU.is_equal))
                        hit4 = hit[:].rearrange("p (h k) r -> p h k r", h=PH)
                        link(V.tensor_tensor(hit4, hit4, idxf[:, b, own].rearrange("p (h r) -> p h r", h=PH).unsqueeze(2)
                                             .broadcast_to([128, PH, TOPK, TOPK]), ALU.mult))
                        link(V.tensor_reduce(chosen[:, b, own], hit[:], AXX, ALU.add))
                dve.wait_ge(S("gate_exp"), 1)
                g3 = chosen[:, 2, :].rearrange("p (u k) -> p u k", u=UNITS)
                link(V.tensor_reduce(total[:], g3, AXX, ALU.add))
                link(V.reciprocal(total[:], total[:]))
                V.tensor_tensor(g3, g3, total[:].unsqueeze(2).broadcast_to([128, UNITS, TOPK]), ALU.mult).then_inc(S("chosen_ready"), 1)
                dve.wait_ge(S("chosen_transposed"), 1)
                link(V.tensor_copy(chosenT[:], cps[:, :, 0:T]))
                for p in range(3):
                    link(V.tensor_copy(gbf[:], chosenT[:, 2, :]))
                    link(V.tensor_copy(gpart[:, p, :], gbf[:]))
                    if p < 2:
                        link(V.tensor_tensor(chosenT[:, 2, :], chosenT[:, 2, :], gpart[:, p, :], ALU.subtract))

                def ones(u, j):
                    wait(dve, "gates_done", u, PG, j - 1)
                    for i in range(UG):
                        tok = bass.ds(u * (PG * UG) + (j * UG + i), 1)
                        V.tensor_scalar(one1[:, j % 2, i, :], iota128[:], chosenT[:, 0, tok], None, ALU.is_equal)
                        for p in range(3):
                            last = V.tensor_scalar(one2[:, j % 2, i, p, :], iota128[:], chosenT[:, 1, tok], gpart[:, p, tok],
                                                   ALU.is_equal, ALU.mult)
                    last.then_inc(S("ones_ready"), 1)

                def use(u, j):
                    wait(dve, "gates_done", u, PG, j + 1)
                    at = act_all[:, :, bass.ds(u * (PG * UG) + j * UG, UG)]
                    V.tensor_tensor(at, at, gps[:, j].rearrange("p i e -> p e i"), ALU.mult).then_inc(S("gates_used"), 1)

                def body(u):
                    for j in range(PG):
                        if not (isinstance(u, int) and u == NG - 1 and j == PG - 1):
                            ones(u, j + 1) if j < PG - 1 else ones(u + 1, 0)
                        use(u, j)

                ones(0, 0)
                steps(dve, NG, body)

        upx = ExitStack()
        with upx:
            wu = sc[:].rearrange("p t h b n -> p (t h b n)").rearrange("p (s d) -> p s d", s=4)
            wuh = sb(upx, "wuh", [128, 2, D], f32r)
            wul = sb(upx, "wul", [128, 2, D], f32r)
            ah = sb(upx, "ah", [128, 2, T], f32r)
            al = sb(upx, "al", [128, 2, T], f32r)
            acc = ps(upx, "acc", [128, TT, D])
            blk = upx.enter_context(nc.Block())
            POOL_UP = 640
            NC = NK // UC
            act_flat = act_all[:].rearrange("p e t -> p (e t)")

            @blk.sync
            def _(sp):
                def body(u):
                    for j in range(UC):
                        wait(sp, "up_hi", u, UC, j - 3)
                        wait(sp, "up_lo_pool", u, UC, j - 3)
                        wait(sp, "up_lo_dve", u, UC, j - 3)
                        sp.dma_start(wu[:, j % 4, :], w_up[:, bass.ds((u * UC + j) * D, D)]).then_inc(S("wu_loaded%d" % (j % 4)), 16)
                steps(sp, NC, body)
                dst = out.rearrange("o (t p) d -> p (o t) d", p=128)
                for t in range(TT):
                    sp.wait_ge(S("x_final"), t + 1)
                    sp.dma_start(dst[:, t, :], x[:, t, :]).then_inc(S("out_stored"), 16)
                sp.wait_ge(S("out_stored"), 16 * TT)

            @blk.scalar
            def _(act):
                def body(u):
                    for j in range(UC):
                        wait(act, "wu_loaded%d" % (j % 4), u, 16 * UC // 4, 16 * (j // 4 + 1))
                        wait(act, "up_done", u, UC, j - 1)
                        nc.scalar.activation(wuh[:, j % 2, :], wu[:, j % 4, :], ACT.Copy)
                        nc.scalar.activation(ah[:, j % 2, :], act_flat[:, bass.ds((u * UC + j) * T, T)], ACT.Copy).then_inc(S("up_hi"), 1)
                steps(act, NC, body)

            @blk.gpsimd
            def _(pool):
                def body(u):
                    for j in range(UC):
                        wait(pool, "up_hi", u, UC, j + 1)
                        wait(pool, "wu_loaded%d" % (j % 4), u, 16 * UC // 4, 16 * (j // 4 + 1))
                        wait(pool, "up_done", u, UC, j - 1)
                        nc.gpsimd.tensor_tensor(wul[:, j % 2, 0:POOL_UP], wu[:, j % 4, 0:POOL_UP], wuh[:, j % 2, 0:POOL_UP].bitcast(f32),
                                                ALU.subtract).then_inc(S("up_lo_pool"), 1)
                steps(pool, NC, body)

            @blk.vector
            def _(dve):
                def body(u):
                    for j in range(UC):
                        wait(dve, "up_hi", u, UC, j + 1)
                        wait(dve, "wu_loaded%d" % (j % 4), u, 16 * UC // 4, 16 * (j // 4 + 1))
                        wait(dve, "up_done", u, UC, j - 1)
                        V.tensor_tensor(wul[:, j % 2, POOL_UP:], wu[:, j % 4, POOL_UP:], wuh[:, j % 2, POOL_UP:].bitcast(f32), ALU.subtract)
                        V.tensor_tensor(al[:, j % 2, :], act_flat[:, bass.ds((u * UC + j) * T, T)], ah[:, j % 2, :].bitcast(f32),
                                        ALU.subtract).then_inc(S("up_lo_dve"), 1)
                steps(dve, NC, body)
                for t in range(TT):
                    dve.wait_ge(S("up_done"), NK)
                    V.tensor_tensor(x[:, t, :], x[:, t, :], acc[:, t, :], ALU.add).then_inc(S("x_final"), 1)

            @blk.tensor
            def _(pe):
                def body(u):
                    for j in range(UC):
                        wait(pe, "up_lo_pool", u, UC, j + 1)
                        wait(pe, "up_lo_dve", u, UC, j + 1)
                        for t in range(TT):
                            for half in range(2):
                                cols, toks = slice(512 * half, 512 * half + 512), slice(128 * t, 128 * t + 128)
                                last = three(acc[:, t, cols], ah[:, j % 2, toks], al[:, j % 2, toks], wuh[:, j % 2, cols], wul[:, j % 2, cols],
                                             start=isinstance(u, int) and u == 0 and j == 0,
                                             stop=isinstance(u, int) and u == NC - 1 and j == UC - 1)
                        last.then_inc(S("up_done"), 1)
                steps(pe, NC, body)


_INS = ["x", "mix_norm_w", "w_in", "q_norm_w", "k_norm_w", "conv_w", "conv_b", "igate_b", "fgate_b", "mlstm_norm_w",
        "w_attn_branch", "w_mlstm_branch", "merge_b", "w_out", "ffn_norm_w", "peer_w_query", "peer_keys_1",
        "peer_keys_2", "peer_w_down", "peer_w_up"]


def kernel(**inputs):
    import numpy as np
    import concourse.bacc as bacc
    from concourse.bass_utils import run_bass_kernel_spmd

    freq = np.float32(500000.0) ** (-np.arange(0, ROT, 2, dtype=np.float32) / np.float32(ROT))
    angle = np.arange(T, dtype=np.float32)[:, None] * freq[None, :]
    arrays = {"rope": np.concatenate([np.cos(angle), np.sin(angle)], axis=1).astype(np.float32)}
    for name in _INS:
        arrays[name] = np.ascontiguousarray(inputs[name])
    nc = bacc.Bacc("TRN2", target_bir_lowering=False, num_devices=1)
    aps = {n: nc.dram_tensor("in_" + n, v.shape, mybir.dt.from_np(v.dtype), kind="ExternalInput").ap() for n, v in arrays.items()}
    out = nc.dram_tensor("out", (1, T, D), mybir.dt.float32, kind="ExternalOutput").ap()
    build(nc, aps, out)
    r = run_bass_kernel_spmd(nc, [{"in_" + n: v for n, v in arrays.items()}], core_ids=[0])
    return r.results[0]["out"]
```

```python
from contextlib import ExitStack

import concourse.bass as bass
from concourse import mybir

T, D = 256, 1024
TT, KD = T // 128, D // 128
AH, AD = 8, 64
MH, MD = 4, 128
ROT = AD // 4
CONV = 4
PH, NK, TOPK = 8, 128, 16
EPS = 1e-6
BIG = 1e30
LOWEST = -3.4028234663852886e38

COL = {}
_at = 0
for _n, _w in (("aq", 512), ("ak", 512), ("av", 512), ("mq", 512), ("mk", 512), ("mv", 512),
               ("mo", 512), ("mi", MH), ("mf", MH), ("ga", D), ("gm", D)):
    COL[_n] = _at
    _at += _w

CW = 256
CE = KD * CW
CHUNKS = [(_n, _j) for _n, _k in (("mq", 2), ("mk", 2), ("aq", 2), ("ak", 2), ("av", 2), ("mv", 2),
                                  ("mo", 2), ("ga", 4), ("gm", 4), ("wab", 2), ("wmb", 2),
                                  ("wo", 4), ("wq", 8)) for _j in range(_k)]
INDEX = {_c: _i for _i, _c in enumerate(CHUNKS)}
BRANCH = ("wab", "wmb")
GROUPS = [(_c, _h) for _c in CHUNKS for _h in range(2 if _c[0] in BRANCH else 1)]
BY_DVE = ("wab", "wmb", "wo")
POOL_LO = 704

VEC = {}
_at = 0
for _n, _w in (("mixw", 8), ("cw", 32), ("cb", 8), ("mnw", 4), ("mb", 16), ("ffw", 8)):
    VEC[_n] = _at
    _at += _w
NVEC = _at

MISC = {}
for _n, _k in (("vec", 1), ("xT", 4), ("gates", 1), ("qkT", 4), ("S", 6), ("gcol", 1), ("negM", 2),
               ("ST", 3), ("PT", 6), ("PV", 2), ("num", 4), ("hmT", 2), ("key", 4), ("h2T", 4),
               ("sc", 8)):
    for _j in range(_k):
        MISC[_n, _j] = len(MISC)

XSS, QKSS, MSS, X2SS = 0, 2, 34, 42

UA = 8
NA = NK // UA
UG = 4
EH = NK // 2
UC = 8


def groups_before(group, dve):
    return sum((c[0] in BY_DVE) == dve for c, _ in GROUPS[:group + 1])


def groups_through(n):
    return sum(len([g for g in GROUPS if g[0] == c]) for c in CHUNKS[:n + 1])


def build(nc, a, out):
    f32, f32r, bf16, u32 = mybir.dt.float32, mybir.dt.float32r, mybir.dt.bfloat16, mybir.dt.uint32
    ALU, ACT, AXX = mybir.AluOpType, mybir.ActivationFunctionType, mybir.AxisListType.X
    keep = ExitStack()
    sems = {}

    def S(name):
        if name not in sems:
            sems[name] = keep.enter_context(nc.semaphore(name))
        return sems[name]

    def sb(stack, name, shape, dt=f32):
        return stack.enter_context(nc.sbuf_tensor(name, shape, dt))

    def ps(stack, name, shape, dt=f32):
        return stack.enter_context(nc.psum_tensor(name, shape, dt))

    class Link:

        def __init__(self, eng, name):
            self.eng, self.sem, self.n = eng, S(name), 0

        def mark(self, ins):
            self.n += 1
            ins.then_inc(self.sem, 1)

        def settle(self):
            self.eng.wait_ge(self.sem, self.n)

        def __call__(self, ins):
            self.mark(ins)
            self.settle()

    def three(out_, lh, ll, rh, rl, start, stop):
        nc.tensor.matmul(out_, lh, rh, start=start, stop=False)
        nc.tensor.matmul(out_, lh, rl, start=False, stop=False)
        return nc.tensor.matmul(out_, ll, rh, start=False, stop=stop)

    with keep:
        x = sb(keep, "x", [128, TT, D])
        hT = sb(keep, "hT", [128, KD, 2, T], f32r)
        hTh, hTl = hT[:, :, 0, :], hT[:, :, 1, :]
        ident = sb(keep, "ident", [128, 128])
        sc = sb(keep, "sc", [128, TT, PH, 2, NK])

        front = ExitStack()
        with front:
            raw = sb(front, "raw", [128, 3, CE])
            whi = sb(front, "whi", [128, 2, CE], f32r)
            wlo = sb(front, "wlo", [128, 2, CE], f32r)
            vcol = sb(front, "vcol", [128, NVEC])
            minus_half = sb(front, "minus_half", [128, 32])
            stat = sb(front, "stat", [128, 64])
            work = sb(front, "work", [128, 2048])
            hq = sb(front, "hq", [128, KD, T])
            qk = sb(front, "qk", [128, TT, 2 * AH * AD])
            probT = sb(front, "probT", [128, 3072])
            cv = sb(front, "cv", [128, 2 * MH, T])
            upv = sb(front, "upv", [128, 2072])
            v = sb(front, "v", [128, TT, AH * AD])
            gsig = sb(front, "gsig", [128, 16, T])
            aTh = sb(front, "aTh", [128, 4, T], f32r)
            aTl = sb(front, "aTl", [128, 4, T], f32r)
            mTh = sb(front, "mTh", [128, 4, T], f32r)
            mTl = sb(front, "mTl", [128, 4, T], f32r)
            tri_q = sb(front, "tri_q", [128, 128])
            tri_s = sb(front, "tri_s", [128, 256])
            sel = sb(front, "sel", [MH, MH, 128])
            vrow = sb(front, "vrow", [NVEC, 128])
            qkw = sb(front, "qkw", [128, 2, AD])
            rot = sb(front, "rot", [128, TT, ROT])
            gbias = sb(front, "gbias", [MH, 2])
            wgate = sb(front, "wgate", [128, KD, 2 * MH])
            grow = sb(front, "grow", [MH, 6, T])
            gcol = sb(front, "gcol", [128, TT, 2, MH])
            den = sb(front, "den", [128, TT, MH])
            arow = sb(front, "arow", [128, 3, TT, AH])
            ones4 = sb(front, "ones4", [MH, T])
            proj = ps(front, "proj", [128, 4, 512])
            misc = ps(front, "misc", [128, 4, 512])

            up = upv[:].rearrange("p (c t) -> p c t", c=8)
            v1 = upv[:, 0:TT * MH * (MD + 1)].rearrange("p (t h c) -> p t h c", t=TT, h=MH)
            mosig = upv[:, 1032:1032 + 1024].rearrange("p (t c) -> p t c", t=TT)
            scf = sc[:].rearrange("p a b c d -> p (a b c d)")
            sig = scf[:, 0:2048].rearrange("p (c t) -> p c t", c=8)
            hwork = work[:].rearrange("p (t c) -> p t c", t=TT)
            dT0 = work[:, 0:1024].rearrange("p (h t) -> p h t", h=MH)
            dT1 = work[:, 1024:1536].rearrange("p (h t) -> p h t", h=MH)
            keyn = work[:].rearrange("p (b h d) -> p b h d", b=2, h=PH)
            p0 = scf[:, 0:1024].rearrange("p (h k) -> p h k", h=AH)
            p1 = scf[:, 1024:3072].rearrange("p (h k) -> p h k", h=AH)
            pT0 = probT[:, 0:2048].rearrange("p (h q) -> p h q", h=AH)
            pT1 = probT[:, 2048:3072].rearrange("p (h q) -> p h q", h=AH)
            keyT = probT[:, 0:2048].rearrange("p (b h n) -> p b h n", b=2, h=PH)
            aT = cv[:, 0:4, :]
            mT = cv[:, 4:8, :]
            hm = qk[:, :, 0:512]
            hsq = qk[:, :, 512:1024]
            rI, rLF, rTMP, rF, rG, rNM = range(6)

            def bank(name, i=0):
                return misc[:, MISC[name, i] % 4, :]

            def chunk_source(c):
                name, j = c
                if name in BRANCH:
                    src = a["w_attn_branch" if name == "wab" else "w_mlstm_branch"]
                    return src[:, j * 512:(j + 1) * 512].rearrange("(k p) n -> p k n", p=128)
                if name == "wo":
                    src, at = a["w_out"], j * CW
                elif name == "wq":
                    src, at = a["peer_w_query"], j * CW
                else:
                    src, at = a["w_in"], COL[name] + j * CW
                return src[:, at:at + CW].rearrange("(k p) n -> p k n", p=128)

            def as_chunk(flat, c):
                return flat.rearrange("p (k n) -> p k n", k=4 if c[0] in BRANCH else KD)

            blk = front.enter_context(nc.Block())

            @blk.sync
            def _(sp):
                for t in range(TT):
                    sp.dma_start(x[:, t, :], a["x"][0, t * 128:(t + 1) * 128, :]).then_inc(S("x_loaded%d" % t), 16)
                for n, c in enumerate(CHUNKS):
                    if n >= 3:
                        sp.wait_ge(S("hi_ready"), n - 2)
                        sp.wait_ge(S("lo_dve_ready"), n - 2)
                        sp.wait_ge(S("lo_pool_ready"), n - 2)
                    sp.dma_start(as_chunk(raw[:, n % 3, :], c), chunk_source(c)).then_inc(S("raw_loaded%d" % (n % 3)), 16)
                    if n == 0:
                        for name, src in (("mixw", a["mix_norm_w"]), ("cb", a["conv_b"]),
                                          ("mnw", a["mlstm_norm_w"]), ("ffw", a["ffn_norm_w"])):
                            rows = src.rearrange("(r c) -> r c", c=128)
                            sp.dma_start(vrow[VEC[name]:VEC[name] + rows.shape[0], :], rows).then_inc(S("vec_loaded"), 16)
                        for j in range(CONV):
                            sp.dma_start(vrow[VEC["cw"] + 8 * j:VEC["cw"] + 8 * j + 8, :],
                                         a["conv_w"][j, :].rearrange("(r c) -> r c", c=128)).then_inc(S("vec_loaded"), 16)
                        for j in range(2):
                            sp.dma_start(vrow[VEC["mb"] + 8 * j:VEC["mb"] + 8 * j + 8, :],
                                         a["merge_b"][j, :].rearrange("(r c) -> r c", c=128)).then_inc(S("vec_loaded"), 16)
                        sp.dma_start(qkw[:, 0, :], a["q_norm_w"].partition_broadcast(128)).then_inc(S("small_loaded"), 16)
                        sp.dma_start(qkw[:, 1, :], a["k_norm_w"].partition_broadcast(128)).then_inc(S("small_loaded"), 16)
                        sp.dma_start(rot[:], a["rope"].rearrange("(t p) r -> p t r", p=128)).then_inc(S("small_loaded"), 16)
                        sp.dma_start(gbias[:, 0:1], a["igate_b"].rearrange("(n o) -> n o", o=1)).then_inc(S("small_loaded"), 16)
                        sp.dma_start(gbias[:, 1:2], a["fgate_b"].rearrange("(n o) -> n o", o=1)).then_inc(S("small_loaded"), 16)
                        sp.dma_start(wgate[:], a["w_in"][:, COL["mi"]:COL["mi"] + 2 * MH].rearrange(
                            "(k p) n -> p k n", p=128)).then_inc(S("small_loaded"), 16)
                    if c == ("gm", 3):
                        sp.wait_ge(S("num_done"), 1)
                        sp.dma_start(keyn[:, 0], a["peer_keys_1"].rearrange("h n d -> n h d")).then_inc(S("key_loaded"), 16)
                        sp.dma_start(keyn[:, 1], a["peer_keys_2"].rearrange("h n d -> n h d")).then_inc(S("key_loaded"), 16)

            @blk.gpsimd
            def _(pool):
                link = Link(pool, "pool_link")
                g = nc.gpsimd
                link(g.memset(ident[:], 0.0))
                g.affine_select(out=ident[:], in_=ident[:], compare_op=ALU.not_equal, fill=1.0, base=0,
                                pattern=[[-1, 128]], channel_multiplier=1).then_inc(S("ident_ready"), 1)
                link.mark(g.memset(minus_half[:], -0.5))
                g.memset(up[:, :, 0:CONV - 1], 0.0).then_inc(S("pad_ready"), 1)
                g.memset(ones4[:], 1.0).then_inc(S("const_ready"), 1)
                link.mark(g.memset(tri_q[:], 0.0))
                link.mark(g.memset(tri_s[:], 0.0))
                link(g.memset(sel[:], 0.0))
                g.affine_select(out=tri_q[:], in_=tri_q[:], compare_op=ALU.is_ge, fill=-BIG, base=0,
                                pattern=[[-1, 128]], channel_multiplier=1).then_inc(S("const_ready"), 1)
                g.affine_select(out=tri_s[:], in_=tri_s[:], compare_op=ALU.is_ge, fill=-BIG, base=0,
                                pattern=[[1, 256]], channel_multiplier=-1).then_inc(S("const_ready"), 1)
                g.affine_select(out=sel[:], in_=sel[:], compare_op=ALU.not_equal, fill=1.0, base=0,
                                pattern=[[-1, MH], [0, 128]], channel_multiplier=1).then_inc(S("const_ready"), 1)

                def rsqrt(at, n, width, done):
                    link(g.tensor_scalar(stat[:, at:at + n], stat[:, at:at + n], 1.0 / width, EPS, ALU.mult, ALU.add))
                    g.tensor_tensor(stat[:, at:at + n], stat[:, at:at + n], minus_half[:, 0:n], ALU.pow).then_inc(S(done), 1)

                pool.wait_ge(S("x_squared"), 2)
                rsqrt(XSS, TT, D, "x_rstd")
                for n, c in enumerate(CHUNKS):
                    pool.wait_ge(S("raw_loaded%d" % (n % 3)), 16 * (n // 3 + 1))
                    pool.wait_ge(S("hi_ready"), n + 1)
                    if n >= 2:
                        pool.wait_ge(S("proj_done"), groups_through(n - 2))
                    g.tensor_tensor(wlo[:, n % 2, 0:POOL_LO], raw[:, n % 3, 0:POOL_LO],
                                    whi[:, n % 2, 0:POOL_LO].bitcast(f32), ALU.subtract).then_inc(S("lo_pool_ready"), 1)
                    if c in (("aq", 0), ("ak", 0)):
                        j = 0 if c[0] == "aq" else 1
                        pool.wait_ge(S("conv_sig"), j + 1)
                        g.tensor_tensor(cv[:, 4 * j:4 * j + 4, :], cv[:, 4 * j:4 * j + 4, :],
                                        sig[:, 4 * j:4 * j + 4, :], ALU.mult).then_inc(S("silu_done"), 1)
                    if c == ("av", 0):
                        pool.wait_ge(S("qk_squared"), 1)
                        rsqrt(QKSS, 32, AD, "qk_rstd")
                    if c == ("gm", 1):
                        pool.wait_ge(S("hm_squared"), 1)
                        rsqrt(MSS, 8, MD, "hm_rstd")
                    if c == ("wq", 0):
                        pool.wait_ge(S("x2_squared"), 2)
                        rsqrt(X2SS, TT, D, "x2_rstd")

            @blk.scalar
            def _(act):
                link = Link(act, "act_link")

                def hi(n):
                    act.wait_ge(S("raw_loaded%d" % (n % 3)), 16 * (n // 3 + 1))
                    if n >= 2:
                        act.wait_ge(S("proj_done"), groups_through(n - 2))
                        act.wait_ge(S("lo_dve_ready"), n - 1)
                        act.wait_ge(S("lo_pool_ready"), n - 1)
                    nc.scalar.activation(whi[:, n % 2, :], raw[:, n % 3, :], ACT.Copy).then_inc(S("hi_ready"), 1)

                def take(c):
                    name, j = c
                    g = GROUPS.index((c, 0))
                    bank2 = proj[:, g % 4, :].rearrange("p (i n) -> p i n", i=2)
                    act.wait_ge(S("proj_done"), g + 1)
                    if name in ("mq", "mk"):
                        at = (0 if name == "mq" else 4) + 2 * j
                        nc.scalar.activation(up[:, at:at + 2, CONV - 1:], bank2, ACT.Copy).then_inc(S("proj_taken_act"), 1)
                    elif name in ("aq", "ak"):
                        at = (0 if name == "aq" else 512) + CW * j
                        nc.scalar.activation(qk[:, :, at:at + CW], bank2, ACT.Copy).then_inc(S("proj_taken_act"), 1)
                    elif name == "av":
                        nc.scalar.activation(v[:, :, CW * j:CW * j + CW], bank2, ACT.Copy).then_inc(S("proj_taken_act"), 1)
                    elif name == "mv":
                        act.wait_ge(S("conv_done"), 2)
                        for t in range(TT):
                            last = nc.scalar.activation(v1[:, t, 2 * j:2 * j + 2, 0:MD],
                                                        bank2[:, t, :].rearrange("p (h c) -> p h c", h=2), ACT.Copy)
                            last.then_inc(*((S("proj_taken_act"), 1) if t else (S("v1_half"), 1)))
                    elif name == "mo":
                        nc.scalar.activation(mosig[:, :, CW * j:CW * j + CW], bank2, ACT.Sigmoid).then_inc(S("proj_taken_act"), 1)
                    elif name in ("ga", "gm"):
                        at = (0 if name == "ga" else 8) + 2 * j
                        for i in range(2):
                            b = VEC["mb"] + at + i
                            last = nc.scalar.activation(gsig[:, at + i, :], bank2[:, i, :], ACT.Sigmoid, bias=vcol[:, b:b + 1])
                            last.then_inc(*((S("proj_taken_act"), 1) if i else (S("gate_half"), 1)))
                    elif name == "wq":
                        act.wait_ge(S("y_ready"), 2)
                        nc.scalar.activation(gsig[:, 2 * j:2 * j + 2, :], bank2, ACT.Copy).then_inc(S("proj_taken_act"), 1)

                def split_hi(dst, src, bank_taken, done):
                    act.wait_ge(S("misc_free"), MISC[bank_taken] + 1)
                    nc.scalar.activation(dst, src, ACT.Copy).then_inc(S(done), 1)

                hi(0)
                for t in range(TT):
                    act.wait_ge(S("x_loaded%d" % t), 16)
                    nc.scalar.activation(hwork[:, t, :], x[:, t, :], ACT.Square,
                                         accum_out=stat[:, XSS + t:XSS + t + 1]).then_inc(S("x_squared"), 1)
                split_hi(hTh[:], hq[:], ("xT", 3), "h_hi")
                for n, c in enumerate(CHUNKS):
                    if n + 1 < len(CHUNKS):
                        hi(n + 1)
                    if c[0] not in BY_DVE:
                        take(c)
                    if c == ("mk", 1):
                        for j in range(2):
                            act.wait_ge(S("conv_done"), j + 1)
                            nc.scalar.activation(sig[:, 4 * j:4 * j + 4, :], cv[:, 4 * j:4 * j + 4, :],
                                                 ACT.Sigmoid).then_inc(S("conv_sig"), 1)
                    if c == ("aq", 0):
                        act.wait_ge(S("gates_read"), 1)
                        link(nc.scalar.activation(grow[:, rTMP, :], grow[:, rTMP, :], ACT.Exp, scale=-1.0))
                        nc.scalar.activation(grow[:, rTMP, :], grow[:, rTMP, :], ACT.Ln, bias=1.0).then_inc(S("softplus_done"), 1)
                    if c == ("mo", 1):
                        act.wait_ge(S("s_max"), 1)
                        for t, p in enumerate((p0, p1)):
                            for h in range(AH):
                                nc.scalar.activation(p[:, h, :], p[:, h, :], ACT.Exp, bias=arow[:, 1, t, h:h + 1], scale=AD ** -0.5,
                                                     accum_out=arow[:, 2, t, h:h + 1]).then_inc(S("p_exp"), 1)
                    if c == ("ga", 0):
                        act.wait_ge(S("misc_free"), MISC["negM", 1] + 1)
                        for h in range(MH):
                            nc.scalar.activation(dT0[:, h, :], dT0[:, h, :], ACT.Exp, bias=gcol[:, 0, 0, h:h + 1]).then_inc(S("decay"), 1)
                            nc.scalar.activation(dT1[:, h, :], dT1[:, h, :], ACT.Exp, bias=gcol[:, 1, 0, h:h + 1]).then_inc(S("decay"), 1)
                        nc.scalar.activation(gcol[:, :, 1, :], gcol[:, :, 1, :], ACT.Exp).then_inc(S("decay"), 1)
                    if c == ("gm", 2):
                        split_hi(aTh[:], aT, ("PV", 1), "aT_hi")
                    if c == ("wab", 1):
                        split_hi(mTh[:], mT, ("hmT", 1), "mT_hi")
                    if c == ("wmb", 1):
                        for j in range(2):
                            act.wait_ge(S("y_ready"), j + 1)
                            nc.scalar.activation(hTh[:, 4 * j:4 * j + 4, :], hq[:, 4 * j:4 * j + 4, :], ACT.Copy).then_inc(S("y_hi"), 1)
                    if c == ("wo", 3):
                        act.wait_ge(S("proj_taken_dve"), groups_before(len(GROUPS) - 1, True))
                        act.wait_ge(S("misc_free"), MISC["key", 3] + 1)
                        for t in range(TT):
                            nc.scalar.activation(hwork[:, t, :], x[:, t, :], ACT.Square,
                                                 accum_out=stat[:, X2SS + t:X2SS + t + 1]).then_inc(S("x2_squared"), 1)
                        for j in range(2):
                            split_hi(hTh[:, 4 * j:4 * j + 4, :], hq[:, 4 * j:4 * j + 4, :], ("h2T", 2 * j + 1), "h2_hi")

            @blk.vector
            def _(dve):
                link = Link(dve, "dve_link")
                V = nc.vector

                def lo(n):
                    dve.wait_ge(S("raw_loaded%d" % (n % 3)), 16 * (n // 3 + 1))
                    dve.wait_ge(S("hi_ready"), n + 1)
                    if n >= 2:
                        dve.wait_ge(S("proj_done"), groups_through(n - 2))
                    V.tensor_tensor(wlo[:, n % 2, POOL_LO:], raw[:, n % 3, POOL_LO:],
                                    whi[:, n % 2, POOL_LO:].bitcast(f32), ALU.subtract).then_inc(S("lo_dve_ready"), 1)

                def full(name, i=0):
                    dve.wait_ge(S("misc_full"), MISC[name, i] + 1)
                    return bank(name, i)

                def free(ins):
                    ins.then_inc(S("misc_free"), 1)

                def by2(ap):
                    return ap.rearrange("p (i n) -> p i n", i=2)

                free(V.tensor_copy(vcol[:], full("vec")[:, 0:NVEC]))
                dve.wait_ge(S("misc_free"), 1)
                dve.wait_ge(S("x_rstd"), 1)
                for t in range(TT):
                    dve.wait_ge(S("x_loaded%d" % t), 16)
                    V.tensor_scalar(hwork[:, t, :], x[:, t, :], stat[:, XSS + t:XSS + t + 1], None, ALU.mult).then_inc(S("h_nat"), 1)

                def weighted_transpose(name, vec):
                    for b in range(4):
                        src = by2(full(name, b))
                        for i in range(2):
                            k = 2 * b + i
                            ins = V.tensor_scalar(hq[:, k, :], src[:, i, :], vcol[:, VEC[vec] + k:VEC[vec] + k + 1], None, ALU.mult)
                        free(ins)

                weighted_transpose("xT", "mixw")
                dve.wait_ge(S("h_hi"), 1)
                V.tensor_tensor(hTl[:], hq[:], hTh[:].bitcast(f32), ALU.subtract).then_inc(S("h_lo"), 1)
                lo(0)
                for n, c in enumerate(CHUNKS):
                    if n + 1 < len(CHUNKS):
                        lo(n + 1)
                    if c in (("mk", 0), ("mk", 1)):
                        j = c[1]
                        dve.wait_ge(S("pad_ready"), 1)
                        dve.wait_ge(S("proj_taken_act"), 2 * j + 2)
                        for tap in range(CONV):
                            for i in range(4 * j, 4 * j + 4):
                                w = vcol[:, VEC["cw"] + 8 * tap + i:VEC["cw"] + 8 * tap + i + 1]
                                src = up[:, i, tap:tap + T]
                                if tap == 0:
                                    ins = V.tensor_scalar(cv[:, i, :], src, w, None, ALU.mult)
                                else:
                                    ins = V.scalar_tensor_tensor(out=cv[:, i, :], in0=src, scalar=w, in1=cv[:, i, :],
                                                                 op0=ALU.mult, op1=ALU.add)
                                link.mark(ins)
                            link.settle()
                        for i in range(4 * j, 4 * j + 4):
                            ins = V.tensor_scalar(cv[:, i, :], cv[:, i, :], vcol[:, VEC["cb"] + i:VEC["cb"] + i + 1], None, ALU.add)
                        ins.then_inc(S("conv_done"), 1)
                        if j == 1:
                            dve.wait_ge(S("small_loaded"), 96)
                            src = by2(full("gates"))
                            link.mark(V.tensor_scalar(grow[:, rI, :], src[0:MH, 0, :], gbias[:, 0:1], None, ALU.add))
                            free(V.tensor_scalar(grow[:, rLF, :], src[0:MH, 1, :], gbias[:, 1:2], None, ALU.add))
                            dve.wait_ge(S("misc_free"), MISC["gates", 0] + 1)
                            V.scalar_tensor_tensor(out=grow[:, rTMP, :], in0=grow[:, rLF, :], scalar=-1.0, in1=grow[:, rLF, :],
                                                   op0=ALU.mult, op1=ALU.max).then_inc(S("gates_read"), 1)
                    if c == ("aq", 1):
                        dve.wait_ge(S("softplus_done"), 1)
                        dve.wait_ge(S("const_ready"), 4)
                        link(V.scalar_tensor_tensor(out=grow[:, rLF, :], in0=grow[:, rLF, :], scalar=0.0, in1=grow[:, rTMP, :],
                                                    op0=ALU.min, op1=ALU.subtract))
                        link(V.tensor_tensor_scan(grow[:, rF, :], ones4[:], grow[:, rLF, :], 0.0, ALU.mult, ALU.add))
                        link(V.tensor_tensor(grow[:, rG, :], grow[:, rI, :], grow[:, rF, :], ALU.subtract))
                        link(V.tensor_tensor_scan(grow[:, rNM, :], grow[:, rG, :], grow[:, rG, :], 0.0, ALU.max, ALU.max))
                        link(V.scalar_tensor_tensor(out=grow[:, rTMP, :], in0=grow[:, rF, :], scalar=-1.0, in1=grow[:, rNM, :],
                                                    op0=ALU.mult, op1=ALU.subtract))
                        V.tensor_scalar(grow[:, rNM, :], grow[:, rNM, :], -1.0, None, ALU.mult).then_inc(S("gate_rows"), 1)
                    if c == ("ak", 1):
                        dve.wait_ge(S("proj_taken_act"), 8)
                        dve.wait_ge(S("h_hi"), 1)
                        link(V.tensor_tensor(hwork[:], qk[:], qk[:], ALU.mult))
                        V.tensor_reduce(stat[:, QKSS:QKSS + 32], hwork[:].rearrange("p t (h c) -> p (t h) c", c=AD), AXX,
                                        ALU.add).then_inc(S("qk_squared"), 1)
                    if c == ("mv", 0):
                        dve.wait_ge(S("qk_rstd"), 1)
                        qh = qk[:].rearrange("p t (h c) -> p (t h) c", c=AD)
                        link(V.tensor_tensor(qh, qh, stat[:, QKSS:QKSS + 32].unsqueeze(2).broadcast_to([128, 32, AD]), ALU.mult))
                        for t in range(TT):
                            for i in range(2):
                                q1 = qk[:, t, 512 * i:512 * i + 512].rearrange("p (h c) -> p h c", c=AD)
                                link.mark(V.tensor_tensor(q1, q1, qkw[:, i, :].unsqueeze(1).broadcast_to([128, AH, AD]), ALU.mult))
                        link.settle()
                        half = ROT // 2
                        for t in range(TT):
                            qt = qk[:, t, :].rearrange("p (h c) -> p h c", c=AD)
                            x1, x2 = qt[:, :, 0:half], qt[:, :, half:ROT]
                            cos = rot[:, t, 0:half].unsqueeze(1).broadcast_to([128, 2 * AH, half])
                            sin = rot[:, t, half:ROT].unsqueeze(1).broadcast_to([128, 2 * AH, half])
                            tmp = [hwork[:, t, 128 * i:128 * i + 128].rearrange("p (h c) -> p h c", c=half) for i in range(4)]
                            for i, (u, w) in enumerate(((x1, cos), (x2, sin), (x2, cos), (x1, sin))):
                                link.mark(V.tensor_tensor(tmp[i], u, w, ALU.mult))
                            link.settle()
                            link.mark(V.tensor_tensor(x1, tmp[0], tmp[1], ALU.subtract))
                            V.tensor_tensor(x2, tmp[2], tmp[3], ALU.add).then_inc(S("qk_ready"), 1)
                        link.settle()
                    if c == ("mv", 1):
                        dve.wait_ge(S("conv_done"), 2)
                        V.memset(v1[:, :, :, MD:MD + 1], 1.0).then_inc(S("v1_ones"), 1)
                        for b in range(4):
                            src = by2(full("qkT", b))
                            free(V.tensor_copy(hq[:, 2 * b:2 * b + 2, :], src))
                    if c == ("mo", 1):
                        dve.wait_ge(S("silu_done"), 2)
                        for b in range(2):
                            src = full("S", b).rearrange("p (h k) -> p h k", h=4)
                            free(V.tensor_tensor(p0.rearrange("p (i o) k -> p o i k", o=2)[:, b], src, tri_q[:].unsqueeze(1).broadcast_to([128, 4, 128]), ALU.add))
                        for b in range(4):
                            src = full("S", 2 + b).rearrange("p (h k) -> p h k", h=2)
                            dst = p1.rearrange("p (q i o) k -> p q o i k", i=2, o=2)[:, b // 2, b % 2]
                            link.mark(V.tensor_copy(dst[:, :, 0:128], src[:, :, 0:128]))
                            free(V.tensor_tensor(dst[:, :, 128:256], src[:, :, 128:256],
                                                 tri_q[:].unsqueeze(1).broadcast_to([128, 2, 128]), ALU.add))
                        link.settle()
                        dve.wait_ge(S("misc_free"), MISC["S", 5] + 1)
                        link.mark(V.tensor_reduce(arow[:, 0, 0, :], p0, AXX, ALU.max))
                        link.mark(V.tensor_reduce(arow[:, 0, 1, :], p1, AXX, ALU.max))
                        link.settle()
                        V.tensor_scalar(arow[:, 1], arow[:, 0], -(AD ** -0.5), None, ALU.mult).then_inc(S("s_max"), 1)
                    if c == ("ga", 0):
                        free(V.tensor_copy(gcol[:].rearrange("p t a h -> p (t a h)"), full("gcol")[:, 0:16]))
                        for b in range(2):
                            src = by2(full("negM", b))
                            V.tensor_tensor(dT0[:, 2 * b:2 * b + 2, :], src, tri_s[:].unsqueeze(1).broadcast_to([128, 2, 256]), ALU.add)
                            free(V.tensor_tensor(dT1[:, 2 * b:2 * b + 2, :], src[:, :, 128:256],
                                                 tri_s[:, 0:128].unsqueeze(1).broadcast_to([128, 2, 128]), ALU.add))
                        dve.wait_ge(S("p_exp"), 16)
                        link(V.reciprocal(arow[:, 0], arow[:, 2]))
                        for t, p in enumerate((p0, p1)):
                            V.tensor_tensor(p, p, arow[:, 0, t, :].unsqueeze(2).broadcast_to([128, AH, 128 * (t + 1)]),
                                            ALU.mult).then_inc(S("p_ready"), 1)
                    if c == ("ga", 1):
                        dve.wait_ge(S("decay"), 9)
                        for b in range(2):
                            src = by2(full("ST", b))
                            free(V.scalar_tensor_tensor(out=dT0[:, 2 * b:2 * b + 2, :], in0=src, scalar=MD ** -0.5,
                                                        in1=dT0[:, 2 * b:2 * b + 2, :], op0=ALU.mult, op1=ALU.mult))
                        src = full("ST", 2).rearrange("p (h t) -> p h t", h=MH)
                        free(V.scalar_tensor_tensor(out=dT1, in0=src, scalar=MD ** -0.5, in1=dT1, op0=ALU.mult, op1=ALU.mult))
                    if c == ("ga", 2):
                        for b in range(6):
                            src = full("PT", b).rearrange("p (h k) -> p h k", h=4)
                            if b < 2:
                                dst = pT0[:, 4 * b:4 * b + 4, 0:128]
                            elif b < 4:
                                dst = pT0[:, 4 * (b - 2):4 * (b - 2) + 4, 128:256]
                            else:
                                dst = pT1[:, 4 * (b - 4):4 * (b - 4) + 4, :]
                            free(V.tensor_copy(dst, src))
                    if c == ("gm", 0):
                        for b in range(2):
                            free(V.tensor_copy(aT[:, 2 * b:2 * b + 2, :], by2(full("PV", b))))
                        for b in range(4):
                            t, hp = b // 2, b % 2
                            src = by2(full("num", b))
                            dd = den[:, t, 2 * hp:2 * hp + 2]
                            link(V.scalar_tensor_tensor(out=dd, in0=src[:, :, MD], scalar=-1.0,
                                                        in1=gcol[:, t, 1, 2 * hp:2 * hp + 2], op0=ALU.mult, op1=ALU.max))
                            link(V.tensor_tensor(dd, src[:, :, MD], dd, ALU.max))
                            link(V.reciprocal(dd, dd))
                            free(V.tensor_tensor(hm[:, t, 256 * hp:256 * hp + 256].rearrange("p (h c) -> p h c", h=2), src[:, :, 0:MD],
                                                 dd.unsqueeze(2).broadcast_to([128, 2, MD]), ALU.mult))
                        dve.wait_ge(S("misc_free"), MISC["num", 3] + 1)
                        link(V.tensor_tensor(hsq, hm, hm, ALU.mult))
                        for t in range(TT):
                            ins = V.tensor_reduce(stat[:, MSS + 4 * t:MSS + 4 * t + 4], hsq[:, t, :].rearrange("p (h c) -> p h c", h=MH), AXX, ALU.add)
                            if t == 0:
                                link(ins)
                        ins.then_inc(S("hm_squared"), 1)
                    if c == ("gm", 2):
                        dve.wait_ge(S("aT_hi"), 1)
                        V.tensor_tensor(aTl[:], aT, aTh[:].bitcast(f32), ALU.subtract).then_inc(S("aT_lo"), 1)
                    if c == ("gm", 3):
                        dve.wait_ge(S("hm_rstd"), 1)
                        for t in range(TT):
                            hh = hm[:, t, :].rearrange("p (h c) -> p h c", h=MH)
                            link.mark(V.tensor_tensor(hh, hh, stat[:, MSS + 4 * t:MSS + 4 * t + 4].unsqueeze(2).broadcast_to([128, MH, MD]), ALU.mult))
                        link.settle()
                        V.tensor_tensor(hm, hm, mosig, ALU.mult).then_inc(S("hm_ready"), 1)
                        for b in range(2):
                            src = by2(full("hmT", b))
                            for i in range(2):
                                h = 2 * b + i
                                ins = V.tensor_scalar(mT[:, h, :], src[:, i, :], vcol[:, VEC["mnw"] + h:VEC["mnw"] + h + 1], None, ALU.mult)
                            free(ins)
                        for b in range(4):
                            free(V.tensor_copy(keyT[:, b // 2, 4 * (b % 2):4 * (b % 2) + 4, :],
                                               full("key", b).rearrange("p (h n) -> p h n", h=4)))
                    if c == ("wab", 0):
                        dve.wait_ge(S("mT_hi"), 1)
                        V.tensor_tensor(mTl[:], mT, mTh[:].bitcast(f32), ALU.subtract).then_inc(S("mT_lo"), 1)
                    if c[0] in BRANCH:
                        for half in range(2):
                            g = GROUPS.index((c, half))
                            at = 4 * c[1] + 2 * half
                            dve.wait_ge(S("proj_done"), g + 1)
                            dve.wait_ge(S("proj_taken_act"), groups_before(g, False))
                            src = by2(proj[:, g % 4, :])
                            if c[0] == "wab":
                                V.tensor_tensor(hq[:, at:at + 2, :], gsig[:, at:at + 2, :], src, ALU.mult).then_inc(S("proj_taken_dve"), 1)
                            else:
                                V.tensor_tensor(gsig[:, 8 + at:10 + at, :], gsig[:, 8 + at:10 + at, :], src, ALU.mult).then_inc(S("proj_taken_dve"), 1)
                                dve.wait_ge(S("proj_taken_dve"), groups_before(g, True))
                                ins = V.tensor_tensor(hq[:, at:at + 2, :], hq[:, at:at + 2, :], gsig[:, 8 + at:10 + at, :], ALU.add)
                                if half == 0:
                                    link(ins)
                                else:
                                    ins.then_inc(S("y_ready"), 1)
                    if c == ("wmb", 1):
                        for j in range(2):
                            dve.wait_ge(S("y_hi"), j + 1)
                            V.tensor_tensor(hTl[:, 4 * j:4 * j + 4, :], hq[:, 4 * j:4 * j + 4, :], hTh[:, 4 * j:4 * j + 4, :].bitcast(f32),
                                            ALU.subtract).then_inc(S("y_lo"), 1)
                    if c[0] == "wo":
                        g = GROUPS.index((c, 0))
                        dve.wait_ge(S("proj_done"), g + 1)
                        xx = x[:, :, CW * c[1]:CW * c[1] + CW]
                        V.tensor_tensor(xx, xx, by2(proj[:, g % 4, :]), ALU.add).then_inc(S("proj_taken_dve"), 1)
                        if c[1] == 3:
                            dve.wait_ge(S("proj_taken_dve"), groups_before(g, True))
                            dve.wait_ge(S("x2_rstd"), 1)
                            for t in range(TT):
                                V.tensor_scalar(hwork[:, t, :], x[:, t, :], stat[:, X2SS + t:X2SS + t + 1], None, ALU.mult).then_inc(S("h_nat"), 1)
                            weighted_transpose("h2T", "ffw")
                            for j in range(2):
                                dve.wait_ge(S("h2_hi"), j + 1)
                                V.tensor_tensor(hTl[:, 4 * j:4 * j + 4, :], hq[:, 4 * j:4 * j + 4, :], hTh[:, 4 * j:4 * j + 4, :].bitcast(f32),
                                                ALU.subtract).then_inc(S("h2_lo"), 1)
                for b in range(8):
                    free(V.tensor_copy(sc[:, b // 4, 4 * (b % 2):4 * (b % 2) + 4, (b // 2) % 2, :],
                                       full("sc", b).rearrange("p (h n) -> p h n", h=4)))

            @blk.tensor
            def _(pe):
                mm = nc.tensor.matmul

                def use(name, i=0):
                    if MISC[name, i] >= 4:
                        pe.wait_ge(S("misc_free"), MISC[name, i] - 3)
                    return bank(name, i)

                def filled(ins):
                    ins.then_inc(S("misc_full"), 1)

                def transposes(name, src, n, ready=None):
                    for b in range(n):
                        dst = use(name, b)
                        for i in range(4):
                            last = nc.tensor.transpose(dst[:, 128 * i:128 * i + 128], src(2 * b + i // 2, i % 2), ident[:])
                        filled(last)

                pe.wait_ge(S("ident_ready"), 1)
                pe.wait_ge(S("vec_loaded"), 16 * 10)
                filled(nc.tensor.transpose(use("vec")[:, 0:NVEC], vrow[:], ident[0:NVEC, 0:NVEC]))
                pe.wait_ge(S("h_nat"), 2)
                transposes("xT", lambda k, t: hwork[:, t, 128 * k:128 * k + 128], 4)
                pe.wait_ge(S("h_lo"), 1)
                for n, c in enumerate(CHUNKS):
                    name, j = c
                    if c == ("wab", 0):
                        pe.wait_ge(S("aT_lo"), 1)
                    if c == ("wmb", 0):
                        pe.wait_ge(S("mT_lo"), 1)
                    if c == ("wo", 0):
                        pe.wait_ge(S("y_lo"), 2)
                    if c == ("wq", 0):
                        pe.wait_ge(S("h_nat"), 4)
                        transposes("h2T", lambda k, t: hwork[:, t, 128 * k:128 * k + 128], 4)
                        pe.wait_ge(S("h2_lo"), 2)
                    pe.wait_ge(S("hi_ready"), n + 1)
                    pe.wait_ge(S("lo_dve_ready"), n + 1)
                    pe.wait_ge(S("lo_pool_ready"), n + 1)
                    wh, wl = as_chunk(whi[:, n % 2, :], c), as_chunk(wlo[:, n % 2, :], c)
                    parts = [g for g in GROUPS if g[0] == c]
                    for gr in parts:
                        g = GROUPS.index(gr)
                        if g >= 4:
                            old = g - 4
                            by_dve = GROUPS[old][0][0] in BY_DVE
                            pe.wait_ge(S("proj_taken_dve" if by_dve else "proj_taken_act"), groups_before(old, by_dve))
                        for i in range(2):
                            dst = proj[:, g % 4, 256 * i:256 * i + 256]
                            for k in range(4 if name in BRANCH else KD):
                                f = dict(start=k == 0, stop=k == (3 if name in BRANCH else KD - 1))
                                if name in BRANCH:
                                    th, tl = (aTh, aTl) if name == "wab" else (mTh, mTl)
                                    at = 256 * gr[1] + 128 * i
                                    last = three(dst, wh[:, k, at:at + 128], wl[:, k, at:at + 128], th[:, k, :], tl[:, k, :], **f)
                                elif name in ("aq", "ak", "av", "mv", "mo", "wo"):
                                    tk = slice(128 * i, 128 * i + 128)
                                    last = three(dst, hTh[:, k, tk], hTl[:, k, tk], wh[:, k, :], wl[:, k, :], **f)
                                else:
                                    at = 128 * i
                                    last = three(dst, wh[:, k, at:at + 128], wl[:, k, at:at + 128], hTh[:, k, :], hTl[:, k, :], **f)
                        last.then_inc(S("proj_done"), 1)
                    if c == ("mk", 1):
                        pe.wait_ge(S("small_loaded"), 96)
                        dst = use("gates")
                        for i in range(2):
                            for k in range(KD):
                                last = mm(dst[0:MH, 256 * i:256 * i + 256], wgate[:, k, MH * i:MH * i + MH], hq[:, k, :],
                                          start=k == 0, stop=k == KD - 1)
                        filled(last)
                    if c == ("mv", 1):
                        pe.wait_ge(S("qk_ready"), 2)
                        transposes("qkT", lambda k, t: qk[:, t, 128 * k:128 * k + 128], 4)
                    if c == ("mo", 1):
                        pe.wait_ge(S("misc_free"), MISC["qkT", 3] + 1)
                        for t in range(TT):
                            per, w = (4, 128) if t == 0 else (2, 256)
                            for b in range(AH // per):
                                dst = use("S", b + 2 * t)
                                rows = slice(64 * (b % 2), 64 * (b % 2) + 64)
                                for i in range(per):
                                    pr = per * (b // 2) + i
                                    last = mm(dst[:, i * w:i * w + w], hq[rows, pr, 128 * t:128 * t + 128], hq[rows, 4 + pr, 0:w],
                                              start=True, stop=True)
                                filled(last)
                        pe.wait_ge(S("gate_rows"), 1)
                        dst = use("gcol")
                        for t in range(TT):
                            for i, r in enumerate((rG, rTMP)):
                                at = 8 * t + 4 * i
                                last = mm(dst[:, at:at + MH], grow[:, r, 128 * t:128 * t + 128], ident[0:MH, 0:MH], start=True, stop=True)
                        filled(last)
                        for h in range(MH):
                            if h % 2 == 0:
                                dst = use("negM", h // 2)
                            last = mm(dst[:, 256 * (h % 2):256 * (h % 2) + 256], sel[:, h, :], grow[:, rNM, :], start=True, stop=True)
                            if h % 2:
                                filled(last)
                    if c == ("ga", 0):
                        pe.wait_ge(S("silu_done"), 2)
                        for h in range(MH):
                            if h % 2 == 0:
                                dst = use("ST", h // 2)
                            last = mm(dst[:, 256 * (h % 2):256 * (h % 2) + 256], cv[:, MH + h, 0:128], cv[:, h, :], start=True, stop=True)
                            if h % 2:
                                filled(last)
                        dst = use("ST", 2)
                        for h in range(MH):
                            last = mm(dst[:, 128 * h:128 * h + 128], cv[:, MH + h, 128:256], cv[:, h, 128:256], start=True, stop=True)
                        filled(last)
                    if c == ("ga", 1):
                        pe.wait_ge(S("p_ready"), 2)
                        for b in range(6):
                            dst = use("PT", b)
                            for i in range(4):
                                h = 4 * (b % 2) + i
                                src = p0[:, h, :] if b < 2 else p1[:, h, 128 * (b // 4):128 * (b // 4) + 128]
                                last = nc.tensor.transpose(dst[:, 128 * i:128 * i + 128], src, ident[:])
                            filled(last)
                    if c == ("ga", 3):
                        pe.wait_ge(S("misc_free"), MISC["PT", 5] + 1)
                        pe.wait_ge(S("proj_taken_act"), 10)
                        for h in range(AH):
                            if h % 4 == 0:
                                dst = use("PV", h // 4)
                            rows = slice(64 * (h % 2), 64 * (h % 2) + 64)
                            at = 256 * ((h // 2) % 2)
                            mm(dst[rows, at:at + 256], v[:, 0, AD * h:AD * h + AD], pT0[:, h, :], start=True, stop=False)
                            last = mm(dst[rows, at + 128:at + 256], v[:, 1, AD * h:AD * h + AD], pT1[:, h, :], start=False, stop=True)
                            if h % 4 == 3:
                                filled(last)
                        pe.wait_ge(S("v1_ones"), 1)
                        pe.wait_ge(S("v1_half"), 2)
                        pe.wait_ge(S("proj_taken_act"), 12)
                        for b in range(4):
                            t, hp = b // 2, b % 2
                            dst = use("num", b)
                            for i in range(2):
                                h = 2 * hp + i
                                o = dst[:, 256 * i:256 * i + MD + 1]
                                last = mm(o, dT0[:, h, 128 * t:128 * t + 128], v1[:, 0, h, :], start=True, stop=t == 0)
                                if t == 1:
                                    last = mm(o, dT1[:, h, :], v1[:, 1, h, :], start=False, stop=True)
                            filled(last)
                        pe.wait_ge(S("misc_full"), MISC["num", 3] + 1)
                        pe.sem_inc(S("num_done"), 1)
                    if c == ("gm", 3):
                        pe.wait_ge(S("hm_ready"), 1)
                        transposes("hmT", lambda k, t: hm[:, t, 128 * k:128 * k + 128], 2)
                        pe.wait_ge(S("key_loaded"), 32)
                        for b in range(4):
                            dst = use("key", b)
                            for i in range(4):
                                last = nc.tensor.transpose(dst[:, 128 * i:128 * i + 128], keyn[:, b // 2, 4 * (b % 2) + i, :], ident[:])
                            filled(last)
                pe.wait_ge(S("proj_taken_act"), groups_before(len(GROUPS) - 1, False))
                pe.wait_ge(S("misc_free"), MISC["key", 3] + 1)
                for b in range(8):
                    t, half, hh = b // 4, (b // 2) % 2, b % 2
                    dst = use("sc", b)
                    for i in range(4):
                        h = 4 * hh + i
                        last = mm(dst[:, 128 * i:128 * i + 128], gsig[:, 2 * h + half, 128 * t:128 * t + 128], keyT[:, half, h, :],
                                  start=True, stop=True)
                    filled(last)
        build_peer(nc, a, out, keep, S, Link, three, sb, ps, x, hT, ident, sc)


def build_peer(nc, a, out, keep, S, Link, three, sb, ps, x, hT, ident, sc):
    f32, f32r, bf16, u32 = mybir.dt.float32, mybir.dt.float32r, mybir.dt.bfloat16, mybir.dt.uint32
    ALU, ACT, AXX = mybir.AluOpType, mybir.ActivationFunctionType, mybir.AxisListType.X
    w_down = a["peer_w_down"].rearrange("(p e) d -> p (e d)", e=NK)
    w_up = a["peer_w_up"].rearrange("(p e) d -> p (e d)", e=NK)
    V = nc.vector
    UNITS = TT * PH
    SA = NA // 2
    SC = NK // UC // 2
    UPS = UNITS // SA
    POOL_ONES = 3
    NG = T // UG

    def wait(eng, name, u, per, at):
        if not (isinstance(u, int) and u * per + at <= 0):
            eng.wait_ge(S(name), u * per + at)

    def halves(eng, n, body, between=None):
        body(0, False)
        with eng.Fori(1, n // 2 - 1) as u:
            body(u, False)
        body(n // 2 - 1, False)
        if between:
            between()
        body(n // 2, True)
        with eng.Fori(n // 2 + 1, n - 1) as u:
            body(u, True)
        body(n - 1, True)

    def at_step(u, n):
        return isinstance(u, int) and u == n

    peer = ExitStack()
    with peer:
        act_all = sb(peer, "act_all", [128, NK, T])
        act_flat = act_all[:].rearrange("p e t -> p (e t)")
        iota16 = sb(peer, "iota16", [128, TOPK])
        iota128 = sb(peer, "iota128", [128, NK], bf16)
        found = sb(peer, "found", [128, UG, EH], bf16)
        column = sb(peer, "column", [128, 2, UG])
        gps = ps(peer, "gps", [128, 2, 512])
        scf = sc[:].rearrange("p t h b n -> p (t h b n)")
        chosenT = scf[:, 0:3 * T].rearrange("p (i t) -> p i t", i=3)
        gpart = scf[:, 3 * T:6 * T].rearrange("p (i t) -> p i t", i=3)
        at1, at2, at3 = 6 * T, 6 * T + UG * NK, 6 * T + UG * NK + UG * 3 * EH
        one1 = scf[:, at1:at2].bitcast(bf16).rearrange("p (s i e) -> p s i e", s=2, i=UG)
        one2 = scf[:, at2:at3].bitcast(bf16).rearrange("p (s i q e) -> p s i q e", s=2, i=UG, q=3)
        gbf = scf[:, at3:at3 + T // 2].bitcast(bf16)

        def group_count(second):
            return NG if second else -EH

        def make_one1(pool, u, j, second):
            wait(pool, "gates_done", u, UA, j - 1 + group_count(second))
            tok = bass.ds(u * (UA * UG) + (j * UG - (0 if second else EH * UG)), UG)
            nc.gpsimd.tensor_copy(column[:, j % 2, :], chosenT[:, 0, tok]).then_inc(S("column_ready"), 1)
            wait(pool, "column_ready", u, UA, j + 1 + group_count(second))
            pool.sem_inc(S("column_go"), 1)
            for i in range(POOL_ONES):
                last = nc.gpsimd.tensor_scalar(one1[:, j % 2, i, :], iota128[:], column[:, j % 2, i:i + 1], None, ALU.is_equal)
            last.then_inc(S("one1_ready"), 1)

        def make_one2(dve, u, j, second):
            wait(dve, "gates_done", u, UA, j - 1 + group_count(second))
            wait(dve, "one2_ready", u, UA, j + group_count(second))
            first = j * UG - (0 if second else EH * UG)
            toks = bass.ds(u * (UA * UG) + first, UG)
            V.tensor_tensor(found[:], iota128[:, EH * second:EH * second + EH].unsqueeze(1).broadcast_to([128, UG, EH]),
                            chosenT[:, 1, toks].unsqueeze(2).broadcast_to([128, UG, EH]), ALU.is_equal).then_inc(S("e2_found"), 1)
            for i in range(POOL_ONES, UG):
                V.tensor_scalar(one1[:, j % 2, i, :], iota128[:], chosenT[:, 0, bass.ds(u * (UA * UG) + (first + i), 1)], None, ALU.is_equal)
            wait(dve, "e2_found", u, UA, j + 1 + group_count(second))
            V.tensor_tensor(one2[:, j % 2], found[:].unsqueeze(2).broadcast_to([128, UG, 3, EH]),
                            gpart[:, :, toks].rearrange("p q i -> p i q").unsqueeze(3).broadcast_to([128, UG, 3, EH]),
                            ALU.mult).then_inc(S("one2_ready"), 1)

        def make_gates(pe, u, j, second):
            wait(pe, "one1_ready", u, UA, j + 1 + group_count(second))
            wait(pe, "one2_ready", u, UA, j + 1 + group_count(second))
            wait(pe, "gates_used", u, UA, j - 1 + group_count(second))
            for i in range(UG):
                for p in range(3):
                    last = nc.tensor.matmul(gps[:, j % 2, EH * i:EH * i + EH], one1[:, j % 2, i, :], one2[:, j % 2, i, p, :],
                                            start=p == 0, stop=p == 2)
            last.then_inc(S("gates_done"), 1)

        def use_gates(dve, u, j, second):
            wait(dve, "gates_done", u, UA, j + 1 + group_count(second))
            tok = bass.ds(u * (UA * UG) + (j * UG - (0 if second else EH * UG)), UG)
            at = act_all[:, EH * second:EH * second + EH, tok]
            V.tensor_tensor(at, at, gps[:, j % 2, 0:UG * EH].rearrange("p (i e) -> p e i", i=UG), ALU.mult).then_inc(S("gates_used"), 1)

        down = ExitStack()
        with down:
            wd = sb(down, "wd", [128, 2, D])
            wTh = sb(down, "wTh", [128, 2, KD, 128], f32r)
            wTl = sb(down, "wTl", [128, 2, KD, 128], f32r)
            ucopy = sb(down, "ucopy", [128, 2, 2 * T])
            hit = sb(down, "hit", [128, UPS, 2 * TOPK, TOPK])
            hitf = hit[:].rearrange("p u n r -> p (u n r)")
            score = hitf[:, 0:UPS * 2 * NK].rearrange("p (s n) -> p s n", n=NK)
            cand = hitf[:, UPS * 2 * NK:UPS * (2 * NK + TOPK * TOPK)].rearrange("p (u n) -> p u n", u=UPS)
            val = sb(down, "val", [128, UPS * 2, TOPK])
            key = sb(down, "key", [128, UPS * 2, TOPK], u32)
            pair = sb(down, "pair", [128, UPS, TOPK], u32)
            top = sb(down, "top", [128, UPS, TOPK])
            part = sb(down, "part", [128, UPS, 2, TOPK], u32)
            rank = sb(down, "rank", [128, 2, UPS * 2 * TOPK])
            picked = sb(down, "picked", [128, UPS, 3, TOPK])
            chosen = sb(down, "chosen", [128, 3, UNITS * TOPK])
            total = sb(down, "total", [128, UNITS])
            tps = ps(down, "tps", [128, 2, KD, 128])
            ups = ps(down, "ups", [128, 2, 2 * T])
            blk = down.enter_context(nc.Block())
            PER = 38

            def key_at_rank():
                return rank[:, 1].rearrange("p (b r) -> p b r", r=TOPK).unsqueeze(2).broadcast_to([128, UPS * 2, TOPK, TOPK])

            @blk.sync
            def _(sp):
                def body(u, second):
                    for j in range(UA):
                        wait(sp, "wd_transposed", u, UA, j - 1)
                        sp.dma_start(wd[:, j % 2, :], w_down[:, bass.ds((u * UA + j) * D, D)]).then_inc(S("wd_loaded%d" % (j % 2)), 16)
                halves(sp, NA, body)

            @blk.tensor
            def _(pe):
                mm = nc.tensor.matmul

                def transpose_tile(u, m):
                    wait(pe, "wd_loaded%d" % (m % 2), u, 16 * UA // 2, 16 * (m // 2 + 1))
                    wait(pe, "wT_hi", u, UA, m - 1)
                    wait(pe, "wT_lo", u, UA, m - 1)
                    for k in range(KD):
                        last = nc.tensor.transpose(tps[:, m % 2, k, :], wd[:, m % 2, 128 * k:128 * k + 128], ident[:])
                    last.then_inc(S("wd_transposed"), 1)

                def body(u, second):
                    for j in range(UA):
                        if not (at_step(u, NA - 1) and j == UA - 1):
                            transpose_tile(u, j + 1)
                        wait(pe, "wT_hi", u, UA, j + 1)
                        wait(pe, "wT_lo", u, UA, j + 1)
                        wait(pe, "u_copied", u, UA, j - 1)
                        dst = ups[:, j % 2, :]
                        for k in range(KD):
                            wide = lambda: mm(dst, wTh[:, j % 2, k, :], hT[:, k, :, :].rearrange("p s t -> p (s t)"), start=k == 0, stop=k == KD - 1)
                            narrow = lambda: mm(dst[:, T:2 * T], wTl[:, j % 2, k, :], hT[:, k, 0, :], start=False, stop=False)
                            if k < KD - 1:
                                wide()
                                narrow()
                            else:
                                narrow()
                                last = wide()
                        last.then_inc(S("u_done"), 1)
                        if at_step(u, SA - 1) and j == UA - 2:
                            pe.wait_ge(S("chosen_ready"), 1)
                            flat = gps[:].rearrange("p b n -> p (b n)")
                            for i in range(3):
                                for t in range(TT):
                                    at = T * i + 128 * t
                                    last = nc.tensor.transpose(flat[:, at:at + 128], chosen[:, i, 128 * t:128 * t + 128], ident[:])
                            last.then_inc(S("chosen_transposed"), 1)
                        if second:
                            make_gates(pe, u, j, False)

                transpose_tile(0, 0)
                halves(pe, NA, body, lambda: pe.wait_ge(S("chosen_taken"), 1))

            @blk.scalar
            def _(act):
                def hi(u, m):
                    wait(act, "wd_transposed", u, UA, m + 1)
                    wait(act, "u_done", u, UA, m - 1)
                    nc.scalar.activation(wTh[:, m % 2], tps[:, m % 2], ACT.Copy).then_inc(S("wT_hi"), 1)

                def gelu(u, m):
                    wait(act, "u_added", u, UA, m + 1)
                    nc.scalar.activation(act_flat[:, bass.ds((u * UA + m) * T, T)], ucopy[:, m % 2, 0:T], ACT.Gelu).then_inc(S("gelu_done"), 1)

                def body(u, second):
                    for j in range(UA):
                        if at_step(u, SA - 1) and j == UA - 2:
                            act.wait_ge(S("choice_step"), SA * PER)
                            nc.scalar.activation(chosen[:, 2, :], chosen[:, 2, :], ACT.Exp).then_inc(S("gate_exp"), 1)
                        if not (at_step(u, NA - 1) and j == UA - 1):
                            hi(u, j + 1)
                        if not second and j == 0:
                            wait(act, "choice_step", u, PER, 0)
                            nc.scalar.activation(hitf[:, 0:UPS * 2 * NK], scf[:, bass.ds(u * (UPS * 2 * NK), UPS * 2 * NK)],
                                                 ACT.Copy).then_inc(S("scores_copied"), 1)
                        wait(act, "u_done", u, UA, j + 1)
                        wait(act, "gelu_done", u, UA, j - 1)
                        nc.scalar.activation(ucopy[:, j % 2, :], ups[:, j % 2, :], ACT.Copy).then_inc(S("u_copied"), 1)
                        if not (at_step(u, 0) and j == 0):
                            gelu(u, j - 1)

                hi(0, 0)
                halves(act, NA, body)
                gelu(NA - 1, UA - 1)

            @blk.gpsimd
            def _(pool):
                iota = dict(base=0, channel_multiplier=0, allow_small_or_imprecise_dtypes=True)
                nc.gpsimd.iota(iota16[:], [[1, TOPK]], **iota).then_inc(S("iotas"), 1)
                nc.gpsimd.iota(iota128[:], [[1, NK]], **iota).then_inc(S("iotas"), 1)
                pool.wait_ge(S("iotas"), 2)

                def body(u, second):
                    for j in range(UA):
                        if second and not (at_step(u, NA - 1) and j == UA - 1):
                            make_one1(pool, u, j + 1, False)
                        wait(pool, "u_copied", u, UA, j + 1)
                        nc.gpsimd.tensor_tensor(ucopy[:, j % 2, 0:T], ucopy[:, j % 2, 0:T], ucopy[:, j % 2, T:2 * T], ALU.add).then_inc(S("u_added"), 1)
                        if not second and j == (UA - 4 if at_step(u, SA - 1) else UA - 2):
                            wait(pool, "hit_found", u, 1, 1)
                            hits = hitf.rearrange("p (b k r) -> p b k r", k=TOPK, r=TOPK)
                            nc.gpsimd.tensor_tensor(hits, hits, key_at_rank(), ALU.mult).then_inc(S("hit_weighted"), 1)

                def between():
                    pool.wait_ge(S("chosen_taken"), 1)
                    make_one1(pool, SA, 0, False)

                halves(pool, NA, body, between)

            @blk.vector
            def _(dve):
                link = Link(dve, "gate_link")

                def lo(u, m):
                    wait(dve, "wT_hi", u, UA, m + 1)
                    wait(dve, "u_done", u, UA, m - 1)
                    V.tensor_tensor(wTl[:, m % 2], tps[:, m % 2], wTh[:, m % 2].bitcast(f32), ALU.subtract).then_inc(S("wT_lo"), 1)

                def choice(u):
                    done = [0]

                    def mark(ins):
                        ins.then_inc(S("choice_step"), 1)
                        done[0] += 1

                    def settle():
                        wait(dve, "choice_step", u, PER, done[0])
                        dve.sem_inc(S("choice_go"), 1)

                    wait(dve, "scores_copied", u, 1, 1)
                    dve.sem_inc(S("choice_go"), 1)
                    for r in range(2):
                        eight = slice(8 * r, 8 * r + 8)
                        for b in range(UPS * 2):
                            mark(V.max(val[:, b, eight], score[:, b, :]))
                        yield
                        settle()
                        for b in range(UPS * 2):
                            mark(V.max_index(key[:, b, eight], val[:, b, eight], score[:, b, :]))
                        yield
                        settle()
                        if r == 0:
                            for b in range(UPS * 2):
                                mark(V.match_replace(score[:, b, :], val[:, b, eight], score[:, b, :], LOWEST))
                            yield
                            settle()
                    both = val[:].rearrange("p (u b) k -> p u b k", b=2)
                    shape = [128, UPS, TOPK, TOPK]
                    mark(V.tensor_tensor(cand.rearrange("p u (i j) -> p u i j", i=TOPK), both[:, :, 0, :].unsqueeze(3).broadcast_to(shape),
                                         both[:, :, 1, :].unsqueeze(2).broadcast_to(shape), ALU.add))
                    yield
                    settle()
                    for r in range(2):
                        eight = slice(8 * r, 8 * r + 8)
                        for i in range(UPS):
                            mark(V.max(top[:, i, eight], cand[:, i, :]))
                        yield
                        settle()
                        for i in range(UPS):
                            mark(V.max_index(pair[:, i, eight], top[:, i, eight], cand[:, i, :]))
                        yield
                        settle()
                        if r == 0:
                            for i in range(UPS):
                                mark(V.match_replace(cand[:, i, :], top[:, i, eight], cand[:, i, :], LOWEST))
                            yield
                            settle()
                    mark(V.tensor_scalar(part[:, :, 0, :], pair[:], 4, None, ALU.logical_shift_right))
                    mark(V.tensor_scalar(part[:, :, 1, :], pair[:], TOPK - 1, None, ALU.bitwise_and))
                    mark(V.tensor_copy(rank[:, 1], key[:].rearrange("p b k -> p (b k)")))
                    mark(V.tensor_tensor(picked[:, :, 2, :], top[:], top[:, :, 0:1].broadcast_to([128, UPS, TOPK]), ALU.subtract))
                    yield
                    settle()
                    mark(V.tensor_copy(rank[:, 0], part[:].rearrange("p u b k -> p (u b k)")))
                    settle()
                    n = UPS * 2 * TOPK
                    V.tensor_tensor(hitf.rearrange("p (n r) -> p n r", r=TOPK), rank[:, 0].unsqueeze(2).broadcast_to([128, n, TOPK]),
                                    iota16[:].unsqueeze(1).broadcast_to([128, n, TOPK]), ALU.is_equal).then_inc(S("hit_found"), 1)
                    yield
                    yield
                    wait(dve, "hit_weighted", u, 1, 1)
                    mark(V.tensor_reduce(picked[:, :, 0:2, :].rearrange("p u b k -> p u (b k)"), hit[:], AXX, ALU.add))
                    yield
                    settle()
                    mark(V.tensor_copy(chosen[:, :, bass.ds(u * (UPS * TOPK), UPS * TOPK)].rearrange("p i (u k) -> p i u k", u=UPS),
                                       picked[:].rearrange("p u i k -> p i u k")))
                    assert done[0] == PER, done
                    yield

                def softmax():
                    dve.wait_ge(S("gate_exp"), 1)
                    g3 = chosen[:, 2, :].rearrange("p (u k) -> p u k", u=UNITS)
                    link(V.tensor_reduce(total[:], g3, AXX, ALU.add))
                    link(V.reciprocal(total[:], total[:]))
                    V.tensor_tensor(g3, g3, total[:].unsqueeze(2).broadcast_to([128, UNITS, TOPK]), ALU.mult).then_inc(S("chosen_ready"), 1)

                def split_gates():
                    dve.wait_ge(S("chosen_transposed"), 1)
                    link(V.tensor_copy(chosenT, gps[:].rearrange("p b n -> p (b n)")[:, 0:3 * T].rearrange("p (i t) -> p i t", i=3)))
                    dve.sem_inc(S("chosen_taken"), 1)
                    for p in range(3):
                        link(V.tensor_copy(gbf, chosenT[:, 2, :]))
                        link(V.tensor_copy(gpart[:, p, :], gbf))
                        if p < 2:
                            link(V.tensor_tensor(chosenT[:, 2, :], chosenT[:, 2, :], gpart[:, p, :], ALU.subtract))

                def body(u, second):
                    parts = () if second else choice(u)
                    for j in range(UA):
                        if second:
                            if not (at_step(u, NA - 1) and j == UA - 1):
                                make_one2(dve, u, j + 1, False)
                            if not (at_step(u, SA) and j == 0):
                                use_gates(dve, u, j - 1, False)
                        if not (at_step(u, NA - 1) and j == UA - 1):
                            lo(u, j + 1)
                        if at_step(u, SA - 1):
                            for _ in range((3, 3, 3, 3, 2, 99, 0, 0)[j]):
                                next(parts, None)
                            if j == UA - 2:
                                softmax()
                            if j == UA - 1:
                                split_gates()
                                make_one2(dve, SA, 0, False)
                        elif not second:
                            for _ in range(2 if j < UA - 1 else 99):
                                next(parts, None)

                dve.wait_ge(S("iotas"), 2)
                lo(0, 0)
                halves(dve, NA, body, lambda: dve.wait_ge(S("gelu_done"), EH))
                use_gates(dve, NA - 1, UA - 1, False)

        upx = ExitStack()
        with upx:
            wu = sb(upx, "wu", [128, 4, D])
            wuh = hT[:].rearrange("p k s t -> p (k s t)").rearrange("p (s d) -> p s d", s=4)
            wul = sb(upx, "wul", [128, 4, D], f32r)
            ah = sb(upx, "ah", [128, 2, T], f32r)
            al = sb(upx, "al", [128, 2, T], f32r)
            acc = ps(upx, "acc", [128, TT, D])
            blk = upx.enter_context(nc.Block())
            NC = NK // UC
            POOL_UP = (400, 640)

            def is_last(u, j):
                return at_step(u, NC - 1) and j == UC - 1

            def last_group(u, j):
                return at_step(u, SC - 1) and j == UC - 1

            @blk.sync
            def _(sp):
                def body(u, second):
                    for j in range(UC):
                        wait(sp, "wu_hi", u, UC, j - 3)
                        wait(sp, "wu_lo_pool", u, UC, j - 3)
                        wait(sp, "wu_lo_dve", u, UC, j - 3)
                        sp.dma_start(wu[:, j % 4, :], w_up[:, bass.ds((u * UC + j) * D, D)]).then_inc(S("wu_loaded%d" % (j % 4)), 16)
                halves(sp, NC, body)
                dst = out.rearrange("o (t p) d -> p (o t) d", p=128)
                for t in range(TT):
                    sp.wait_ge(S("x_final"), t + 1)
                    sp.dma_start(dst[:, t, :], x[:, t, :]).then_inc(S("out_stored"), 16)
                sp.wait_ge(S("out_stored"), 16 * TT)

            @blk.scalar
            def _(act):
                def weights_hi(u, m):
                    wait(act, "wu_loaded%d" % (m % 4), u, 16 * UC // 4, 16 * (m // 4 + 1))
                    wait(act, "up_done", u, UC, m - 3)
                    nc.scalar.activation(wuh[:, m % 4, :], wu[:, m % 4, :], ACT.Copy).then_inc(S("wu_hi"), 1)

                def acts_hi(u, m):
                    wait(act, "up_done", u, UC, m - 1)
                    nc.scalar.activation(ah[:, m % 2, :], act_flat[:, bass.ds((u * UC + m) * T, T)], ACT.Copy).then_inc(S("act_hi"), 1)

                def body(u, second):
                    for j in range(UC):
                        if not is_last(u, j):
                            if last_group(u, j):
                                act.wait_ge(S("gates_used"), 2 * NG)
                            acts_hi(u, j + 1)
                        if not (is_last(u, j) or is_last(u, j + 1)):
                            weights_hi(u, j + 2)

                acts_hi(0, 0)
                weights_hi(0, 0)
                weights_hi(0, 1)
                halves(act, NC, body)

            @blk.gpsimd
            def _(pool):
                def weights_lo(u, m, second):
                    wait(pool, "wu_hi", u, UC, m + 1)
                    wait(pool, "up_done", u, UC, m - 3)
                    cols = slice(0, POOL_UP[second])
                    nc.gpsimd.tensor_tensor(wul[:, m % 4, cols], wu[:, m % 4, cols], wuh[:, m % 4, cols].bitcast(f32),
                                            ALU.subtract).then_inc(S("wu_lo_pool"), 1)

                def body(u, second):
                    for j in range(UC):
                        if not is_last(u, j):
                            weights_lo(u, j + 1, second)
                        if not second and not last_group(u, j):
                            make_one1(pool, u, j + 1, True)

                make_one1(pool, 0, 0, True)
                weights_lo(0, 0, False)
                halves(pool, NC, body)

            @blk.vector
            def _(dve):
                def weights_lo(u, m, second):
                    wait(dve, "wu_hi", u, UC, m + 1)
                    wait(dve, "up_done", u, UC, m - 3)
                    cols = slice(POOL_UP[second], D)
                    V.tensor_tensor(wul[:, m % 4, cols], wu[:, m % 4, cols], wuh[:, m % 4, cols].bitcast(f32),
                                    ALU.subtract).then_inc(S("wu_lo_dve"), 1)

                def acts_lo(u, m):
                    wait(dve, "act_hi", u, UC, m + 1)
                    wait(dve, "up_done", u, UC, m - 1)
                    V.tensor_tensor(al[:, m % 2, :], act_flat[:, bass.ds((u * UC + m) * T, T)], ah[:, m % 2, :].bitcast(f32),
                                    ALU.subtract).then_inc(S("act_lo"), 1)

                def body(u, second):
                    for j in range(UC):
                        if not second:
                            if not last_group(u, j):
                                make_one2(dve, u, j + 1, True)
                            if not (at_step(u, 0) and j == 0):
                                use_gates(dve, u, j - 1, True)
                            if last_group(u, j):
                                use_gates(dve, u, j, True)
                                dve.wait_ge(S("gates_used"), 2 * NG)
                        if not is_last(u, j):
                            acts_lo(u, j + 1)
                            weights_lo(u, j + 1, second)

                acts_lo(0, 0)
                weights_lo(0, 0, False)
                make_one2(dve, 0, 0, True)
                halves(dve, NC, body)
                for t in range(TT):
                    dve.wait_ge(S("up_done"), NK)
                    V.tensor_tensor(x[:, t, :], x[:, t, :], acc[:, t, :], ALU.add).then_inc(S("x_final"), 1)

            @blk.tensor
            def _(pe):
                def body(u, second):
                    for j in range(UC):
                        wait(pe, "wu_lo_pool", u, UC, j + 1)
                        wait(pe, "wu_lo_dve", u, UC, j + 1)
                        wait(pe, "act_lo", u, UC, j + 1)
                        for t in range(TT):
                            for half in range(2):
                                cols, toks = slice(512 * half, 512 * half + 512), slice(128 * t, 128 * t + 128)
                                last = three(acc[:, t, cols], ah[:, j % 2, toks], al[:, j % 2, toks], wuh[:, j % 4, cols], wul[:, j % 4, cols],
                                             start=at_step(u, 0) and j == 0, stop=is_last(u, j))
                        last.then_inc(S("up_done"), 1)
                        if not second:
                            make_gates(pe, u, j, True)
                halves(pe, NC, body)


_INS = ["x", "mix_norm_w", "w_in", "q_norm_w", "k_norm_w", "conv_w", "conv_b", "igate_b", "fgate_b", "mlstm_norm_w",
        "w_attn_branch", "w_mlstm_branch", "merge_b", "w_out", "ffn_norm_w", "peer_w_query", "peer_keys_1",
        "peer_keys_2", "peer_w_down", "peer_w_up"]


def kernel(**inputs):
    import numpy as np
    import concourse.bacc as bacc
    from concourse.bass_utils import run_bass_kernel_spmd

    freq = np.float32(500000.0) ** (-np.arange(0, ROT, 2, dtype=np.float32) / np.float32(ROT))
    angle = np.arange(T, dtype=np.float32)[:, None] * freq[None, :]
    arrays = {"rope": np.concatenate([np.cos(angle), np.sin(angle)], axis=1).astype(np.float32)}
    for name in _INS:
        arrays[name] = np.ascontiguousarray(inputs[name])
    nc = bacc.Bacc("TRN2", target_bir_lowering=False, num_devices=1)
    aps = {n: nc.dram_tensor("in_" + n, v.shape, mybir.dt.from_np(v.dtype), kind="ExternalInput").ap() for n, v in arrays.items()}
    out = nc.dram_tensor("out", (1, T, D), mybir.dt.float32, kind="ExternalOutput").ap()
    build(nc, aps, out)
    r = run_bass_kernel_spmd(nc, [{"in_" + n: v for n, v in arrays.items()}], core_ids=[0])
    return r.results[0]["out"]
```

```python
from contextlib import ExitStack

import concourse.bass as bass
from concourse import mybir

T, D = 256, 1024
TT, KD = T // 128, D // 128
AH, AD = 8, 64
MH, MD = 4, 128
ROT = AD // 4
CONV = 4
PH, NK, TOPK = 8, 128, 16
EPS = 1e-6
BIG = 1e30
LOWEST = -3.4028234663852886e38

COL = {}
_at = 0
for _n, _w in (("aq", 512), ("ak", 512), ("av", 512), ("mq", 512), ("mk", 512), ("mv", 512),
               ("mo", 512), ("mi", MH), ("mf", MH), ("ga", D), ("gm", D)):
    COL[_n] = _at
    _at += _w

CW = 256
CE = KD * CW
CHUNKS = [(_n, _j) for _n, _k in (("mq", 2), ("mk", 2), ("aq", 2), ("ak", 2), ("av", 2), ("mv", 2),
                                  ("mo", 2), ("ga", 4), ("gm", 4), ("wab", 2), ("wmb", 2),
                                  ("wo", 4), ("wq", 8)) for _j in range(_k)]
INDEX = {_c: _i for _i, _c in enumerate(CHUNKS)}
BRANCH = ("wab", "wmb")
GROUPS = [(_c, _h) for _c in CHUNKS for _h in range(2 if _c[0] in BRANCH else 1)]
BY_DVE = ("wab", "wmb", "wo")


def pool_lo(n):
    return 0 if CHUNKS[n] == ("mv", 0) else 704


VEC = {}
_at = 0
for _n, _w in (("mixw", 8), ("cw", 32), ("cb", 8), ("mnw", 4), ("mb", 16), ("ffw", 8)):
    VEC[_n] = _at
    _at += _w
NVEC = _at

MISC = {}
for _n, _k in (("vec", 1), ("xT", 4), ("gates", 1), ("qkT", 4), ("S", 6), ("gcol", 1), ("negM", 2),
               ("ST", 3), ("PT", 6), ("PV", 2), ("num", 4), ("hmT", 2), ("key", 4), ("h2T", 4),
               ("sc", 8)):
    for _j in range(_k):
        MISC[_n, _j] = len(MISC)

XSS, QKSS, MSS, X2SS, X2SUM = 0, 2, 34, 42, 50

FG = 32

UA = 8
NA = NK // UA
UG = 4
EH = NK // 2
UC = 8


def groups_before(group, dve):
    return sum((c[0] in BY_DVE) == dve for c, _ in GROUPS[:group + 1])


def groups_through(n):
    return sum(len([g for g in GROUPS if g[0] == c]) for c in CHUNKS[:n + 1])


def build(nc, a, out):
    f32, f32r, bf16, u32 = mybir.dt.float32, mybir.dt.float32r, mybir.dt.bfloat16, mybir.dt.uint32
    ALU, ACT, AXX = mybir.AluOpType, mybir.ActivationFunctionType, mybir.AxisListType.X
    keep = ExitStack()
    sems = {}

    def S(name):
        if name not in sems:
            sems[name] = keep.enter_context(nc.semaphore(name))
        return sems[name]

    def sb(stack, name, shape, dt=f32):
        return stack.enter_context(nc.sbuf_tensor(name, shape, dt))

    def ps(stack, name, shape, dt=f32):
        return stack.enter_context(nc.psum_tensor(name, shape, dt))

    class Link:

        def __init__(self, eng, name):
            self.eng, self.sem, self.n = eng, S(name), 0

        def mark(self, ins):
            self.n += 1
            ins.then_inc(self.sem, 1)

        def settle(self):
            self.eng.wait_ge(self.sem, self.n)

        def __call__(self, ins):
            self.mark(ins)
            self.settle()

    with keep:
        x = sb(keep, "x", [128, TT, D])
        hT = sb(keep, "hT", [128, KD, 2, T], f32r)
        hTh, hTl = hT[:, :, 0, :], hT[:, :, 1, :]
        ident = sb(keep, "ident", [128, 128])
        sc = sb(keep, "sc", [128, TT, PH, 2, NK])

        work = sb(keep, "work", [128, 2048])

        front = ExitStack()
        with front:
            raw = sb(front, "raw", [128, 3, CE])
            whi = sb(front, "whi", [128, 3, CE], f32r)
            wlo = sb(front, "wlo", [128, 3, CE], f32r)
            vcol = sb(front, "vcol", [128, NVEC])
            minus_half = sb(front, "minus_half", [128, 32])
            stat = sb(front, "stat", [128, 64])
            hq = sb(front, "hq", [128, KD, T])
            qk = sb(front, "qk", [128, TT, 2 * AH * AD])
            probT = sb(front, "probT", [128, 3072])
            cv = sb(front, "cv", [128, 2 * MH, T])
            upv = sb(front, "upv", [128, 2072])
            v = sb(front, "v", [128, TT, AH * AD])
            gsig = sb(front, "gsig", [128, 16, T])
            branch = sb(front, "branch", [128, 4, 2, T], f32r)
            tri_q = sb(front, "tri_q", [128, 128])
            tri_s = sb(front, "tri_s", [128, 256])
            sel = sb(front, "sel", [MH, MH, 128])
            vrow = sb(front, "vrow", [NVEC, 128])
            qkw = sb(front, "qkw", [128, 2, AD])
            rot = sb(front, "rot", [128, TT, ROT])
            gbias = sb(front, "gbias", [MH, 2])
            wgate = sb(front, "wgate", [128, KD, 2 * MH])
            wpair = sb(front, "wpair", [128, KD, FG + MH])
            grow = sb(front, "grow", [MH, 6, T])
            gcol = sb(front, "gcol", [128, TT, 2, MH])
            den = sb(front, "den", [128, TT, MH])
            arow = sb(front, "arow", [128, 3, TT, AH])
            ones4 = sb(front, "ones4", [MH, T])
            proj = ps(front, "proj", [128, 4, 512])
            misc = ps(front, "misc", [128, 4, 512])

            up = upv[:].rearrange("p (c t) -> p c t", c=8)
            v1 = upv[:, 0:TT * MH * (MD + 1)].rearrange("p (t h c) -> p t h c", t=TT, h=MH)
            mosig = upv[:, 1032:1032 + 1024].rearrange("p (t c) -> p t c", t=TT)
            scf = sc[:].rearrange("p a b c d -> p (a b c d)")
            sig = scf[:, 0:2048].rearrange("p (c t) -> p c t", c=8)
            hwork = work[:].rearrange("p (t c) -> p t c", t=TT)
            dT0 = work[:, 0:1024].rearrange("p (h t) -> p h t", h=MH)
            dT1 = work[:, 1024:1536].rearrange("p (h t) -> p h t", h=MH)
            keyn = work[:].rearrange("p (b h d) -> p b h d", b=2, h=PH)
            p0 = scf[:, 0:1024].rearrange("p (h k) -> p h k", h=AH)
            p1 = scf[:, 1024:3072].rearrange("p (h k) -> p h k", h=AH)
            pT0 = probT[:, 0:2048].rearrange("p (h q) -> p h q", h=AH)
            pT1 = probT[:, 2048:3072].rearrange("p (h q) -> p h q", h=AH)
            keyT = probT[:, 0:2048].rearrange("p (b h n) -> p b h n", b=2, h=PH)
            aTh, aTl = branch[:, :, 0, :], branch[:, :, 1, :]
            mTh, mTl = hT[:, 0:4, 0, :], hT[:, 0:4, 1, :]

            def y_part(k, n, s):
                return (branch if k < 4 else hT)[:, k:k + n, s, :]

            aT = cv[:, 0:4, :]
            mT = cv[:, 4:8, :]
            hm = qk[:, :, 0:512]
            hsq = qk[:, :, 512:1024]
            rI, rLF, rTMP, rF, rG, rNM = range(6)

            def bank(name, i=0):
                return misc[:, MISC[name, i] % 4, :]

            def chunk_source(c):
                name, j = c
                if name in BRANCH:
                    src = a["w_attn_branch" if name == "wab" else "w_mlstm_branch"]
                    return src[:, j * 512:(j + 1) * 512].rearrange("(k p) n -> p k n", p=128)
                if name == "wo":
                    src, at = a["w_out"], j * CW
                elif name == "wq":
                    src, at = a["peer_w_query"], j * CW
                else:
                    src, at = a["w_in"], COL[name] + j * CW
                return src[:, at:at + CW].rearrange("(k p) n -> p k n", p=128)

            def as_chunk(flat, c):
                return flat.rearrange("p (k n) -> p k n", k=4 if c[0] in BRANCH else KD)

            blk = front.enter_context(nc.Block())

            @blk.sync
            def _(sp):
                for t in range(TT):
                    sp.dma_start(x[:, t, :], a["x"][0, t * 128:(t + 1) * 128, :]).then_inc(S("x_loaded%d" % t), 16)
                for name, rows in (("mixw", a["mix_norm_w"].rearrange("(r c) -> r c", c=128)),
                                   ("cw", a["conv_w"].rearrange("j (r c) -> (j r) c", c=128)),
                                   ("cb", a["conv_b"].rearrange("(r c) -> r c", c=128)),
                                   ("mnw", a["mlstm_norm_w"].rearrange("(r c) -> r c", c=128)),
                                   ("mb", a["merge_b"].rearrange("j (r c) -> (j r) c", c=128)),
                                   ("ffw", a["ffn_norm_w"].rearrange("(r c) -> r c", c=128))):
                    sp.dma_start(vrow[VEC[name]:VEC[name] + rows.shape[0], :], rows).then_inc(S("vec_loaded"), 16)
                for n, c in enumerate(CHUNKS):
                    if n >= 3:
                        sp.wait_ge(S("hi_ready"), n - 2)
                        sp.wait_ge(S("lo_dve_ready"), n - 2)
                        sp.wait_ge(S("lo_pool_ready"), n - 2)
                    sp.dma_start(as_chunk(raw[:, n % 3, :], c), chunk_source(c)).then_inc(S("raw_loaded%d" % (n % 3)), 16)
                    if n == 1:
                        sp.dma_start(qkw[:, 0, :], a["q_norm_w"].partition_broadcast(128)).then_inc(S("small_loaded"), 16)
                        sp.dma_start(qkw[:, 1, :], a["k_norm_w"].partition_broadcast(128)).then_inc(S("small_loaded"), 16)
                        sp.dma_start(rot[:], a["rope"].rearrange("(t p) r -> p t r", p=128)).then_inc(S("small_loaded"), 16)
                        sp.dma_start(gbias[:, 0:1], a["igate_b"].rearrange("(n o) -> n o", o=1)).then_inc(S("small_loaded"), 16)
                        sp.dma_start(gbias[:, 1:2], a["fgate_b"].rearrange("(n o) -> n o", o=1)).then_inc(S("small_loaded"), 16)
                        sp.dma_start(wgate[:], a["w_in"][:, COL["mi"]:COL["mi"] + 2 * MH].rearrange(
                            "(k p) n -> p k n", p=128)).then_inc(S("small_loaded"), 16)
                    if c == ("gm", 3):
                        sp.wait_ge(S("num_done"), 1)
                        sp.dma_start(keyn[:, 0], a["peer_keys_1"].rearrange("h n d -> n h d")).then_inc(S("key_loaded"), 16)
                        sp.dma_start(keyn[:, 1], a["peer_keys_2"].rearrange("h n d -> n h d")).then_inc(S("key_loaded"), 16)
                sp.wait_ge(S("misc_full"), MISC["h2T", 3] + 1)
                w_down = a["peer_w_down"].rearrange("(p e) d -> p (e d)", e=NK)
                for j in range(2):
                    sp.dma_start(work[:, D * j:D * j + D], w_down[:, D * j:D * j + D]).then_inc(S("wd_loaded%d" % j), 16)

            @blk.gpsimd
            def _(pool):
                link = Link(pool, "pool_link")
                g = nc.gpsimd
                link(g.memset(ident[:], 0.0))
                g.affine_select(out=ident[:], in_=ident[:], compare_op=ALU.not_equal, fill=1.0, base=0,
                                pattern=[[-1, 128]], channel_multiplier=1).then_inc(S("ident_ready"), 1)
                link.mark(g.memset(minus_half[:], -0.5))
                g.memset(up[:, :, 0:CONV - 1], 0.0).then_inc(S("pad_ready"), 1)
                g.memset(ones4[:], 1.0).then_inc(S("const_ready"), 1)
                link.mark(g.memset(wpair[:], 0.0))
                link.mark(g.memset(tri_q[:], 0.0))
                link.mark(g.memset(tri_s[:], 0.0))
                link(g.memset(sel[:], 0.0))
                g.affine_select(out=tri_q[:], in_=tri_q[:], compare_op=ALU.is_ge, fill=-BIG, base=0,
                                pattern=[[-1, 128]], channel_multiplier=1).then_inc(S("const_ready"), 1)
                g.affine_select(out=tri_s[:], in_=tri_s[:], compare_op=ALU.is_ge, fill=-BIG, base=0,
                                pattern=[[1, 256]], channel_multiplier=-1).then_inc(S("const_ready"), 1)
                g.affine_select(out=sel[:], in_=sel[:], compare_op=ALU.not_equal, fill=1.0, base=0,
                                pattern=[[-1, MH], [0, 128]], channel_multiplier=1).then_inc(S("const_ready"), 1)

                def rsqrt(at, n, width, done):
                    link(g.tensor_scalar(stat[:, at:at + n], stat[:, at:at + n], 1.0 / width, EPS, ALU.mult, ALU.add))
                    g.tensor_tensor(stat[:, at:at + n], stat[:, at:at + n], minus_half[:, 0:n], ALU.pow).then_inc(S(done), 1)

                pool.wait_ge(S("x_squared"), 2)
                rsqrt(XSS, TT, D, "x_rstd")
                for n, c in enumerate(CHUNKS):
                    pool.wait_ge(S("raw_loaded%d" % (n % 3)), 16 * (n // 3 + 1))
                    pool.wait_ge(S("hi_ready"), n + 1)
                    if n >= 3:
                        pool.wait_ge(S("proj_done"), groups_through(n - 3))
                    own = slice(0, pool_lo(n))
                    if pool_lo(n):
                        g.tensor_tensor(wlo[:, n % 3, own], raw[:, n % 3, own],
                                        whi[:, n % 3, own].bitcast(f32), ALU.subtract).then_inc(S("lo_pool_ready"), 1)
                    else:
                        pool.sem_inc(S("lo_pool_ready"), 1)
                    if c == ("mq", 1):
                        pool.wait_ge(S("small_loaded"), 96)
                        for i in range(2):
                            g.tensor_copy(wpair[:, :, FG * i:FG * i + MH], wgate[:, :, MH * i:MH * i + MH]).then_inc(S("wpair_ready"), 1)
                    if c in (("aq", 0), ("ak", 0)):
                        j = 0 if c[0] == "aq" else 1
                        pool.wait_ge(S("conv_sig"), j + 1)
                        g.tensor_tensor(cv[:, 4 * j:4 * j + 4, :], cv[:, 4 * j:4 * j + 4, :],
                                        sig[:, 4 * j:4 * j + 4, :], ALU.mult).then_inc(S("silu_done"), 1)
                    if c == ("av", 1):
                        pool.wait_ge(S("qk_squared"), 1)
                        rsqrt(QKSS, 32, AD, "qk_rstd")
                    if c == ("gm", 1):
                        pool.wait_ge(S("hm_squared"), 1)
                        rsqrt(MSS, 8, MD, "hm_rstd")
                    if c == ("wq", 0):
                        pool.wait_ge(S("x2_summed"), 1)
                        rsqrt(X2SUM, TT, D, "x2_rstd")

            @blk.scalar
            def _(act):
                link = Link(act, "act_link")

                def hi(n):
                    act.wait_ge(S("raw_loaded%d" % (n % 3)), 16 * (n // 3 + 1))
                    if n >= 3:
                        act.wait_ge(S("proj_done"), groups_through(n - 3))
                        act.wait_ge(S("lo_dve_ready"), n - 2)
                        act.wait_ge(S("lo_pool_ready"), n - 2)
                    nc.scalar.activation(whi[:, n % 3, :], raw[:, n % 3, :], ACT.Copy).then_inc(S("hi_ready"), 1)

                def take(c):
                    name, j = c
                    g = GROUPS.index((c, 0))
                    bank2 = proj[:, g % 4, :].rearrange("p (i n) -> p i n", i=2)
                    act.wait_ge(S("proj_done"), g + 1)
                    if name in ("mq", "mk"):
                        at = (0 if name == "mq" else 4) + 2 * j
                        nc.scalar.activation(up[:, at:at + 2, CONV - 1:], bank2, ACT.Copy).then_inc(S("proj_taken_act"), 1)
                    elif name in ("aq", "ak"):
                        at = (0 if name == "aq" else 512) + CW * j
                        nc.scalar.activation(qk[:, :, at:at + CW], bank2, ACT.Copy).then_inc(S("proj_taken_act"), 1)
                    elif name == "av":
                        nc.scalar.activation(v[:, :, CW * j:CW * j + CW], bank2, ACT.Copy).then_inc(S("proj_taken_act"), 1)
                    elif name == "mv":
                        act.wait_ge(S("conv_done"), 2)
                        for t in range(TT):
                            last = nc.scalar.activation(v1[:, t, 2 * j:2 * j + 2, 0:MD],
                                                        bank2[:, t, :].rearrange("p (h c) -> p h c", h=2), ACT.Copy)
                            last.then_inc(*((S("proj_taken_act"), 1) if t else (S("v1_half"), 1)))
                    elif name == "mo":
                        nc.scalar.activation(mosig[:, :, CW * j:CW * j + CW], bank2, ACT.Sigmoid).then_inc(S("proj_taken_act"), 1)
                    elif name in ("ga", "gm"):
                        at = (0 if name == "ga" else 8) + 2 * j
                        for i in range(2):
                            b = VEC["mb"] + at + i
                            last = nc.scalar.activation(gsig[:, at + i, :], bank2[:, i, :], ACT.Sigmoid, bias=vcol[:, b:b + 1])
                            last.then_inc(*((S("proj_taken_act"), 1) if i else (S("gate_half"), 1)))
                    elif name == "wq":
                        act.wait_ge(S("y_ready"), 4)
                        nc.scalar.activation(gsig[:, 2 * j:2 * j + 2, :], bank2, ACT.Copy).then_inc(S("proj_taken_act"), 1)

                def split_hi(dst, src, bank_taken, done):
                    act.wait_ge(S("misc_free"), MISC[bank_taken] + 1)
                    nc.scalar.activation(dst, src, ACT.Copy).then_inc(S(done), 1)

                for t in range(TT):
                    act.wait_ge(S("x_loaded%d" % t), 16)
                    nc.scalar.activation(hwork[:, t, :], x[:, t, :], ACT.Square,
                                         accum_out=stat[:, XSS + t:XSS + t + 1]).then_inc(S("x_squared"), 1)
                hi(0)
                for b in range(4):
                    split_hi(hTh[:, 2 * b:2 * b + 2, :], hq[:, 2 * b:2 * b + 2, :], ("xT", b), "h_hi")
                hi(1)
                for n, c in enumerate(CHUNKS):
                    if n + 2 < len(CHUNKS):
                        hi(n + 2)
                    if c[0] not in BY_DVE:
                        take(c)
                    if c in (("mk", 1), ("aq", 0)):
                        j = 0 if c[0] == "mk" else 1
                        act.wait_ge(S("conv_done"), j + 1)
                        nc.scalar.activation(sig[:, 4 * j:4 * j + 4, :], cv[:, 4 * j:4 * j + 4, :],
                                             ACT.Sigmoid).then_inc(S("conv_sig"), 1)
                    if c == ("aq", 1):
                        act.wait_ge(S("gates_read"), 1)
                        link(nc.scalar.activation(grow[:, rTMP, :], grow[:, rTMP, :], ACT.Exp, scale=-1.0))
                        nc.scalar.activation(grow[:, rTMP, :], grow[:, rTMP, :], ACT.Ln, bias=1.0).then_inc(S("softplus_done"), 1)
                    if c == ("mo", 1):
                        act.wait_ge(S("s_max"), 1)
                        for t, p in enumerate((p0, p1)):
                            for h in range(AH):
                                nc.scalar.activation(p[:, h, :], p[:, h, :], ACT.Exp, bias=arow[:, 1, t, h:h + 1], scale=AD ** -0.5,
                                                     accum_out=arow[:, 2, t, h:h + 1]).then_inc(S("p_exp"), 1)
                        act.wait_ge(S("misc_free"), MISC["negM", 1] + 1)
                        for h in range(MH):
                            nc.scalar.activation(dT0[:, h, :], dT0[:, h, :], ACT.Exp, bias=gcol[:, 0, 0, h:h + 1]).then_inc(S("decay"), 1)
                            nc.scalar.activation(dT1[:, h, :], dT1[:, h, :], ACT.Exp, bias=gcol[:, 1, 0, h:h + 1]).then_inc(S("decay"), 1)
                        nc.scalar.activation(gcol[:, :, 1, :], gcol[:, :, 1, :], ACT.Exp).then_inc(S("decay"), 1)
                    if c == ("gm", 2):
                        split_hi(aTh[:], aT, ("PV", 1), "aT_hi")
                    if c == ("wab", 0):
                        act.wait_ge(S("proj_done"), groups_through(INDEX["gm", 3]))
                        split_hi(mTh[:], mT, ("hmT", 1), "mT_hi")
                    if c[0] == "wmb":
                        for q in range(2 * c[1], 2 * c[1] + 2):
                            act.wait_ge(S("y_ready"), q + 1)
                            nc.scalar.activation(y_part(2 * q, 2, 0), hq[:, 2 * q:2 * q + 2, :], ACT.Copy).then_inc(S("y_hi"), 1)
                    if c[0] == "wo":
                        act.wait_ge(S("proj_taken_dve"), groups_before(GROUPS.index((c, 0)), True))
                        act.wait_ge(S("misc_free"), MISC["key", 3] + 1)
                        cols = slice(CW * c[1], CW * c[1] + CW)
                        for t in range(TT):
                            at = X2SS + 4 * t + c[1]
                            nc.scalar.activation(hwork[:, t, cols], x[:, t, cols], ACT.Square,
                                                 accum_out=stat[:, at:at + 1]).then_inc(S("x2_squared"), 1)
                    if c == ("wo", 3):
                        for b in range(4):
                            split_hi(hTh[:, 2 * b:2 * b + 2, :], hq[:, 2 * b:2 * b + 2, :], ("h2T", b), "h2_hi")

            @blk.vector
            def _(dve):
                link = Link(dve, "dve_link")
                V = nc.vector

                def lo(n):
                    dve.wait_ge(S("raw_loaded%d" % (n % 3)), 16 * (n // 3 + 1))
                    dve.wait_ge(S("hi_ready"), n + 1)
                    if n >= 3:
                        dve.wait_ge(S("proj_done"), groups_through(n - 3))
                    own = slice(pool_lo(n), CE)
                    V.tensor_tensor(wlo[:, n % 3, own], raw[:, n % 3, own],
                                    whi[:, n % 3, own].bitcast(f32), ALU.subtract).then_inc(S("lo_dve_ready"), 1)

                def full(name, i=0):
                    dve.wait_ge(S("misc_full"), MISC[name, i] + 1)
                    return bank(name, i)

                def free(ins):
                    ins.then_inc(S("misc_free"), 1)

                def by2(ap):
                    return ap.rearrange("p (i n) -> p i n", i=2)

                def normalise(at):
                    for half in range(2):
                        cols = slice(512 * half, 512 * half + 512)
                        for t in range(TT):
                            V.tensor_scalar(hwork[:, t, cols], x[:, t, cols], stat[:, at + t:at + t + 1], None, ALU.mult).then_inc(S("h_nat"), 1)

                dve.wait_ge(S("x_rstd"), 1)
                for t in range(TT):
                    dve.wait_ge(S("x_loaded%d" % t), 16)
                normalise(XSS)
                free(V.tensor_copy(vcol[:], full("vec")[:, 0:NVEC]))
                dve.wait_ge(S("misc_free"), 1)

                def weighted_transpose(name, vec, hi_done, lo_done, before=None):
                    def low(b):
                        dve.wait_ge(S(hi_done), b + 1)
                        V.tensor_tensor(hTl[:, 2 * b:2 * b + 2, :], hq[:, 2 * b:2 * b + 2, :], hTh[:, 2 * b:2 * b + 2, :].bitcast(f32),
                                        ALU.subtract).then_inc(S(lo_done), 1)
                    for b in range(4):
                        src = by2(full(name, b))
                        for i in range(2):
                            k = 2 * b + i
                            ins = V.tensor_scalar(hq[:, k, :], src[:, i, :], vcol[:, VEC[vec] + k:VEC[vec] + k + 1], None, ALU.mult)
                        free(ins)
                    if before:
                        before()
                    for b in range(4):
                        low(b)

                weighted_transpose("xT", "mixw", "h_hi", "h_lo", lambda: lo(0))
                lo(1)
                for n, c in enumerate(CHUNKS):
                    if c in (("mk", 0), ("mk", 1)):
                        j = c[1]
                        dve.wait_ge(S("pad_ready"), 1)
                        dve.wait_ge(S("proj_taken_act"), 2 * j + 2)
                        for tap in range(CONV):
                            for i in range(4 * j, 4 * j + 4):
                                w = vcol[:, VEC["cw"] + 8 * tap + i:VEC["cw"] + 8 * tap + i + 1]
                                src = up[:, i, tap:tap + T]
                                if tap == 0:
                                    ins = V.tensor_scalar(cv[:, i, :], src, w, None, ALU.mult)
                                else:
                                    ins = V.scalar_tensor_tensor(out=cv[:, i, :], in0=src, scalar=w, in1=cv[:, i, :],
                                                                 op0=ALU.mult, op1=ALU.add)
                                link.mark(ins)
                            link.settle()
                        for i in range(4 * j, 4 * j + 4):
                            ins = V.tensor_scalar(cv[:, i, :], cv[:, i, :], vcol[:, VEC["cb"] + i:VEC["cb"] + i + 1], None, ALU.add)
                        ins.then_inc(S("conv_done"), 1)
                        if j == 1:
                            dve.wait_ge(S("small_loaded"), 96)
                            src = full("gates")[:, 0:T]
                            link.mark(V.tensor_scalar(grow[:, rI, :], src[0:MH], gbias[:, 0:1], None, ALU.add))
                            free(V.tensor_scalar(grow[:, rLF, :], src[FG:FG + MH], gbias[:, 1:2], None, ALU.add))
                            dve.wait_ge(S("misc_free"), MISC["gates", 0] + 1)
                            V.scalar_tensor_tensor(out=grow[:, rTMP, :], in0=grow[:, rLF, :], scalar=-1.0, in1=grow[:, rLF, :],
                                                   op0=ALU.mult, op1=ALU.max).then_inc(S("gates_read"), 1)
                    if c == ("ak", 0):
                        dve.wait_ge(S("softplus_done"), 1)
                        dve.wait_ge(S("const_ready"), 4)
                        link(V.scalar_tensor_tensor(out=grow[:, rLF, :], in0=grow[:, rLF, :], scalar=0.0, in1=grow[:, rTMP, :],
                                                    op0=ALU.min, op1=ALU.subtract))
                        link(V.tensor_tensor_scan(grow[:, rF, :], ones4[:], grow[:, rLF, :], 0.0, ALU.mult, ALU.add))
                        link(V.tensor_tensor(grow[:, rG, :], grow[:, rI, :], grow[:, rF, :], ALU.subtract))
                        link(V.tensor_tensor_scan(grow[:, rNM, :], grow[:, rG, :], grow[:, rG, :], 0.0, ALU.max, ALU.max))
                        link(V.scalar_tensor_tensor(out=grow[:, rTMP, :], in0=grow[:, rF, :], scalar=-1.0, in1=grow[:, rNM, :],
                                                    op0=ALU.mult, op1=ALU.subtract))
                        V.tensor_scalar(grow[:, rNM, :], grow[:, rNM, :], -1.0, None, ALU.mult).then_inc(S("gate_rows"), 1)
                    if c == ("ak", 1):
                        dve.wait_ge(S("proj_taken_act"), 8)
                        dve.wait_ge(S("h_nat"), 4)
                        dve.wait_ge(S("misc_full"), MISC["xT", 3] + 1)
                        link(V.tensor_tensor(hwork[:], qk[:], qk[:], ALU.mult))
                        V.tensor_reduce(stat[:, QKSS:QKSS + 32], hwork[:].rearrange("p t (h c) -> p (t h) c", c=AD), AXX,
                                        ALU.add).then_inc(S("qk_squared"), 1)
                    if c == ("mv", 0):
                        dve.wait_ge(S("qk_rstd"), 1)
                        qh = qk[:].rearrange("p t (h c) -> p (t h) c", c=AD)
                        link(V.tensor_tensor(qh, qh, stat[:, QKSS:QKSS + 32].unsqueeze(2).broadcast_to([128, 32, AD]), ALU.mult))
                        for t in range(TT):
                            for i in range(2):
                                q1 = qk[:, t, 512 * i:512 * i + 512].rearrange("p (h c) -> p h c", c=AD)
                                link.mark(V.tensor_tensor(q1, q1, qkw[:, i, :].unsqueeze(1).broadcast_to([128, AH, AD]), ALU.mult))
                        link.settle()
                        half = ROT // 2
                        for t in range(TT):
                            qt = qk[:, t, :].rearrange("p (h c) -> p h c", c=AD)
                            x1, x2 = qt[:, :, 0:half], qt[:, :, half:ROT]
                            cos = rot[:, t, 0:half].unsqueeze(1).broadcast_to([128, 2 * AH, half])
                            sin = rot[:, t, half:ROT].unsqueeze(1).broadcast_to([128, 2 * AH, half])
                            tmp = [hwork[:, t, 128 * i:128 * i + 128].rearrange("p (h c) -> p h c", c=half) for i in range(4)]
                            for i, (u, w) in enumerate(((x1, cos), (x2, sin), (x2, cos), (x1, sin))):
                                link.mark(V.tensor_tensor(tmp[i], u, w, ALU.mult))
                            link.settle()
                            link.mark(V.tensor_tensor(x1, tmp[0], tmp[1], ALU.subtract))
                            V.tensor_tensor(x2, tmp[2], tmp[3], ALU.add).then_inc(S("qk_ready"), 1)
                        link.settle()
                    if c == ("mv", 1):
                        dve.wait_ge(S("conv_done"), 2)
                        V.memset(v1[:, :, :, MD:MD + 1], 1.0).then_inc(S("v1_ones"), 1)
                        for b in range(4):
                            src = by2(full("qkT", b))
                            free(V.tensor_copy(hq[:, 2 * b:2 * b + 2, :], src))
                    if c == ("mo", 1):
                        dve.wait_ge(S("silu_done"), 2)
                        for b in range(2):
                            src = full("S", b).rearrange("p (h k) -> p h k", h=4)
                            free(V.tensor_tensor(p0.rearrange("p (i o) k -> p o i k", o=2)[:, b], src, tri_q[:].unsqueeze(1).broadcast_to([128, 4, 128]), ALU.add))
                        for b in range(4):
                            src = full("S", 2 + b).rearrange("p (h k) -> p h k", h=2)
                            dst = p1.rearrange("p (q i o) k -> p q o i k", i=2, o=2)[:, b // 2, b % 2]
                            link.mark(V.tensor_copy(dst[:, :, 0:128], src[:, :, 0:128]))
                            free(V.tensor_tensor(dst[:, :, 128:256], src[:, :, 128:256],
                                                 tri_q[:].unsqueeze(1).broadcast_to([128, 2, 128]), ALU.add))
                        link.settle()
                        dve.wait_ge(S("misc_free"), MISC["S", 5] + 1)
                        link.mark(V.tensor_reduce(arow[:, 0, 0, :], p0, AXX, ALU.max))
                        link.mark(V.tensor_reduce(arow[:, 0, 1, :], p1, AXX, ALU.max))
                        link.settle()
                        V.tensor_scalar(arow[:, 1], arow[:, 0], -(AD ** -0.5), None, ALU.mult).then_inc(S("s_max"), 1)
                    if c == ("ga", 0):
                        free(V.tensor_copy(gcol[:].rearrange("p t a h -> p (t a h)"), full("gcol")[:, 0:16]))
                        for b in range(2):
                            src = by2(full("negM", b))
                            V.tensor_tensor(dT0[:, 2 * b:2 * b + 2, :], src, tri_s[:].unsqueeze(1).broadcast_to([128, 2, 256]), ALU.add)
                            free(V.tensor_tensor(dT1[:, 2 * b:2 * b + 2, :], src[:, :, 128:256],
                                                 tri_s[:, 0:128].unsqueeze(1).broadcast_to([128, 2, 128]), ALU.add))
                        dve.wait_ge(S("p_exp"), 16)
                        link(V.reciprocal(arow[:, 0], arow[:, 2]))
                        for t, p in enumerate((p0, p1)):
                            V.tensor_tensor(p, p, arow[:, 0, t, :].unsqueeze(2).broadcast_to([128, AH, 128 * (t + 1)]),
                                            ALU.mult).then_inc(S("p_ready"), 1)
                        dve.wait_ge(S("decay"), 9)
                        for b in range(2):
                            src = by2(full("ST", b))
                            free(V.scalar_tensor_tensor(out=dT0[:, 2 * b:2 * b + 2, :], in0=src, scalar=MD ** -0.5,
                                                        in1=dT0[:, 2 * b:2 * b + 2, :], op0=ALU.mult, op1=ALU.mult))
                        src = full("ST", 2).rearrange("p (h t) -> p h t", h=MH)
                        free(V.scalar_tensor_tensor(out=dT1, in0=src, scalar=MD ** -0.5, in1=dT1, op0=ALU.mult, op1=ALU.mult))
                    if c == ("ga", 1):
                        for b in range(6):
                            src = full("PT", b).rearrange("p (h k) -> p h k", h=4)
                            if b < 2:
                                dst = pT0[:, 4 * b:4 * b + 4, 0:128]
                            elif b < 4:
                                dst = pT0[:, 4 * (b - 2):4 * (b - 2) + 4, 128:256]
                            else:
                                dst = pT1[:, 4 * (b - 4):4 * (b - 4) + 4, :]
                            free(V.tensor_copy(dst, src))
                    if c == ("gm", 0):
                        for b in range(2):
                            free(V.tensor_copy(aT[:, 2 * b:2 * b + 2, :], by2(full("PV", b))))
                        for b in range(4):
                            t, hp = b // 2, b % 2
                            src = by2(full("num", b))
                            dd = den[:, t, 2 * hp:2 * hp + 2]
                            link(V.scalar_tensor_tensor(out=dd, in0=src[:, :, MD], scalar=-1.0,
                                                        in1=gcol[:, t, 1, 2 * hp:2 * hp + 2], op0=ALU.mult, op1=ALU.max))
                            link(V.tensor_tensor(dd, src[:, :, MD], dd, ALU.max))
                            link(V.reciprocal(dd, dd))
                            free(V.tensor_tensor(hm[:, t, 256 * hp:256 * hp + 256].rearrange("p (h c) -> p h c", h=2), src[:, :, 0:MD],
                                                 dd.unsqueeze(2).broadcast_to([128, 2, MD]), ALU.mult))
                        dve.wait_ge(S("misc_free"), MISC["num", 3] + 1)
                        link(V.tensor_tensor(hsq, hm, hm, ALU.mult))
                        for t in range(TT):
                            ins = V.tensor_reduce(stat[:, MSS + 4 * t:MSS + 4 * t + 4], hsq[:, t, :].rearrange("p (h c) -> p h c", h=MH), AXX, ALU.add)
                            if t == 0:
                                link(ins)
                        ins.then_inc(S("hm_squared"), 1)
                    if c == ("gm", 2):
                        dve.wait_ge(S("hm_rstd"), 1)
                        for t in range(TT):
                            hh = hm[:, t, :].rearrange("p (h c) -> p h c", h=MH)
                            link.mark(V.tensor_tensor(hh, hh, stat[:, MSS + 4 * t:MSS + 4 * t + 4].unsqueeze(2).broadcast_to([128, MH, MD]), ALU.mult))
                        link.settle()
                        V.tensor_tensor(hm, hm, mosig, ALU.mult).then_inc(S("hm_ready"), 1)
                        dve.wait_ge(S("aT_hi"), 1)
                        V.tensor_tensor(aTl[:], aT, aTh[:].bitcast(f32), ALU.subtract).then_inc(S("aT_lo"), 1)
                    if c == ("gm", 3):
                        for b in range(2):
                            src = by2(full("hmT", b))
                            for i in range(2):
                                h = 2 * b + i
                                ins = V.tensor_scalar(mT[:, h, :], src[:, i, :], vcol[:, VEC["mnw"] + h:VEC["mnw"] + h + 1], None, ALU.mult)
                            free(ins)
                    if c == ("wab", 0):
                        dve.wait_ge(S("mT_hi"), 1)
                        V.tensor_tensor(mTl[:], mT, mTh[:].bitcast(f32), ALU.subtract).then_inc(S("mT_lo"), 1)
                    if c[0] in BRANCH:
                        for half in range(2):
                            g = GROUPS.index((c, half))
                            at = 4 * c[1] + 2 * half
                            dve.wait_ge(S("proj_done"), g + 1)
                            dve.wait_ge(S("proj_taken_act"), groups_before(g, False))
                            src = by2(proj[:, g % 4, :])
                            if c[0] == "wab":
                                V.tensor_tensor(hq[:, at:at + 2, :], gsig[:, at:at + 2, :], src, ALU.mult).then_inc(S("proj_taken_dve"), 1)
                            else:
                                V.tensor_tensor(gsig[:, 8 + at:10 + at, :], gsig[:, 8 + at:10 + at, :], src, ALU.mult).then_inc(S("proj_taken_dve"), 1)
                                dve.wait_ge(S("proj_taken_dve"), groups_before(g, True))
                                ins = V.tensor_tensor(hq[:, at:at + 2, :], hq[:, at:at + 2, :], gsig[:, 8 + at:10 + at, :], ALU.add)
                                ins.then_inc(S("y_ready"), 1)
                                for q in {0: (), 1: (0,), 2: (1,), 3: (2, 3)}[2 * c[1] + half]:
                                    dve.wait_ge(S("y_hi"), q + 1)
                                    V.tensor_tensor(y_part(2 * q, 2, 1), hq[:, 2 * q:2 * q + 2, :], y_part(2 * q, 2, 0).bitcast(f32),
                                                    ALU.subtract).then_inc(S("y_lo"), 1)
                    if c == ("wo", 0):
                        for b in range(4):
                            free(V.tensor_copy(keyT[:, b // 2, 4 * (b % 2):4 * (b % 2) + 4, :],
                                               full("key", b).rearrange("p (h n) -> p h n", h=4)))
                    if c[0] == "wo":
                        g = GROUPS.index((c, 0))
                        dve.wait_ge(S("proj_done"), g + 1)
                        xx = x[:, :, CW * c[1]:CW * c[1] + CW]
                        V.tensor_tensor(xx, xx, by2(proj[:, g % 4, :]), ALU.add).then_inc(S("proj_taken_dve"), 1)
                        if c[1] == 3:
                            dve.wait_ge(S("proj_taken_dve"), groups_before(g, True))
                            dve.wait_ge(S("x2_squared"), 4 * TT)
                            V.tensor_reduce(stat[:, X2SUM:X2SUM + TT], stat[:, X2SS:X2SS + 4 * TT].rearrange("p (t j) -> p t j", t=TT),
                                            AXX, ALU.add).then_inc(S("x2_summed"), 1)
                            dve.wait_ge(S("x2_rstd"), 1)
                            normalise(X2SUM)
                            weighted_transpose("h2T", "ffw", "h2_hi", "h2_lo")
                    if n + 2 < len(CHUNKS):
                        lo(n + 2)
                for b in range(8):
                    hh, t, half = b // 4, (b // 2) % 2, b % 2
                    free(V.tensor_copy(sc[:, t, 4 * hh:4 * hh + 4, half, :],
                                       full("sc", b).rearrange("p (h n) -> p h n", h=4)))

            @blk.tensor
            def _(pe):
                mm = nc.tensor.matmul

                def use(name, i=0):
                    if MISC[name, i] >= 4:
                        pe.wait_ge(S("misc_free"), MISC[name, i] - 3)
                    return bank(name, i)

                def filled(ins):
                    ins.then_inc(S("misc_full"), 1)

                def transposes(name, src, n, h_before=None):
                    for b in range(n):
                        if h_before is not None and b % 2 == 0:
                            pe.wait_ge(S("h_nat"), h_before + b + 2)
                        dst = use(name, b)
                        for i in range(4):
                            last = nc.tensor.transpose(dst[:, 128 * i:128 * i + 128], src(2 * b + i // 2, i % 2), ident[:])
                        filled(last)

                split_done = {("mq", 0): "h", ("wo", 0): "y", ("wq", 0): "h2"}
                pe.wait_ge(S("ident_ready"), 1)
                pe.wait_ge(S("vec_loaded"), 16 * 6)
                filled(nc.tensor.transpose(use("vec")[:, 0:NVEC], vrow[:], ident[0:NVEC, 0:NVEC]))
                transposes("xT", lambda k, t: hwork[:, t, 128 * k:128 * k + 128], 4, 0)
                for n, c in enumerate(CHUNKS):
                    name, j = c
                    if c == ("wab", 0):
                        pe.wait_ge(S("aT_lo"), 1)
                    if c == ("wmb", 0):
                        pe.wait_ge(S("mT_lo"), 1)
                    if c == ("wo", 0):
                        pe.wait_ge(S("key_loaded"), 32)
                        for b in range(4):
                            dst = use("key", b)
                            for i in range(4):
                                last = nc.tensor.transpose(dst[:, 128 * i:128 * i + 128], keyn[:, b // 2, 4 * (b % 2) + i, :], ident[:])
                            filled(last)
                    if c == ("wq", 0):
                        transposes("h2T", lambda k, t: hwork[:, t, 128 * k:128 * k + 128], 4, 4)
                    wh, wl = as_chunk(whi[:, n % 3, :], c), as_chunk(wlo[:, n % 3, :], c)
                    slices = 4 if name in BRANCH else KD
                    parts = [g for g in GROUPS if g[0] == c]
                    for gr in parts:
                        g = GROUPS.index(gr)
                        if g >= 4:
                            old = g - 4
                            by_dve = GROUPS[old][0][0] in BY_DVE
                            pe.wait_ge(S("proj_taken_dve" if by_dve else "proj_taken_act"), groups_before(old, by_dve))
                        for i in range(2):
                            dst = proj[:, g % 4, 256 * i:256 * i + 256]
                            for p, (in_lo, w) in enumerate(((0, wh), (1, wh), (0, wl))):
                                if gr == parts[0] and i == 0 and p != 1:
                                    for sem in ("hi_ready",) if p == 0 else ("lo_dve_ready", "lo_pool_ready"):
                                        pe.wait_ge(S(sem), n + 1)
                                for k in range(slices):
                                    if gr == parts[0] and i == 0 and p < 2 and k % 2 == 0 and c in split_done:
                                        pe.wait_ge(S(split_done[c] + ("_lo" if p else "_hi")), k // 2 + 1)
                                    f = dict(start=p == 0 and k == 0, stop=p == 2 and k == slices - 1)
                                    if name in BRANCH:
                                        th, tl = (aTh, aTl) if name == "wab" else (mTh, mTl)
                                        at = 256 * gr[1] + 128 * i
                                        last = mm(dst, w[:, k, at:at + 128], (tl if in_lo else th)[:, k, :], **f)
                                    elif name in ("aq", "ak", "av", "mv", "mo", "wo"):
                                        part = y_part(k, 1, in_lo)[:, 0] if name == "wo" else (hTl if in_lo else hTh)[:, k]
                                        last = mm(dst, part[:, 128 * i:128 * i + 128], w[:, k, :], **f)
                                    else:
                                        last = mm(dst, w[:, k, 128 * i:128 * i + 128], (hTl if in_lo else hTh)[:, k, :], **f)
                        last.then_inc(S("proj_done"), 1)
                    if c == ("mk", 1):
                        pe.wait_ge(S("wpair_ready"), 2)
                        dst = use("gates")
                        for k in range(KD):
                            last = mm(dst[0:FG + MH, 0:T], wpair[:, k, :], hq[:, k, :], start=k == 0, stop=k == KD - 1)
                        filled(last)
                    if c == ("mv", 1):
                        pe.wait_ge(S("qk_ready"), 2)
                        transposes("qkT", lambda k, t: qk[:, t, 128 * k:128 * k + 128], 4)
                    if c == ("mo", 1):
                        pe.wait_ge(S("misc_free"), MISC["qkT", 3] + 1)
                        for t in range(TT):
                            per, w = (4, 128) if t == 0 else (2, 256)
                            for b in range(AH // per):
                                dst = use("S", b + 2 * t)
                                rows = slice(64 * (b % 2), 64 * (b % 2) + 64)
                                for i in range(per):
                                    pr = per * (b // 2) + i
                                    last = mm(dst[:, i * w:i * w + w], hq[rows, pr, 128 * t:128 * t + 128], hq[rows, 4 + pr, 0:w],
                                              start=True, stop=True)
                                filled(last)
                        pe.wait_ge(S("gate_rows"), 1)
                        dst = use("gcol")
                        for t in range(TT):
                            for i, r in enumerate((rG, rTMP)):
                                at = 8 * t + 4 * i
                                last = mm(dst[:, at:at + MH], grow[:, r, 128 * t:128 * t + 128], ident[0:MH, 0:MH], start=True, stop=True)
                        filled(last)
                        for h in range(MH):
                            if h % 2 == 0:
                                dst = use("negM", h // 2)
                            last = mm(dst[:, 256 * (h % 2):256 * (h % 2) + 256], sel[:, h, :], grow[:, rNM, :], start=True, stop=True)
                            if h % 2:
                                filled(last)
                    if c == ("ga", 0):
                        pe.wait_ge(S("silu_done"), 2)
                        for h in range(MH):
                            if h % 2 == 0:
                                dst = use("ST", h // 2)
                            last = mm(dst[:, 256 * (h % 2):256 * (h % 2) + 256], cv[:, MH + h, 0:128], cv[:, h, :], start=True, stop=True)
                            if h % 2:
                                filled(last)
                        dst = use("ST", 2)
                        for h in range(MH):
                            last = mm(dst[:, 128 * h:128 * h + 128], cv[:, MH + h, 128:256], cv[:, h, 128:256], start=True, stop=True)
                        filled(last)
                    if c == ("ga", 1):
                        pe.wait_ge(S("p_ready"), 2)
                        for b in range(6):
                            dst = use("PT", b)
                            for i in range(4):
                                h = 4 * (b % 2) + i
                                src = p0[:, h, :] if b < 2 else p1[:, h, 128 * (b // 4):128 * (b // 4) + 128]
                                last = nc.tensor.transpose(dst[:, 128 * i:128 * i + 128], src, ident[:])
                            filled(last)
                    if c == ("ga", 3):
                        pe.wait_ge(S("misc_free"), MISC["PT", 5] + 1)
                        pe.wait_ge(S("proj_taken_act"), 10)
                        for h in range(AH):
                            if h % 4 == 0:
                                dst = use("PV", h // 4)
                            rows = slice(64 * (h % 2), 64 * (h % 2) + 64)
                            at = 256 * ((h // 2) % 2)
                            mm(dst[rows, at:at + 256], v[:, 0, AD * h:AD * h + AD], pT0[:, h, :], start=True, stop=False)
                            last = mm(dst[rows, at + 128:at + 256], v[:, 1, AD * h:AD * h + AD], pT1[:, h, :], start=False, stop=True)
                            if h % 4 == 3:
                                filled(last)
                        pe.wait_ge(S("v1_ones"), 1)
                        pe.wait_ge(S("v1_half"), 2)
                        pe.wait_ge(S("proj_taken_act"), 12)
                        for b in range(4):
                            t, hp = b // 2, b % 2
                            dst = use("num", b)
                            for i in range(2):
                                h = 2 * hp + i
                                o = dst[:, 256 * i:256 * i + MD + 1]
                                last = mm(o, dT0[:, h, 128 * t:128 * t + 128], v1[:, 0, h, :], start=True, stop=t == 0)
                                if t == 1:
                                    last = mm(o, dT1[:, h, :], v1[:, 1, h, :], start=False, stop=True)
                            filled(last)
                        pe.wait_ge(S("misc_full"), MISC["num", 3] + 1)
                        pe.sem_inc(S("num_done"), 1)
                    if c == ("gm", 3):
                        pe.wait_ge(S("hm_ready"), 1)
                        transposes("hmT", lambda k, t: hm[:, t, 128 * k:128 * k + 128], 2)
                pe.wait_ge(S("misc_free"), MISC["key", 3] + 1)
                for b in range(8):
                    hh, t, half = b // 4, (b // 2) % 2, b % 2
                    pe.wait_ge(S("proj_taken_act"), groups_before(GROUPS.index((("wq", 4 * hh + 3), 0)), False))
                    dst = use("sc", b)
                    for i in range(4):
                        h = 4 * hh + i
                        last = mm(dst[:, 128 * i:128 * i + 128], gsig[:, 2 * h + half, 128 * t:128 * t + 128], keyT[:, half, h, :],
                                  start=True, stop=True)
                    filled(last)
        build_peer(nc, a, out, keep, S, Link, sb, ps, x, hT, ident, sc, work)


def build_peer(nc, a, out, keep, S, Link, sb, ps, x, hT, ident, sc, work):
    f32, f32r, bf16, u32 = mybir.dt.float32, mybir.dt.float32r, mybir.dt.bfloat16, mybir.dt.uint32
    ALU, ACT, AXX = mybir.AluOpType, mybir.ActivationFunctionType, mybir.AxisListType.X
    w_down = a["peer_w_down"].rearrange("(p e) d -> p (e d)", e=NK)
    w_up = a["peer_w_up"].rearrange("(p e) d -> p (e d)", e=NK)
    V = nc.vector
    UNITS = TT * PH
    SA = NA // 2
    SC = NK // UC // 2
    UPS = UNITS // SA
    NG = T // UG

    def wait(eng, name, u, per, at):
        if not (isinstance(u, int) and u * per + at <= 0):
            eng.wait_ge(S(name), u * per + at)

    def halves(eng, n, body, between=None):
        body(0, False)
        with eng.Fori(1, n // 2 - 1) as u:
            body(u, False)
        body(n // 2 - 1, False)
        if between:
            between()
        body(n // 2, True)
        with eng.Fori(n // 2 + 1, n - 1) as u:
            body(u, True)
        body(n - 1, True)

    def at_step(u, n):
        return isinstance(u, int) and u == n

    peer = ExitStack()
    with peer:
        act_all = sb(peer, "act_all", [128, NK, T])
        act_flat = act_all[:].rearrange("p e t -> p (e t)")
        iota16 = sb(peer, "iota16", [128, TOPK])
        iota128 = sb(peer, "iota128", [128, NK], bf16)
        found = sb(peer, "found", [128, UG, EH], bf16)
        gps = ps(peer, "gps", [128, 2, 512])
        scf = sc[:].rearrange("p t h b n -> p (t h b n)")
        chosenT = scf[:, 0:3 * T].rearrange("p (i t) -> p i t", i=3)
        gpart = scf[:, 3 * T:3 * T + 3 * T // 2].bitcast(bf16).rearrange("p (i t) -> p i t", i=3)
        at1, at2, at3 = 6 * T, 6 * T + UG * NK, 6 * T + UG * NK + UG * 3 * EH
        one1 = scf[:, at1:at2].bitcast(bf16).rearrange("p (s i e) -> p s i e", s=2, i=UG)
        one2 = scf[:, at2:at3].bitcast(bf16).rearrange("p (s i q e) -> p s i q e", s=2, i=UG, q=3)

        def group_count(second):
            return NG if second else -EH

        assert UA == UC and NG == EH

        def make_ones(dve, u, j, second):
            wait(dve, "gates_done", u, UA, j - 1 + group_count(second))
            wait(dve, "ones_ready", u, UA, j + group_count(second))
            first = j * UG - (0 if second else EH * UG)
            toks = bass.ds(u * (UA * UG) + first, UG)
            V.tensor_tensor(found[:], iota128[:, EH * second:EH * second + EH].unsqueeze(1).broadcast_to([128, UG, EH]),
                            chosenT[:, 1, toks].unsqueeze(2).broadcast_to([128, UG, EH]), ALU.is_equal).then_inc(S("e2_found"), 1)
            V.tensor_tensor(one1[:, j % 2], iota128[:].unsqueeze(1).broadcast_to([128, UG, NK]),
                            chosenT[:, 0, toks].unsqueeze(2).broadcast_to([128, UG, NK]), ALU.is_equal)
            wait(dve, "e2_found", u, UA, j + 1 + group_count(second))
            V.tensor_tensor(one2[:, j % 2], found[:].unsqueeze(2).broadcast_to([128, UG, 3, EH]),
                            gpart[:, :, toks].rearrange("p q i -> p i q").unsqueeze(3).broadcast_to([128, UG, 3, EH]),
                            ALU.mult).then_inc(S("ones_ready"), 1)

        def make_gates(pe, u, j, second):
            wait(pe, "ones_ready", u, UA, j + 1 + group_count(second))
            wait(pe, "gates_used", u, UA, j - 1 + group_count(second))
            for i in range(UG):
                for p in range(3):
                    last = nc.tensor.matmul(gps[:, j % 2, EH * i:EH * i + EH], one1[:, j % 2, i, :], one2[:, j % 2, i, p, :],
                                            start=p == 0, stop=p == 2)
            last.then_inc(S("gates_done"), 1)

        def use_gates(dve, u, j, second):
            wait(dve, "gates_done", u, UA, j + 1 + group_count(second))
            tok = bass.ds(u * (UA * UG) + (j * UG - (0 if second else EH * UG)), UG)
            at = act_all[:, EH * second:EH * second + EH, tok]
            V.tensor_tensor(at, at, gps[:, j % 2, 0:UG * EH].rearrange("p (i e) -> p e i", i=UG), ALU.mult).then_inc(S("gates_used"), 1)

        down = ExitStack()
        with down:
            wd = work[:].rearrange("p (s d) -> p s d", s=2)
            wTh = sb(down, "wTh", [128, 2, KD, 128], f32r)
            wTl = sb(down, "wTl", [128, 2, KD, 128], f32r)
            ucopy = sb(down, "ucopy", [128, 2, 2 * T])
            hit = sb(down, "hit", [128, UPS, 2 * TOPK, TOPK])
            hitf = hit[:].rearrange("p u n r -> p (u n r)")
            score = hitf[:, 0:UPS * 2 * NK].rearrange("p (s n) -> p s n", n=NK)
            cand = hitf[:, UPS * 2 * NK:UPS * (2 * NK + TOPK * TOPK)].rearrange("p (u n) -> p u n", u=UPS)
            val = sb(down, "val", [128, UPS * 2, TOPK])
            key = sb(down, "key", [128, UPS * 2, TOPK], u32)
            pair = sb(down, "pair", [128, UPS, TOPK], u32)
            top = sb(down, "top", [128, UPS, TOPK])
            part = sb(down, "part", [128, UPS, 2, TOPK], u32)
            rank = sb(down, "rank", [128, 2, UPS * 2 * TOPK])
            picked = sb(down, "picked", [128, UPS, 3, TOPK])
            chosen = sb(down, "chosen", [128, 3, UNITS * TOPK])
            total = sb(down, "total", [128, UNITS])
            tps = ps(down, "tps", [128, 2, KD, 128])
            ups = ps(down, "ups", [128, 2, 2 * T])
            blk = down.enter_context(nc.Block())
            PER = 38

            def key_at_rank():
                return rank[:, 1].rearrange("p (b r) -> p b r", r=TOPK).unsqueeze(2).broadcast_to([128, UPS * 2, TOPK, TOPK])

            @blk.sync
            def _(sp):
                def body(u, second):
                    for j in range(UA):
                        if at_step(u, 0) and j < 2:
                            continue
                        wait(sp, "wd_transposed", u, UA, j - 1)
                        sp.dma_start(wd[:, j % 2, :], w_down[:, bass.ds((u * UA + j) * D, D)]).then_inc(S("wd_loaded%d" % (j % 2)), 16)
                halves(sp, NA, body)
                for j in range(2):
                    sp.wait_ge(S("wd_transposed"), NK - 1 + j)
                    sp.dma_start(wd[:, j, :], w_up[:, D * j:D * j + D]).then_inc(S("wu_loaded%d" % j), 16)

            @blk.tensor
            def _(pe):
                mm = nc.tensor.matmul

                def transpose_tile(u, m):
                    wait(pe, "wd_loaded%d" % (m % 2), u, 16 * UA // 2, 16 * (m // 2 + 1))
                    wait(pe, "wT_hi", u, UA, m - 1)
                    wait(pe, "wT_lo", u, UA, m - 1)
                    for k in range(KD):
                        last = nc.tensor.transpose(tps[:, m % 2, k, :], wd[:, m % 2, 128 * k:128 * k + 128], ident[:])
                    last.then_inc(S("wd_transposed"), 1)

                def body(u, second):
                    for j in range(UA):
                        if not (at_step(u, NA - 1) and j == UA - 1):
                            transpose_tile(u, j + 1)
                        wait(pe, "wT_hi", u, UA, j + 1)
                        wait(pe, "u_copied", u, UA, j - 1)
                        dst = ups[:, j % 2, :]
                        for k in range(KD):
                            mm(dst, wTh[:, j % 2, k, :], hT[:, k, :, :].rearrange("p s t -> p (s t)"), start=k == 0, stop=False)
                        if at_step(u, SA - 1) and j == UA - 1:
                            pe.wait_ge(S("chosen_ready"), 1)
                            flat = gps[:].rearrange("p b n -> p (b n)")
                            for i in range(3):
                                for t in range(TT):
                                    at = T * i + 128 * t
                                    last = nc.tensor.transpose(flat[:, at:at + 128], chosen[:, i, 128 * t:128 * t + 128], ident[:])
                            last.then_inc(S("chosen_transposed"), 1)
                        wait(pe, "wT_lo", u, UA, j + 1)
                        for k in range(KD):
                            last = mm(dst[:, T:2 * T], wTl[:, j % 2, k, :], hT[:, k, 0, :], start=False, stop=k == KD - 1)
                        last.then_inc(S("u_done"), 1)
                        if second:
                            make_gates(pe, u, j, False)

                transpose_tile(0, 0)
                halves(pe, NA, body)

            @blk.scalar
            def _(act):
                def hi(u, m):
                    wait(act, "wd_transposed", u, UA, m + 1)
                    wait(act, "u_done", u, UA, m - 1)
                    nc.scalar.activation(wTh[:, m % 2], tps[:, m % 2], ACT.Copy).then_inc(S("wT_hi"), 1)

                def gelu(u, m):
                    wait(act, "u_added", u, UA, m + 1)
                    nc.scalar.activation(act_flat[:, bass.ds((u * UA + m) * T, T)], ucopy[:, m % 2, 0:T], ACT.Gelu).then_inc(S("gelu_done"), 1)

                def body(u, second):
                    for j in range(UA):
                        if at_step(u, SA - 1) and j == UA - 2:
                            act.wait_ge(S("choice_step"), SA * PER)
                            nc.scalar.activation(chosen[:, 2, :], chosen[:, 2, :], ACT.Exp).then_inc(S("gate_exp"), 1)
                        if not (at_step(u, NA - 1) and j == UA - 1):
                            hi(u, j + 1)
                        if not second and j == 0:
                            wait(act, "choice_step", u, PER, 0)
                            nc.scalar.activation(hitf[:, 0:UPS * 2 * NK], scf[:, bass.ds(u * (UPS * 2 * NK), UPS * 2 * NK)],
                                                 ACT.Copy).then_inc(S("scores_copied"), 1)
                        wait(act, "u_done", u, UA, j + 1)
                        wait(act, "gelu_done", u, UA, j - 1)
                        nc.scalar.activation(ucopy[:, j % 2, :], ups[:, j % 2, :], ACT.Copy).then_inc(S("u_copied"), 1)
                        if not (at_step(u, 0) and j == 0):
                            gelu(u, j - 1)

                hi(0, 0)
                halves(act, NA, body)
                gelu(NA - 1, UA - 1)

            @blk.gpsimd
            def _(pool):
                iota = dict(base=0, channel_multiplier=0, allow_small_or_imprecise_dtypes=True)
                nc.gpsimd.iota(iota16[:], [[1, TOPK]], **iota).then_inc(S("iotas"), 1)
                nc.gpsimd.iota(iota128[:], [[1, NK]], **iota).then_inc(S("iotas"), 1)
                pool.wait_ge(S("iotas"), 2)

                def body(u, second):
                    for j in range(UA):
                        wait(pool, "u_copied", u, UA, j + 1)
                        nc.gpsimd.tensor_tensor(ucopy[:, j % 2, 0:T], ucopy[:, j % 2, 0:T], ucopy[:, j % 2, T:2 * T], ALU.add).then_inc(S("u_added"), 1)
                        if not second and j == (UA - 4 if at_step(u, SA - 1) else UA - 2):
                            wait(pool, "hit_found", u, 1, 1)
                            hits = hitf.rearrange("p (b k r) -> p b k r", k=TOPK, r=TOPK)
                            nc.gpsimd.tensor_tensor(hits, hits, key_at_rank(), ALU.mult).then_inc(S("hit_weighted"), 1)

                halves(pool, NA, body)

            @blk.vector
            def _(dve):
                link = Link(dve, "gate_link")

                def lo(u, m):
                    wait(dve, "wT_hi", u, UA, m + 1)
                    wait(dve, "u_done", u, UA, m - 1)
                    V.tensor_tensor(wTl[:, m % 2], tps[:, m % 2], wTh[:, m % 2].bitcast(f32), ALU.subtract).then_inc(S("wT_lo"), 1)

                def choice(u):
                    done = [0]

                    def mark(ins):
                        ins.then_inc(S("choice_step"), 1)
                        done[0] += 1

                    def settle():
                        wait(dve, "choice_step", u, PER, done[0])
                        dve.sem_inc(S("choice_go"), 1)

                    wait(dve, "scores_copied", u, 1, 1)
                    dve.sem_inc(S("choice_go"), 1)
                    for r in range(2):
                        eight = slice(8 * r, 8 * r + 8)
                        for b in range(UPS * 2):
                            mark(V.max(val[:, b, eight], score[:, b, :]))
                        yield
                        settle()
                        for b in range(UPS * 2):
                            mark(V.max_index(key[:, b, eight], val[:, b, eight], score[:, b, :]))
                        yield
                        settle()
                        if r == 0:
                            for b in range(UPS * 2):
                                mark(V.match_replace(score[:, b, :], val[:, b, eight], score[:, b, :], LOWEST))
                            yield
                            settle()
                    both = val[:].rearrange("p (u b) k -> p u b k", b=2)
                    shape = [128, UPS, TOPK, TOPK]
                    mark(V.tensor_tensor(cand.rearrange("p u (i j) -> p u i j", i=TOPK), both[:, :, 0, :].unsqueeze(3).broadcast_to(shape),
                                         both[:, :, 1, :].unsqueeze(2).broadcast_to(shape), ALU.add))
                    yield
                    settle()
                    for r in range(2):
                        eight = slice(8 * r, 8 * r + 8)
                        for i in range(UPS):
                            mark(V.max(top[:, i, eight], cand[:, i, :]))
                        yield
                        settle()
                        for i in range(UPS):
                            mark(V.max_index(pair[:, i, eight], top[:, i, eight], cand[:, i, :]))
                        yield
                        settle()
                        if r == 0:
                            for i in range(UPS):
                                mark(V.match_replace(cand[:, i, :], top[:, i, eight], cand[:, i, :], LOWEST))
                            yield
                            settle()
                    mark(V.tensor_scalar(part[:, :, 0, :], pair[:], 4, None, ALU.logical_shift_right))
                    mark(V.tensor_scalar(part[:, :, 1, :], pair[:], TOPK - 1, None, ALU.bitwise_and))
                    mark(V.tensor_copy(rank[:, 1], key[:].rearrange("p b k -> p (b k)")))
                    mark(V.tensor_tensor(picked[:, :, 2, :], top[:], top[:, :, 0:1].broadcast_to([128, UPS, TOPK]), ALU.subtract))
                    yield
                    settle()
                    mark(V.tensor_copy(rank[:, 0], part[:].rearrange("p u b k -> p (u b k)")))
                    settle()
                    n = UPS * 2 * TOPK
                    V.tensor_tensor(hitf.rearrange("p (n r) -> p n r", r=TOPK), rank[:, 0].unsqueeze(2).broadcast_to([128, n, TOPK]),
                                    iota16[:].unsqueeze(1).broadcast_to([128, n, TOPK]), ALU.is_equal).then_inc(S("hit_found"), 1)
                    yield
                    yield
                    wait(dve, "hit_weighted", u, 1, 1)
                    mark(V.tensor_reduce(picked[:, :, 0:2, :].rearrange("p u b k -> p u (b k)"), hit[:], AXX, ALU.add))
                    yield
                    settle()
                    mark(V.tensor_copy(chosen[:, :, bass.ds(u * (UPS * TOPK), UPS * TOPK)].rearrange("p i (u k) -> p i u k", u=UPS),
                                       picked[:].rearrange("p u i k -> p i u k")))
                    assert done[0] == PER, done
                    yield

                def softmax():
                    dve.wait_ge(S("gate_exp"), 1)
                    g3 = chosen[:, 2, :].rearrange("p (u k) -> p u k", u=UNITS)
                    link(V.tensor_reduce(total[:], g3, AXX, ALU.add))
                    link(V.reciprocal(total[:], total[:]))
                    V.tensor_tensor(g3, g3, total[:].unsqueeze(2).broadcast_to([128, UNITS, TOPK]), ALU.mult).then_inc(S("chosen_ready"), 1)

                def split_gates():
                    dve.wait_ge(S("chosen_transposed"), 1)
                    link(V.tensor_copy(chosenT, gps[:].rearrange("p b n -> p (b n)")[:, 0:3 * T].rearrange("p (i t) -> p i t", i=3)))
                    for p in range(3):
                        link(V.tensor_copy(gpart[:, p, :], chosenT[:, 2, :]))
                        if p < 2:
                            link(V.tensor_tensor(chosenT[:, 2, :], chosenT[:, 2, :], gpart[:, p, :], ALU.subtract))

                def body(u, second):
                    parts = () if second else choice(u)
                    for j in range(UA):
                        if at_step(u, SA) and j == 0:
                            lo(u, 1)
                            make_ones(dve, u, 1, False)
                            continue
                        if second:
                            if not (at_step(u, NA - 1) and j == UA - 1):
                                make_ones(dve, u, j + 1, False)
                            use_gates(dve, u, j - 1, False)
                        if not (at_step(u, NA - 1) and j == UA - 1):
                            lo(u, j + 1)
                        if at_step(u, SA - 1):
                            for _ in range((4, 4, 3, 2, 1, 99, 0, 0)[j]):
                                next(parts, None)
                            if j == UA - 2:
                                softmax()
                            if j == UA - 1:
                                split_gates()
                                make_ones(dve, SA, 0, False)
                        elif not second:
                            for _ in range(2 if j < UA - 1 else 99):
                                next(parts, None)

                dve.wait_ge(S("iotas"), 2)
                lo(0, 0)
                halves(dve, NA, body, lambda: dve.wait_ge(S("gelu_done"), EH))
                use_gates(dve, NA - 1, UA - 1, False)

        upx = ExitStack()
        with upx:
            wu_more = sb(upx, "wu_more", [128, 2, D])
            wu = [work[:, 0:D], work[:, D:2 * D], wu_more[:, 0, :], wu_more[:, 1, :]]
            wuh = hT[:].rearrange("p k s t -> p (k s t)").rearrange("p (s d) -> p s d", s=4)
            wul = sb(upx, "wul", [128, 4, D], f32r)
            ah = sb(upx, "ah", [128, 2, T], f32r)
            al = sb(upx, "al", [128, 2, T], f32r)
            acc = ps(upx, "acc", [128, TT, D])
            blk = upx.enter_context(nc.Block())
            NC = NK // UC

            def pool_up(u, m, second):
                return 640 if second else (384, 512, 640, 800)[m] if at_step(u, 0) and m < 4 else 960

            def is_last(u, j):
                return at_step(u, NC - 1) and j == UC - 1

            def last_group(u, j):
                return at_step(u, SC - 1) and j == UC - 1

            @blk.sync
            def _(sp):
                def body(u, second):
                    for j in range(UC):
                        if at_step(u, 0) and j < 2:
                            continue
                        wait(sp, "wu_hi", u, UC, j - 3)
                        wait(sp, "wu_lo_pool", u, UC, j - 3)
                        wait(sp, "wu_lo_dve", u, UC, j - 3)
                        sp.dma_start(wu[j % 4], w_up[:, bass.ds((u * UC + j) * D, D)]).then_inc(S("wu_loaded%d" % (j % 4)), 16)
                halves(sp, NC, body)
                dst = out.rearrange("o (t p) d -> p (o t) d", p=128)
                for t in range(TT):
                    sp.wait_ge(S("x_final"), t + 1)
                    sp.dma_start(dst[:, t, :], x[:, t, :]).then_inc(S("out_stored"), 16)
                sp.wait_ge(S("out_stored"), 16 * TT)

            @blk.scalar
            def _(act):
                def weights_hi(u, m):
                    wait(act, "wu_loaded%d" % (m % 4), u, 16 * UC // 4, 16 * (m // 4 + 1))
                    wait(act, "up_done", u, UC, m - 3)
                    nc.scalar.activation(wuh[:, m % 4, :], wu[m % 4], ACT.Copy).then_inc(S("wu_hi"), 1)

                def acts_hi(u, m):
                    wait(act, "up_done", u, UC, m - 1)
                    nc.scalar.activation(ah[:, m % 2, :], act_flat[:, bass.ds((u * UC + m) * T, T)], ACT.Copy).then_inc(S("act_hi"), 1)

                def body(u, second):
                    for j in range(UC):
                        if not is_last(u, j):
                            if last_group(u, j):
                                act.wait_ge(S("gates_used"), 2 * NG)
                            acts_hi(u, j + 1)
                        if not (is_last(u, j) or is_last(u, j + 1)):
                            weights_hi(u, j + 2)

                weights_hi(0, 0)
                acts_hi(0, 0)
                weights_hi(0, 1)
                halves(act, NC, body)

            @blk.gpsimd
            def _(pool):
                def weights_lo(u, m, second):
                    wait(pool, "wu_hi", u, UC, m + 1)
                    wait(pool, "up_done", u, UC, m - 3)
                    cols = slice(0, pool_up(u, m, second))
                    nc.gpsimd.tensor_tensor(wul[:, m % 4, cols], wu[m % 4][:, cols], wuh[:, m % 4, cols].bitcast(f32),
                                            ALU.subtract).then_inc(S("wu_lo_pool"), 1)

                def body(u, second):
                    for j in range(UC):
                        if not is_last(u, j):
                            weights_lo(u, j + 1, second)

                weights_lo(0, 0, False)
                halves(pool, NC, body)

            @blk.vector
            def _(dve):
                def weights_lo(u, m, second):
                    wait(dve, "wu_hi", u, UC, m + 1)
                    wait(dve, "up_done", u, UC, m - 3)
                    cols = slice(pool_up(u, m, second), D)
                    V.tensor_tensor(wul[:, m % 4, cols], wu[m % 4][:, cols], wuh[:, m % 4, cols].bitcast(f32),
                                    ALU.subtract).then_inc(S("wu_lo_dve"), 1)

                def acts_lo(u, m):
                    wait(dve, "act_hi", u, UC, m + 1)
                    wait(dve, "up_done", u, UC, m - 1)
                    V.tensor_tensor(al[:, m % 2, :], act_flat[:, bass.ds((u * UC + m) * T, T)], ah[:, m % 2, :].bitcast(f32),
                                    ALU.subtract).then_inc(S("act_lo"), 1)

                def body(u, second):
                    for j in range(UC):
                        first = at_step(u, 0) and j == 0
                        if first:
                            acts_lo(u, 1)
                            weights_lo(u, 1, second)
                        if at_step(u, 0):
                            make_ones(dve, u, j + 1, True)
                            if not first:
                                use_gates(dve, u, j - 1, True)
                        elif not second:
                            if not (at_step(u, SC - 1) and j >= UC - 2):
                                make_ones(dve, u, j + 2, True)
                            use_gates(dve, u, j, True)
                            if last_group(u, j):
                                dve.wait_ge(S("gates_used"), 2 * NG)
                        if not (first or is_last(u, j)):
                            acts_lo(u, j + 1)
                            weights_lo(u, j + 1, second)
                        if at_step(u, 0) and j == UC - 1:
                            make_ones(dve, u, j + 2, True)
                            use_gates(dve, u, j, True)

                weights_lo(0, 0, False)
                acts_lo(0, 0)
                make_ones(dve, 0, 0, True)
                halves(dve, NC, body)
                for t in range(TT):
                    dve.wait_ge(S("up_done"), NK)
                    V.tensor_tensor(x[:, t, :], x[:, t, :], acc[:, t, :], ALU.add).then_inc(S("x_final"), 1)

            @blk.tensor
            def _(pe):
                def body(u, second):
                    for j in range(UC):
                        wait(pe, "wu_hi", u, UC, j + 1)
                        wait(pe, "act_hi", u, UC, j + 1)
                        quarters = [(t, slice(512 * half, 512 * half + 512), slice(128 * t, 128 * t + 128)) for t in range(TT) for half in range(2)]
                        for t, cols, toks in quarters:
                            nc.tensor.matmul(acc[:, t, cols], ah[:, j % 2, toks], wuh[:, j % 4, cols], start=at_step(u, 0) and j == 0, stop=False)
                        wait(pe, "act_lo", u, UC, j + 1)
                        for t, cols, toks in quarters:
                            nc.tensor.matmul(acc[:, t, cols], al[:, j % 2, toks], wuh[:, j % 4, cols], start=False, stop=False)
                        wait(pe, "wu_lo_pool", u, UC, j + 1)
                        wait(pe, "wu_lo_dve", u, UC, j + 1)
                        for t, cols, toks in quarters:
                            last = nc.tensor.matmul(acc[:, t, cols], ah[:, j % 2, toks], wul[:, j % 4, cols], start=False, stop=is_last(u, j))
                        last.then_inc(S("up_done"), 1)
                        if at_step(u, 0):
                            make_gates(pe, u, j, True)
                        if not second and not last_group(u, j) and (j == UC - 1 or not at_step(u, 0)):
                            make_gates(pe, u, j + 1, True)
                halves(pe, NC, body)


_INS = ["x", "mix_norm_w", "w_in", "q_norm_w", "k_norm_w", "conv_w", "conv_b", "igate_b", "fgate_b", "mlstm_norm_w",
        "w_attn_branch", "w_mlstm_branch", "merge_b", "w_out", "ffn_norm_w", "peer_w_query", "peer_keys_1",
        "peer_keys_2", "peer_w_down", "peer_w_up"]


def kernel(**inputs):
    import numpy as np
    import concourse.bacc as bacc
    from concourse.bass_utils import run_bass_kernel_spmd

    freq = np.float32(500000.0) ** (-np.arange(0, ROT, 2, dtype=np.float32) / np.float32(ROT))
    angle = np.arange(T, dtype=np.float32)[:, None] * freq[None, :]
    arrays = {"rope": np.concatenate([np.cos(angle), np.sin(angle)], axis=1).astype(np.float32)}
    for name in _INS:
        arrays[name] = np.ascontiguousarray(inputs[name])
    nc = bacc.Bacc("TRN2", target_bir_lowering=False, num_devices=1)
    aps = {n: nc.dram_tensor("in_" + n, v.shape, mybir.dt.from_np(v.dtype), kind="ExternalInput").ap() for n, v in arrays.items()}
    out = nc.dram_tensor("out", (1, T, D), mybir.dt.float32, kind="ExternalOutput").ap()
    build(nc, aps, out)
    r = run_bass_kernel_spmd(nc, [{"in_" + n: v for n, v in arrays.items()}], core_ids=[0])
    return r.results[0]["out"]
```
